# Optimizing a Trainium2 kernel written in Bass

```python
import functools
import jax, jax.numpy as jnp
from jax import lax
import numpy as np

D_MODEL = 1024
BATCH = 1
SEQ = 1024
DEPTH = 1
DEC_BATCH = 8
DEC_SEQ = 1
PAST_LEN = 1024
PAGE_SIZE = 128

N_META = 16
D_RWKV = D_MODEL // 2
RWKV_HEAD = 64
H_RWKV = D_RWKV // RWKV_HEAD
LORA_DECAY = 64
LORA_A = 64
LORA_GATE = 128
D_FOX = D_MODEL // 2
FOX_HEAD = 64
H_FOX = D_FOX // FOX_HEAD
D_FF = 4 * D_MODEL
Q_BLOCK = 128
D_SHIFT = 3 * D_RWKV + LORA_DECAY + LORA_A + LORA_GATE
D_FOX_IN = 3 * D_FOX + H_FOX
D_GATES = 2 * D_MODEL
D_IN = D_SHIFT + D_FOX_IN + D_GATES
RMS_EPS = 1e-6
GN_EPS = 64e-5

kernel_name = 'rwkv7_fox_gated_hybrid_step'

def rms_norm(x, g):
    xf = x.astype(jnp.float32)
    y = xf * lax.rsqrt(jnp.mean(xf * xf, axis=-1, keepdims=True) + RMS_EPS)
    return (y * g.astype(jnp.float32)).astype(x.dtype)

def wkv_scan(r, decay, k, v, kk, a, state0):
    def step(state, inp):
        r_t, w_t, k_t, v_t, kk_t, a_t = inp
        s_kk = jnp.einsum('bhvk,bhk->bhv', state, kk_t)
        state = (state * w_t[:, :, None, :]
                 - s_kk[..., None] * (kk_t * a_t)[:, :, None, :]
                 + v_t[..., None] * k_t[:, :, None, :])
        return state, jnp.einsum('bhvk,bhk->bhv', state, r_t)
    xs = tuple(jnp.moveaxis(z, 1, 0) for z in (r, decay, k, v, kk, a))
    state, ys = lax.scan(step, state0, xs)
    return jnp.moveaxis(ys, 0, 1), state

def rwkv_time_mix(u_r, shift_prev, wkv0, lw):
    f32 = jnp.float32
    bsz, t = u_r.shape[:2]
    prev = jnp.concatenate([shift_prev[:, None, :].astype(u_r.dtype), u_r[:, :-1]], axis=1)
    us = u_r + lw['mu_shift'] * (prev - u_r)
    cuts = [D_RWKV, 2 * D_RWKV, 3 * D_RWKV, 3 * D_RWKV + LORA_DECAY, 3 * D_RWKV + LORA_DECAY + LORA_A]
    r, k, v, zw, za, zg = jnp.split(us, cuts, axis=-1)
    w_raw = -jax.nn.softplus(-(lw['w0'] + jnp.tanh(zw) @ lw['w_decay_up']).astype(f32)) - 0.5
    decay = jnp.exp(-jnp.exp(w_raw))
    a = jax.nn.sigmoid((lw['a0'] + za @ lw['w_a_up']).astype(f32))
    g = (jax.nn.sigmoid(zg) @ lw['w_g_up']).astype(f32)
    heads = lambda z: z.astype(f32).reshape(bsz, t, H_RWKV, RWKV_HEAD)
    r, k, v, decay, a = heads(r), heads(k), heads(v), heads(decay), heads(a)
    k_k = lw['k_k'].astype(f32).reshape(H_RWKV, RWKV_HEAD)
    k_a = lw['k_a'].astype(f32).reshape(H_RWKV, RWKV_HEAD)
    kk = k * k_k
    kk = kk / jnp.maximum(jnp.sqrt(jnp.sum(kk * kk, axis=-1, keepdims=True)), 1e-12)
    k = k * (1.0 + (a - 1.0) * k_a)
    y, wkv = wkv_scan(r, decay, k, v, kk, a, wkv0.astype(f32))
    mu = jnp.mean(y, axis=-1, keepdims=True)
    var = jnp.mean(jnp.square(y - mu), axis=-1, keepdims=True)
    y = ((y - mu) * lax.rsqrt(var + GN_EPS)).reshape(bsz, t, D_RWKV)
    y = y * lw['ln_x_w'].astype(f32) + lw['ln_x_b'].astype(f32)
    bonus = jnp.sum(r * k * lw['r_k'].astype(f32), axis=-1, keepdims=True) * v
    out = (y + bonus.reshape(bsz, t, D_RWKV)) * g
    return out.astype(u_r.dtype), u_r[:, -1], wkv.astype(wkv0.dtype)

def _fox_block(q, cq, pq, k, v, ck, pk):
    s = jnp.einsum('bhqd,bhkd->bhqk', q, k).astype(jnp.float32) * (FOX_HEAD ** -0.5)
    s = s + cq[..., :, None] - ck[..., None, :]
    s = jnp.where(pk[None, :] <= pq[:, None], s, -jnp.inf)
    p = jax.nn.softmax(s, axis=-1)
    return jnp.einsum('bhqk,bhkd->bhqd', p.astype(v.dtype), v)

def fox_attention(q, cq, pq, k, v, ck, pk):
    bsz, nh, nq, dh = q.shape
    if nq <= Q_BLOCK:
        return _fox_block(q, cq, pq, k, v, ck, pk)
    nb = -(-nq // Q_BLOCK)
    pad = nb * Q_BLOCK - nq
    qb = jnp.pad(q, ((0, 0), (0, 0), (0, pad), (0, 0))).reshape(bsz, nh, nb, Q_BLOCK, dh).transpose(2, 0, 1, 3, 4)
    cqb = jnp.pad(cq, ((0, 0), (0, 0), (0, pad))).reshape(bsz, nh, nb, Q_BLOCK).transpose(2, 0, 1, 3)
    pqb = jnp.pad(pq, (0, pad)).reshape(nb, Q_BLOCK)
    out = lax.map(lambda blk: _fox_block(blk[0], blk[1], blk[2], k, v, ck, pk), (qb, cqb, pqb))
    out = out.transpose(1, 2, 0, 3, 4).reshape(bsz, nh, nb * Q_BLOCK, dh)
    return out[:, :, :nq]

def attend_prompt(q, k, v, lf):
    bsz, t = q.shape[:2]
    pos = jnp.arange(t, dtype=jnp.int32)
    c = jnp.cumsum(lf, axis=1).transpose(0, 2, 1)
    qh, kh, vh = q.transpose(0, 2, 1, 3), k.transpose(0, 2, 1, 3), v.transpose(0, 2, 1, 3)
    m = N_META
    o_meta = fox_attention(qh[:, :, :m], c[:, :, :m], pos[:m], kh[:, :, :m], vh[:, :, :m], c[:, :, :m], pos[:m])
    o_real = fox_attention(qh[:, :, m:], c[:, :, m:], pos[m:], kh, vh, c, pos)
    o = jnp.concatenate([o_meta, o_real], axis=2)
    return o.transpose(0, 2, 1, 3).reshape(bsz, t, D_FOX)

def attend_sample(k_pool, v_pool, lf_pool, page_table, q, k, v, lf):
    nb, n_pages = page_table.shape
    past = n_pages * k_pool.shape[1]
    t = q.shape[1]
    k_past = k_pool[page_table].reshape(nb, past, H_FOX, FOX_HEAD)
    v_past = v_pool[page_table].reshape(nb, past, H_FOX, FOX_HEAD)
    lf_past = lf_pool[page_table].reshape(nb, past, H_FOX).astype(jnp.float32)
    k_all = jnp.concatenate([k_past, k.astype(k_past.dtype)], axis=1).transpose(0, 2, 1, 3)
    v_all = jnp.concatenate([v_past, v.astype(v_past.dtype)], axis=1).transpose(0, 2, 1, 3)
    c = jnp.cumsum(jnp.concatenate([lf_past, lf], axis=1), axis=1).transpose(0, 2, 1)
    pos = jnp.arange(past + t, dtype=jnp.int32)
    o = fox_attention(q.transpose(0, 2, 1, 3).astype(k_all.dtype), c[:, :, past:], pos[past:], k_all, v_all, c, pos)
    return o.transpose(0, 2, 1, 3).reshape(nb, t, D_FOX).astype(q.dtype)

def decoder_layer(x, shift_prev, wkv0, attend, lw):
    bsz, t = x.shape[:2]
    h = rms_norm(x, lw['norm_mix'])
    u = h @ lw['w_in']
    u_r, u_f, u_g = jnp.split(u, [D_SHIFT, D_SHIFT + D_FOX_IN], axis=-1)
    o_r, new_shift, new_wkv = rwkv_time_mix(u_r, shift_prev, wkv0, lw)
    q, k, v, f_logit = jnp.split(u_f, [D_FOX, 2 * D_FOX, 3 * D_FOX], axis=-1)
    q = q.reshape(bsz, t, H_FOX, FOX_HEAD)
    k = k.reshape(bsz, t, H_FOX, FOX_HEAD)
    v = v.reshape(bsz, t, H_FOX, FOX_HEAD)
    lf = jax.nn.log_sigmoid((f_logit + lw['b_forget']).astype(jnp.float32))
    o_f = attend(q, k, v, lf)
    g_r, g_f = jnp.split(u_g, 2, axis=-1)
    merged = jax.nn.sigmoid(g_r) * (o_r @ lw['w_br_rwkv']) + jax.nn.sigmoid(g_f) * (o_f @ lw['w_br_fox'])
    x = x + merged @ lw['w_out']
    h2 = rms_norm(x, lw['norm_ffn'])
    x = x + jnp.square(jax.nn.relu(h2 @ lw['w_ffn_up'])) @ lw['w_ffn_down']
    return x, (new_shift, new_wkv, k, v, lf.astype(x.dtype))

def setup_inputs(seed: int = 0) -> dict:
    key = jax.random.key(seed)
    ks = jax.random.split(key, 32)
    f32 = jnp.float32
    nrm = lambda kk, shape, s: s * jax.random.normal(kk, shape, f32)
    n_pages = PAST_LEN // PAGE_SIZE
    n_used = DEC_BATCH * n_pages
    n_pool = n_used + max(1, n_used // 4)
    perm = jax.random.permutation(ks[0], n_pool)
    page_table = perm[:n_used].reshape(DEC_BATCH, n_pages).astype(jnp.int32)
    L = DEPTH
    return {
        'x_prompt': nrm(ks[1], (BATCH, SEQ, D_MODEL), 1.0),
        'x_sample': nrm(ks[2], (DEC_BATCH, DEC_SEQ, D_MODEL), 1.0),
        'state_shift': nrm(ks[3], (L, DEC_BATCH, D_SHIFT), 1.0),
        'state_wkv': nrm(ks[4], (L, DEC_BATCH, H_RWKV, RWKV_HEAD, RWKV_HEAD), 0.3),
        'cache_k': nrm(ks[5], (L, n_pool, PAGE_SIZE, H_FOX, FOX_HEAD), 1.0),
        'cache_v': nrm(ks[6], (L, n_pool, PAGE_SIZE, H_FOX, FOX_HEAD), 1.0),
        'cache_logf': jax.nn.log_sigmoid(3.0 + nrm(ks[7], (L, n_pool, PAGE_SIZE, H_FOX), 1.0)),
        'page_table': page_table,
        'meta_tokens': nrm(ks[8], (N_META, D_MODEL), 1.0),
        'norm_mix': 1.0 + nrm(ks[9], (L, D_MODEL), 0.02),
        'w_in': nrm(ks[10], (L, D_MODEL, D_IN), D_MODEL ** -0.5),
        'mu_shift': jax.random.uniform(ks[11], (L, D_SHIFT), f32),
        'w0': -2.0 + nrm(ks[12], (L, D_RWKV), 0.5),
        'w_decay_up': nrm(ks[13], (L, LORA_DECAY, D_RWKV), LORA_DECAY ** -0.5),
        'a0': nrm(ks[14], (L, D_RWKV), 0.1),
        'w_a_up': nrm(ks[15], (L, LORA_A, D_RWKV), LORA_A ** -0.5),
        'w_g_up': nrm(ks[16], (L, LORA_GATE, D_RWKV), LORA_GATE ** -0.5),
        'k_k': 0.85 + nrm(ks[17], (L, D_RWKV), 0.05),
        'k_a': 1.0 + nrm(ks[18], (L, D_RWKV), 0.05),
        'r_k': nrm(ks[19], (L, H_RWKV, RWKV_HEAD), 0.1),
        'ln_x_w': 1.0 + nrm(ks[20], (L, D_RWKV), 0.02),
        'ln_x_b': nrm(ks[21], (L, D_RWKV), 0.02),
        'b_forget': jax.random.uniform(ks[22], (L, H_FOX), f32, 1.0, 5.0),
        'w_br_rwkv': nrm(ks[23], (L, D_RWKV, D_MODEL), D_RWKV ** -0.5),
        'w_br_fox': nrm(ks[24], (L, D_FOX, D_MODEL), D_FOX ** -0.5),
        'w_out': nrm(ks[25], (L, D_MODEL, D_MODEL), D_MODEL ** -0.5),
        'norm_ffn': 1.0 + nrm(ks[26], (L, D_MODEL), 0.02),
        'w_ffn_up': nrm(ks[27], (L, D_MODEL, D_FF), D_MODEL ** -0.5),
        'w_ffn_down': nrm(ks[28], (L, D_FF, D_MODEL), D_FF ** -0.5),
        'norm_final': 1.0 + nrm(ks[29], (D_MODEL,), 0.02),
    }

def reference(x_prompt, x_sample, state_shift, state_wkv, cache_k, cache_v, cache_logf, page_table,
              meta_tokens, norm_mix, w_in, mu_shift, w0, w_decay_up, a0, w_a_up, w_g_up, k_k, k_a, r_k,
              ln_x_w, ln_x_b, b_forget, w_br_rwkv, w_br_fox, w_out, norm_ffn, w_ffn_up, w_ffn_down,
              norm_final):
    bsz = x_prompt.shape[0]
    meta = jnp.broadcast_to(meta_tokens[None].astype(x_prompt.dtype), (bsz, N_META, D_MODEL))
    xp = jnp.concatenate([meta, x_prompt], axis=1)
    xs = x_sample
    p_shift, p_wkv, p_k, p_v, p_lf = [], [], [], [], []
    s_shift, s_wkv, s_k, s_v, s_lf = [], [], [], [], []
    for l in range(DEPTH):
        lw = {
            'norm_mix': norm_mix[l], 'w_in': w_in[l], 'mu_shift': mu_shift[l], 'w0': w0[l],
            'w_decay_up': w_decay_up[l], 'a0': a0[l], 'w_a_up': w_a_up[l], 'w_g_up': w_g_up[l],
            'k_k': k_k[l], 'k_a': k_a[l], 'r_k': r_k[l], 'ln_x_w': ln_x_w[l], 'ln_x_b': ln_x_b[l],
            'b_forget': b_forget[l], 'w_br_rwkv': w_br_rwkv[l], 'w_br_fox': w_br_fox[l],
            'w_out': w_out[l], 'norm_ffn': norm_ffn[l], 'w_ffn_up': w_ffn_up[l],
            'w_ffn_down': w_ffn_down[l],
        }
        shift0 = jnp.zeros((bsz, D_SHIFT), xp.dtype)
        wkv0 = jnp.zeros((bsz, H_RWKV, RWKV_HEAD, RWKV_HEAD), xp.dtype)
        xp, (sh, wk, kr, vr, lr) = decoder_layer(xp, shift0, wkv0, attend_prompt, lw)
        p_shift.append(sh); p_wkv.append(wk); p_k.append(kr); p_v.append(vr); p_lf.append(lr)
        attend = functools.partial(attend_sample, cache_k[l], cache_v[l], cache_logf[l], page_table)
        xs, (sh, wk, kr, vr, lr) = decoder_layer(xs, state_shift[l], state_wkv[l], attend, lw)
        s_shift.append(sh); s_wkv.append(wk); s_k.append(kr); s_v.append(vr); s_lf.append(lr)
    y_prompt = rms_norm(xp[:, N_META:], norm_final)
    y_sample = rms_norm(xs, norm_final)
    return (y_prompt, y_sample,
            jnp.stack(p_shift), jnp.stack(p_wkv), jnp.stack(p_k), jnp.stack(p_v), jnp.stack(p_lf),
            jnp.stack(s_shift), jnp.stack(s_wkv), jnp.stack(s_k), jnp.stack(s_v), jnp.stack(s_lf))


_drawn_inputs = setup_inputs


def setup_inputs(seed=0):
    import zlib

    import numpy as np

    out = dict(_drawn_inputs(seed))
    spreads = {}
    factors = {'k_k': 25.417,
     'ln_x_w': 21.747,
     'ln_x_b': 22.068,
     'norm_ffn': 3.221,
     'norm_final': 24.936,
     'cache_logf': 24.239,
     'r_k': 4.428}
    for name, (base, spread) in spreads.items():
        noise = np.random.default_rng([zlib.crc32(name.encode()), seed]).standard_normal(out[name].shape)
        drawn = base * np.exp(spread * noise) if base else spread * noise
        out[name] = __import__('jax').numpy.asarray(drawn.astype(out[name].dtype))
    for name, factor in factors.items():
        out[name] = (out[name] * factor).astype(out[name].dtype)
    return out
```

```python
from contextlib import ExitStack

import concourse.bass as bass
from concourse import mybir
from concourse.alu_op_type import AluOpType as ALU

F32 = mybir.dt.float32
I32 = mybir.dt.int32
ACT = mybir.ActivationFunctionType
AX = mybir.AxisListType

P = 128
D = 1024
KT = D // P
T_META, SEQ, DEC = 16, 1024, 8
TP = T_META + SEQ
TS = TP + DEC
TT = 1050
NG, G = 3, TT // 3
C = 104
NC = TP // C
HD = 64
NH = 8
HP = NH // 2
PAGE, NPG, POOL = 128, 8, 80
VW = NH * HD + NH
FF_CH = 4
RW_T = 14
SCALE = HD ** -0.5
E_HALF = 0.6065306597126334

C_ID, C_ONE, C_BLK, C_SUF = 0, 128, 256, 384
C_AM = 512
C_CM = C_AM + C
C_LV = C_CM + 2 * C
N_LV = 7
C_ALL = C_LV + N_LV * C
V_NM, V_NF, V_NL, V_MU, V_W0, V_A0, V_KK, V_KA, V_RK, V_LW, V_LB, V_EPS, V_GEPS, V_BF = (
    0, 8, 16, 24, 38, 42, 46, 50, 54, 58, 62, 66, 67, 68)
V_ALL = 70

PV_FOX, PV_RW, PV_GATE, PV_OUT, PV_FF = 6, 7, 16, 4, 32
V_RW0 = PV_FOX
V_GATE0 = V_RW0 + PV_RW
V_OUT0 = V_GATE0 + PV_GATE
V_FF0 = V_OUT0 + PV_OUT
PAIRS = V_FF0 + PV_FF

SB_COLS = 56900


class Order:

    def __init__(self, eng, sem):
        self.eng, self.sem, self.base, self.n = eng, sem, 0, 0

    def __call__(self, ins):
        self.n += 1
        ins.then_inc(self.sem, 1)
        self.eng.wait_ge(self.sem, self.base + self.n)

    def enter(self, i, per):
        self.outer, self.per = self.base + self.n, per
        self.base, self.n = self.outer + i * per, 0

    def leave(self, count):
        assert self.n == self.per, ("steps in the loop's body", self.n, self.per)
        self.base, self.n = self.outer + count * self.per, 0


class Steps:

    def __init__(self, sem, names):
        self.sem, self.names, self.next = sem, names, 0

    def after(self, c, name):
        return c * len(self.names) + (self.names.index(name) + 2)

    def before(self, c):
        return c * len(self.names) + 1

    def done(self, ins, name):
        assert self.names[self.next] == name, (self.names[self.next], name)
        self.next = (self.next + 1) % len(self.names)
        ins.then_inc(self.sem, 1)


def build(nc, A, debug=None):
    with ExitStack() as ctx:
        def sem(name):
            return ctx.enter_context(nc.semaphore(name))

        SB = ctx.enter_context(nc.sbuf_tensor("sb", [P, SB_COLS], F32))
        PT_SB = ctx.enter_context(nc.sbuf_tensor("page_ids", [1, DEC * NPG], I32))
        PS = ctx.enter_context(nc.psum_tensor("ps", [P, 8, 512], F32))
        h_dram = nc.dram_tensor("h_dram", [P, KT * TT], F32, kind="Internal").ap()
        cneg_dram = nc.dram_tensor("cneg_dram", [NH, TP], F32, kind="Internal").ap()
        samp_dram = nc.dram_tensor("samp_dram", [6, DEC, NH * HD], F32, kind="Internal").ap()
        ysamp_dram = nc.dram_tensor("ysamp_dram", [DEC, NH, HD], F32, kind="Internal").ap()

        def view(at, *dims):
            n = 1
            for d in dims:
                n *= d
            assert at + n <= SB_COLS, (at, n)
            v = SB[:, at:at + n]
            if len(dims) == 2:
                v = v.rearrange("p (a b) -> p a b", a=dims[0])
            if len(dims) == 3:
                v = v.rearrange("p (a b c) -> p a b c", a=dims[0], b=dims[1])
            if len(dims) == 4:
                v = v.rearrange("p (a b c d) -> p a b c d", a=dims[0], b=dims[1], c=dims[2])
            return v

        class Region:

            def __init__(self, at, n):
                self.at, self.end = at, at + n

            def take(self, *dims):
                n = 1
                for d in dims:
                    n *= d
                v = view(self.at, *dims)
                self.at += n
                assert self.at <= self.end, (self.at, self.end)
                return v

        whole = Region(0, SB_COLS)
        cst = whole.take(C_ALL)
        par = whole.take(V_ALL)
        W = whole.take(2, D)
        wl = whole.take(512)
        wg = whole.take(512)
        wf = whole.take(KT, NH)
        lfT = whole.take(TT)
        ht_at = whole.at
        HT = whole.take(KT, TT)
        xt_at = whole.at
        XT = whole.take(KT, TT)
        FX = whole.take(12, TT)
        rw_at = whole.at
        RW = whole.take(RW_T, TT)
        scr_at = whole.at
        scr_n = SB_COLS - scr_at

        ident = cst[:, C_ID:C_ID + P]
        ones = cst[:, C_ONE:C_ONE + P]
        blk = cst[:, C_BLK:C_BLK + P]
        suf = cst[:, C_SUF:C_SUF + P]

        def grp(slot):
            return PS[:, 3 * slot:3 * slot + 3, 0:G]

        def g3(ap):
            return ap.rearrange("p (g n) -> p g n", g=NG)

        consts_in, x_in, state_in = sem("consts_in"), sem("x_in"), sem("state_in")
        w_in = [sem("w_in0"), sem("w_in1")]
        unit_done = sem("unit_done")
        evac = [sem("evac0"), sem("evac1")]
        act_order, dve_order = sem("act_order"), sem("dve_order")
        out_stored, kv_stored, sh_stored = sem("out_stored"), sem("kv_stored"), sem("sh_stored")
        sq_ready, sq_added = sem("sq_ready"), sem("sq_added")
        ssum_ready, rms_ready, h_ready = sem("ssum_ready"), sem("rms_ready"), sem("h_ready")
        h_stored, h_back = sem("h_stored"), sem("h_back")

        r_norm = Region(scr_at, scr_n)
        sq = r_norm.take(2, TT)
        sqsum = r_norm.take(TT)
        rstd = r_norm.take(TT)

        def pe_unit(pe, v, s, x, nk=KT):
            pe.wait_ge(w_in[s], 16 * (v + 1))
            if not isinstance(v, int) or v > 0:
                pe.wait_ge(evac[s], v)
            for k in range(nk):
                for g in range(NG):
                    last = pe.matmul(PS[:, 3 * s + g, 0:G], W[:, s, k * P:(k + 1) * P],
                                     x[:, k, g * G:(g + 1) * G], start=(k == 0), stop=(k == nk - 1))
            last.then_inc(unit_done, 1)

        def pe_norm(pe, n):
            pe.wait_ge(sq_added, KT * (n + 1))
            for g in range(NG):
                last = pe.matmul(PS[:, g, 0:G], ones, sqsum[:, g * G:(g + 1) * G], start=True, stop=True)
            last.then_inc(ssum_ready, 1)

        def act_norm(act, n):
            for k in range(KT):
                if KT * n + k >= 2:
                    act.wait_ge(sq_added, KT * n + k - 1)
                act.activation(sq[:, k % 2], XT[:, k, :], ACT.Square).then_inc(sq_ready, 1)
            act.wait_ge(ssum_ready, n + 1)
            act.activation(g3(rstd), grp(0), ACT.Sqrt, scale=1.0 / D,
                           bias=par[:, V_EPS:V_EPS + 1]).then_inc(rms_ready, 1)

        def dve_norm(dve, n, gain, order):
            for k in range(KT):
                dve.wait_ge(sq_ready, KT * n + k + 1)
                if k:
                    dve.wait_ge(sq_added, KT * n + k)
                    dve.tensor_tensor(sqsum, sqsum, sq[:, k % 2], ALU.add).then_inc(sq_added, 1)
                else:
                    dve.tensor_copy(sqsum, sq[:, 0]).then_inc(sq_added, 1)
            dve.wait_ge(rms_ready, n + 1)
            order(dve.reciprocal(rstd, rstd))
            for k in range(KT):
                dve.scalar_tensor_tensor(HT[:, k, :], XT[:, k, :], par[:, gain + k:gain + k + 1], rstd,
                                         ALU.mult, ALU.mult).then_inc(h_ready, 1)
            dve.wait_ge(h_ready, KT * (n + 1))

        f_ready, f_read, lf_ready = sem("f_ready"), sem("f_read"), sem("lf_ready")
        cneg_stored, cneg_in = sem("cneg_stored"), [sem("cneg_in0"), sem("cneg_in1")]
        vt_ready, vt_read = sem("vt_ready"), sem("vt_read")
        qk_free, qk_staged = sem("qk_free"), sem("qk_staged")
        s_done, max_ready, p_ready = sem("s_done"), sem("max_ready"), sem("p_ready")
        pt_done, pt_read = sem("pt_done"), [sem("pt_read0"), sem("pt_read1")]
        pv_done, o_read = sem("pv_done"), sem("o_read")
        ot_ready, ot_read = sem("ot_ready"), sem("ot_read")

        r_att = Region(rw_at, SB_COLS - rw_at)
        qa = r_att.take(2, TP)
        ka = r_att.take(2, TP)
        Pm = r_att.take(2, TP)
        PTm = r_att.take(2, NC, C)
        vnat = r_att.take(NC, 512)
        onat = r_att.take(NC, 512)
        rowmax = r_att.take(2)
        rowsum = r_att.take(4)
        rowinv = r_att.take(2)
        r_f = Region(rw_at, 4 * TT)
        f_neg, f_t, f_u, f_c = r_f.take(TT), r_f.take(TT), r_f.take(TT), r_f.take(TP)
        f_ones = r_att.take(TP)
        tiles = [(hl, qt) for hl in range(2) for qt in range(NC)]
        N_IT = len(tiles)
        groups = [-(-(qt + 1) // 4) for _, qt in tiles]
        N_GR = sum(groups)
        assert N_GR % 2 == 0
        gr_before = [sum(groups[:j]) for j in range(N_IT)]

        ids_in = sem("ids_in")
        kp_in = [sem("kp_in0"), sem("kp_in1")]
        vp_in = [sem("vp_in0"), sem("vp_in1")]
        lfp_in = sem("lfp_in")
        da_ready = sem("da_ready")
        da_step = sem("da_step")
        da_exp = sem("da_exp")
        kp_used, vp_used = sem("kp_used"), sem("vp_used")
        Kp = view(xt_at, 2, NPG, HP, PAGE)
        r_da = Region(rw_at, SB_COLS - rw_at)
        Vp = r_da.take(2, NPG, VW)
        lfp = r_da.take(DEC, NPG, NH)
        qbd = r_da.take(HP, DEC, 2)
        qkbd = r_da.take(HP, DEC, 2)
        lfd = r_da.take(DEC, NH)
        da_bias = r_da.take(DEC, NPG, NH)
        da_s = r_da.take(DEC, NPG, NH)
        da_own = r_da.take(DEC * NH)
        da_mx = r_da.take(DEC * NH)
        da_c1 = r_da.take(1)
        da_dg = r_da.take(DEC * NH)
        da_po = r_da.take(DEC * NH)
        da_den = r_da.take(DEC * NH)
        da_o = r_da.take(HP, DEC)

        mixed, mix_order = sem("mixed"), sem("mix_order")
        lora_in = sem("lora_in")
        pp, pa, pd = sem("prep_pe"), sem("prep_act"), sem("prep_dve")
        LW, KK = FX[:, HP:2 * HP, :], FX[:, 2 * HP:3 * HP, :]
        BB, BON = XT[:, 0:HP, :], XT[:, HP:2 * HP, :]
        r_rw = Region(scr_at, SB_COLS - scr_at)
        sh_in = r_rw.take(RW_T, DEC)
        sh_out = r_rw.take(RW_T, DEC + 1)
        mtmp = r_rw.take(TT)
        ptmp = [r_rw.take(TT), r_rw.take(TT)]

        r_ch = Region(ht_at, KT * TT)
        Lc, Lm = r_ch.take(HP, C), r_ch.take(HP, C)
        E1, E2, E3 = r_ch.take(HP, C), r_ch.take(HP, C), r_ch.take(HP, C)
        AR = r_ch.take(HP, 2, C)
        Kc, Bc, Vc = r_ch.take(HP, C), r_ch.take(HP, C), r_ch.take(HP, C)
        Kn, Bn, An, Vn = r_ch.take(512), r_ch.take(512), r_ch.take(512), r_ch.take(512)
        Xm, XTr = r_ch.take(NH, C), r_ch.take(NH, C)
        r_c2 = Region(scr_at, SB_COLS - scr_at)
        MK = r_c2.take(NH, 2, C)
        MB = r_c2.take(NH, 2, C)
        T1 = view(rw_at + 12 * TT, NH, C)
        Bm = r_c2.take(NH, C), r_c2.take(NH, C)
        Zm = r_c2.take(512)
        WT = r_c2.take(HP, C)
        NU = r_c2.take(512)
        St = r_ch.take(HP, HD)
        Yc = r_c2.take(512)
        gst = r_c2.take(4, NH)

        LEVELS = range(1, N_LV)
        ch_pe = Steps(sem("ch_pe"), ["nat_k", "nat_b", "nat_a", "nat_v"]
                      + [f"prod_{m}{i}" for i in range(2) for m in "kb"] + ["z", "x_0", "x_1"]
                      + [f"{t}_{lv}_{q}" for lv in LEVELS for t in ("t1", "t2") for q in range(2)]
                      + ["wt", "u", "y", "s", "yt"])
        ch_act = Steps(sem("ch_act"), ["v", "e1", "e3", "e2", "nat_k", "nat_a", "z", "x_0", "x_1"]
                       + [f"t1_{lv}_{q}" for lv in LEVELS for q in range(2)]
                       + ["wt", "nu", "ln", "rstd"] + [f"y_{p}" for p in range(HP)])
        ch_dve = Steps(sem("ch_dve"), [f"scan_{p}" for p in range(HP)] + ["lm", "r", "k", "b", "a", "nat_b", "nat_v"]
                       + [f"mask_{m}{i}" for i in range(2) for m in "kb"] + ["xt_init"]
                       + [f"x_{lv}_{q}_{t}" for lv in LEVELS for q in range(2)
                          for t in (("x", "xt") if lv < N_LV - 1 else ("xt",))]
                       + ["sum", "mean", "state", "center", "sq", "var", "norm"])
        ch_pool = Steps(sem("ch_pool"), [f"bm_{lv}" for lv in range(N_LV)])

        ds_pe, ds_act, ds_dve = sem("ds_pe"), sem("ds_act"), sem("ds_dve")
        ds_store, ds_load = sem("ds_store"), sem("ds_load")
        ds_y, ds_yb, ds_var = sem("ds_y"), sem("ds_yb"), sem("ds_var")
        o_pe, o_done = sem("o_pe"), sem("o_done")
        r_ds = Region(ht_at, KT * TT)
        dS = r_ds.take(DEC // 2, NH, HD)
        dW, dT = r_ds.take(DEC // 2, NH, HD), r_ds.take(DEC // 2, NH, HD)
        r_d2 = Region(scr_at, SB_COLS - scr_at)
        dKK, dB, dK = (r_d2.take(DEC // 2, NH, HD) for _ in range(3))
        dR = dKK
        r_d3 = Region(ht_at + 3 * 2048, KT * TT - 3 * 2048)
        d_col = r_d3.take(6, HP, DEC)
        d_nat = r_d3.take(6, P)
        dV, dU = r_d3.take(DEC // 2, NH), r_d3.take(DEC // 2, NH)
        dYn = r_d3.take(512)
        dst4 = r_d3.take(4, NH)
        dSQ = Yc

        h2_back, sg_ready, sg_used, mg_ready = h_back, sem("sg_ready"), sem("sg_used"), sem("mg_ready")
        ff_ready = sem("ff_ready")
        x_back = sem("x_back")
        xr_ready = sem("xr_ready")
        MG = FX[:, HP:3 * HP, :]
        SG = [view(scr_at, TT), view(scr_at + TT, TT)]
        gtmp = view(scr_at + 2 * TT, TT)
        FH = view(rw_at, KT, TT)
        RL = [view(rw_at + KT * TT, TT), view(rw_at + (KT + 1) * TT, TT)]
        lastn = sem("y_ready")

        def sflat(bank, n, c0=0):
            return PS[0:C, bank:bank + 3 if bank == 0 else bank + 2, :].rearrange("p a b -> p (a b)")[:, c0:c0 + n]

        block = ctx.enter_context(nc.Block())

        @block.sync
        def _(sp):
            def load_w(v, s, wait=True):
                if wait:
                    sp.wait_ge(unit_done, 2 * v + s - 1)
                sp.dma_start(W[:, s, :], A["wu"][bass.ds(2 * v + s, 1), :, :].rearrange("o p n -> (o p) n")
                             if not isinstance(v, int) else A["wu"][2 * v + s]).then_inc(w_in[s], 16)

            def load_pairs(v0, v1):
                with sp.Fori(v0, v1) as v:
                    load_w(v, 0)
                    load_w(v, 1)

            for n in range(4):
                sp.dma_start(XT[:, 2 * n:2 * n + 2, :], A["xt"][:, 2 * n:2 * n + 2, :]).then_inc(x_in, 16)
            sp.dma_start(cst, A["cst"]).then_inc(consts_in, 16)
            sp.dma_start(par, A["par"]).then_inc(consts_in, 16)
            load_w(0, 0, wait=False)
            load_w(0, 1, wait=False)
            sp.dma_start(wf, A["wf"]).then_inc(consts_in, 16)
            sp.dma_start(wl, A["wl"]).then_inc(consts_in, 16)
            sp.dma_start(wg, A["wg"]).then_inc(consts_in, 16)
            sp.dma_start(PT_SB[:, :], A["page_table"]).then_inc(ids_in, 16)
            load_pairs(1, V_RW0 + 1)
            sp.wait_ge(h_ready, KT)
            sp.dma_start(h_dram, HT.rearrange("p a b -> p (a b)")).then_inc(h_stored, 16)
            sp.wait_ge(lf_ready, 1)
            sp.dma_start(cneg_dram, f_c[0:NH, :]).then_inc(cneg_stored, 16)
            sp.dma_start(A["o_lf"], lfT[0:NH, :]).then_inc(out_stored, 16)
            sp.wait_ge(cneg_stored, 16)
            sp.wait_ge(evac[0], V_RW0)
            sp.wait_ge(evac[1], V_RW0)
            sp.dma_start(A["o_kv"], FX[:, HP:3 * HP, :]).then_inc(kv_stored, 16)
            with sp.Fori(0, HP) as i:
                for hl in range(2):
                    if hl == 0:
                        sp.wait_ge(qk_free, i + 1)
                    sp.dma_start(ka[HD:HD + 1, hl, :], cneg_dram[bass.ds(2 * i + hl, 1), :])\
                      .then_inc(cneg_in[hl], 16)

            sp.wait_ge(ids_in, 16)
            sp.wait_ge(ot_read, NC)

            def page_id(i, s, pg):
                at = bass.ds(i * (2 * NPG) + (s * NPG + pg), 1)
                return sp.value_load(PT_SB[0:1, at], min_val=0, max_val=POOL - 1)

            def load_keys(i, s):
                for pg in range(NPG):
                    page = page_id(i, s, pg)
                    sp.dma_start(Kp[:, s, pg, :, :],
                                 A["kp"][bass.ds(page, 1), :, :, :].rearrange("o p h t -> (o p) h t"))\
                      .then_inc(kp_in[s], 16)
                    sp.dma_start(lfp[:, bass.ds(2 * i + s, 1), pg, :].rearrange("p o h -> p (o h)"),
                                 A["vp"][bass.ds(page, 1), :, NH * HD:VW].rearrange("o p h -> (o p) h"))\
                      .then_inc(lfp_in, 16)

            def load_values(i, s):
                for pg in range(NPG):
                    page = page_id(i, s, pg)
                    sp.dma_start(Vp[:, s, pg, :],
                                 A["vp"][bass.ds(page, 1), :, :].rearrange("o p n -> (o p) n"))\
                      .then_inc(vp_in[s], 16)

            for load, used in ((load_keys, kp_used), (load_values, vp_used)):
                load(0, 0)
                load(0, 1)
                with sp.Fori(1, DEC // 2) as i:
                    for s in range(2):
                        sp.wait_ge(used, 2 * i + s - 1)
                        load(i, s)
            if debug == 'fox':
                sp.wait_ge(da_step, 6)
                sp.dma_start(A['dbg'], FX[:, 0:HP, :]).then_inc(out_stored, 16)
                sp.wait_ge(kv_stored, 16)
                sp.wait_ge(out_stored, 32)
                return

            load_pairs(V_RW0 + 1, V_GATE0 + 1)
            sp.wait_ge(da_step, 6)
            sp.dma_start(sh_in, A["sh"]).then_inc(lora_in, 16)
            sp.wait_ge(mixed, RW_T)
            sp.dma_start(A["o_sh"], sh_out).then_inc(sh_stored, 16)
            sp.wait_ge(ch_pe.sem, ch_pe.before(NC))
            sp.dma_start(A["o_sp"], St).then_inc(out_stored, 16)
            sp.wait_ge(ds_act, 2)
            for p in range(HP):
                sp.dma_start(samp_dram[:, :, p * P:(p + 1) * P].rearrange("k b c -> b k c"),
                             d_nat[p * DEC:(p + 1) * DEC]).then_inc(ds_store, 16)
            sp.dma_start(dS.rearrange("p b h k -> p (b h k)"), A["st"]).then_inc(ds_load, 16)
            sp.wait_ge(ds_store, 16 * HP)

            def spread(dst, kind):
                for e in range(2):
                    sp.dma_start(dst[e * HD:(e + 1) * HD].rearrange("p b h k -> p (b h k)"),
                                 samp_dram[kind, e * (DEC // 2):(e + 1) * (DEC // 2), :]
                                 .rearrange("b n -> (b n)").partition_broadcast(HD)).then_inc(ds_load, 16)

            for dst, kind in ((dKK, 1), (dW, 0), (dB, 2), (dK, 3)):
                spread(dst, kind)
            for e in range(2):
                sp.dma_start(dV[e * HD:(e + 1) * HD],
                             samp_dram[5, e * (DEC // 2):(e + 1) * (DEC // 2), :]
                             .rearrange("b (h v) -> v b h", h=NH),
                             allow_slow_non_contiguous=True).then_inc(ds_load, 16)
            sp.wait_ge(ds_dve, 1)
            spread(dR, 4)
            sp.wait_ge(ds_dve, 2)
            sp.dma_start(A["o_ss"], dS.rearrange("p b h k -> p (b h k)")).then_inc(out_stored, 16)
            sp.wait_ge(ds_dve, 3)
            for e in range(2):
                sp.dma_start(ysamp_dram[e * (DEC // 2):(e + 1) * (DEC // 2)].rearrange("b h v -> v b h"),
                             dU[e * HD:(e + 1) * HD], allow_slow_non_contiguous=True).then_inc(ds_y, 16)
            sp.wait_ge(ds_y, 32)
            sp.dma_start(dYn[0:DEC], ysamp_dram.rearrange("b h v -> b (h v)")).then_inc(ds_yb, 16)
            sp.wait_ge(o_done, HP)
            sp.wait_ge(out_stored, 16 * 3)
            sp.dma_start(HT.rearrange("p a b -> p (a b)"), h_dram).then_inc(h_back, 16)
            sp.dma_start(XT, A["xt"]).then_inc(x_back, 16)
            if debug == 'rw':
                sp.wait_ge(h_back, 16)
                sp.wait_ge(x_back, 16)
                sp.dma_start(A['dbg'], RW[:, 0:HP, :]).then_inc(out_stored, 16)
                sp.wait_ge(out_stored, 64)
                return
            load_pairs(V_GATE0 + 1, PAIRS)
            for k in range(KT):
                sp.wait_ge(lastn, k + 1)
                sp.dma_start(A["o_y"][:, k, :], HT[:, k, :]).then_inc(out_stored, 16)
            sp.wait_ge(out_stored, 16 * (3 + KT))

        @block.tensor
        def _(pe):
            pe.wait_ge(consts_in, 80)
            pe_norm(pe, 0)
            pe.wait_ge(h_ready, KT)
            pe_unit(pe, 0, 0, HT)
            pe_unit(pe, 0, 1, HT)
            with pe.Fori(1, PV_FOX) as v:
                pe_unit(pe, v, 0, HT)
                pe_unit(pe, v, 1, HT)
            pe.wait_ge(evac[0], PV_FOX)
            for k in range(KT):
                for g in range(NG):
                    last = pe.matmul(PS[0:NH, g, 0:G], wf[:, k, :], HT[:, k, g * G:(g + 1) * G],
                                     start=(k == 0), stop=(k == KT - 1))
            last.then_inc(f_ready, 1)
            pe.wait_ge(evac[1], PV_FOX)
            for t in range(NC):
                if t >= 2:
                    pe.wait_ge(vt_read, t - 1)
                for hp in range(HP):
                    last = pe.transpose(PS[0:C, 6 + t % 2, hp * P:(hp + 1) * P],
                                        FX[:, 2 * HP + hp, t * C:(t + 1) * C], ident)
                last.then_inc(vt_ready, 1)

            pe.wait_ge(vt_read, NC)
            pe.wait_ge(f_read, 1)
            with pe.Fori(0, HP) as i:
                def scores(j):
                    hl, qt = tiles[j]
                    if qt == 0:
                        pe.wait_ge(qk_staged, 2 * i + hl + 1)
                        pe.wait_ge(cneg_in[hl], 16 * i + 16)
                    bank = 0 if j % 2 else 3
                    if j >= 2:
                        pe.wait_ge(p_ready, N_IT * i + j - 1)
                    for c0 in range(0, (qt + 1) * C, 512):
                        n = min(512, (qt + 1) * C - c0)
                        last = pe.matmul(PS[0:C, bank + c0 // 512, 0:n],
                                         qa[0:HD + 1, hl, qt * C:(qt + 1) * C],
                                         ka[0:HD + 1, hl, c0:c0 + n], start=True, stop=True)
                    last.then_inc(s_done, 1)

                def transposed(j):
                    hl, qt = tiles[j]
                    pe.wait_ge(p_ready, N_IT * i + j + 1)
                    for g in range(groups[j]):
                        n = gr_before[j] + g
                        slot = n % 2
                        if n >= 2:
                            pe.wait_ge(pt_read[slot], (N_GR // 2) * i + n // 2)
                        for b in range(4 * g, min(4 * g + 4, qt + 1)):
                            last = pe.transpose(PS[0:C, 5 + slot, (b - 4 * g) * C:(b - 4 * g + 1) * C],
                                                Pm[0:C, j % 2, b * C:(b + 1) * C], ident[0:C, 0:C])
                        last.then_inc(pt_done, 1)

                def values(j):
                    hl, qt = tiles[j]
                    end = gr_before[j] + groups[j]
                    pe.wait_ge(pt_read[0], (N_GR // 2) * i + (end + 1) // 2)
                    if end >= 2:
                        pe.wait_ge(pt_read[1], (N_GR // 2) * i + end // 2)
                    if j:
                        pe.wait_ge(o_read, N_IT * i + j)
                    for b in range(qt + 1):
                        last = pe.matmul(PS[0:C, 7, 0:HD], PTm[0:C, j % 2, b, :],
                                         vnat[0:C, b, bass.ds(i * P + hl * HD, HD)],
                                         start=(b == 0), stop=(b == qt))
                    last.then_inc(pv_done, 1)

                scores(0)
                for j in range(N_IT):
                    if j + 1 < N_IT:
                        scores(j + 1)
                    transposed(j)
                    if j:
                        values(j - 1)
                values(N_IT - 1)
            for t in range(NC):
                pe.wait_ge(o_read, N_IT * HP)
                if t >= 2:
                    pe.wait_ge(ot_read, t - 1)
                for hp in range(HP):
                    last = pe.transpose(PS[:, 6 + t % 2, hp * C:(hp + 1) * C],
                                        onat[0:C, t, hp * P:(hp + 1) * P], ident[0:C, 0:C])
                last.then_inc(ot_ready, 1)
            pe.wait_ge(ot_read, NC)

            pe.wait_ge(da_step, 1)
            with pe.Fori(0, DEC // 2) as i:
                for s in range(2):
                    pe.wait_ge(kp_in[s], 16 * NPG * i + 16 * NPG)
                    for pg in range(NPG):
                        for hp in range(HP):
                            last = pe.matmul(
                                PS[:, 6, bass.ds(i * 2 * NPG * NH + (s * NPG + pg) * NH + 2 * hp, 2)],
                                Kp[:, s, pg, hp, :],
                                qbd[:, hp, bass.ds(2 * i + s, 1), :].rearrange("p o h -> p (o h)"),
                                start=True, stop=True)
                    last.then_inc(kp_used, 1)
            pe.wait_ge(lfp_in, 16 * NPG * DEC)
            bias4 = PS[:, 7, :].rearrange("p (b g h) -> p b g h", b=DEC, g=NPG)
            pe.matmul(PS[:, 7, :], suf, lfp.rearrange("p b g h -> p (b g h)"), start=True, stop=False)
            for s in range(1, NPG):
                pe.matmul(bias4[:, :, 0:NPG - s, :], ones, lfp[:, :, s:NPG, :], start=False, stop=False)
            last = pe.matmul(bias4, ones[0:NH, :],
                             lfd[0:NH].unsqueeze(2).to_broadcast([NH, DEC, NPG, NH]), start=False, stop=True)
            last.then_inc(da_ready, 1)
            last = pe.matmul(PS[:, 5, 0:DEC * NH].rearrange("p (b a h) -> p a b h", b=DEC, a=HP), ones,
                             qkbd, start=True, stop=True)
            last.then_inc(da_ready, 1)
            pe.wait_ge(da_step, 2)
            pe.transpose(PS[0:DEC * NH, 4, 0:P], da_mx, ident).then_inc(da_ready, 1)
            pe.wait_ge(da_step, 3)
            pe.matmul(PS[:, 4, 256:256 + DEC * NH], ones[0:DEC * NH, :], da_dg[0:DEC * NH], start=True,
                      stop=True).then_inc(da_ready, 1)
            pe.wait_ge(da_step, 5)
            pe.matmul(PS[:, 4, 384:384 + DEC * NH], ones, da_den, start=True, stop=True)\
              .then_inc(da_ready, 1)
            with pe.Fori(0, DEC // 2) as i:
                for s in range(2):
                    pe.wait_ge(vp_in[s], 16 * NPG * i + 16 * NPG)
                    for hp in range(HP):
                        for pg in range(NPG):
                            last = pe.matmul(
                                PS[:, 7, bass.ds(i * 4 + 2 * s + 2 * DEC * hp, 2)],
                                Vp[:, s, pg, hp * P:(hp + 1) * P],
                                da_s[:, bass.ds(2 * i + s, 1), pg, 2 * hp:2 * hp + 2]
                                .rearrange("p o h -> p (o h)"),
                                start=(pg == 0), stop=(pg == NPG - 1))
                    last.then_inc(vp_used, 1)
            if debug == 'fox':
                return

            pe.wait_ge(da_step, 6)
            with pe.Fori(V_RW0, V_RW0 + PV_RW) as v:
                pe_unit(pe, v, 0, HT)
                pe_unit(pe, v, 1, HT)
            pe.wait_ge(evac[0], V_GATE0)
            pe.wait_ge(evac[1], V_GATE0)
            pe.wait_ge(pa, 2)
            for p in range(HP):
                for m in range(2):
                    if p:
                        pe.wait_ge(pa, 2 + 2 * p - 1 + m)
                    rows = slice(m * HD, (m + 1) * HD)
                    for g in range(NG):
                        last = pe.matmul(PS[:, 3 * m + g, 0:G], wl[rows, p * P:(p + 1) * P],
                                         RW[rows, 12, g * G:(g + 1) * G], start=True, stop=True)
                    last.then_inc(pp, 1)
            for p in range(HP):
                for m in range(2):
                    if p == 0:
                        pe.wait_ge(pa, 10)
                    pe.wait_ge(pd, 3 * p + 1 + m)
                    if p and m == 0:
                        pe.wait_ge(pa, 10 + p)
                    if p and m == 1:
                        pe.wait_ge(pd, 3 * p)
                    for g in range(NG):
                        last = pe.matmul(PS[:, 3 * m + g, 0:G], blk, ptmp[m][:, g * G:(g + 1) * G],
                                         start=True, stop=True)
                    last.then_inc(pp, 1)

            pe.wait_ge(pd, 3 * HP)
            pe.sem_inc(ch_pe.sem, 1)
            with pe.Fori(0, NC) as c:
                def wait(steps, name):
                    pe.wait_ge(steps.sem, steps.after(c, name))

                def natural(src, bank, name):
                    for p in range(HP):
                        last = pe.transpose(PS[0:C, bank, p * P:(p + 1) * P], src[:, p], ident)
                    ch_pe.done(last, name)

                def vcols(h):
                    at = h % HP * P + h // HP * HD
                    return slice(at, at + HD)

                def hrows(h):
                    return slice(h // HP * HD, (h // HP + 1) * HD)

                wait(ch_dve, "k")
                pe.wait_ge(ch_dve.sem, ch_dve.before(c))
                pe.wait_ge(ch_act.sem, ch_act.before(c))
                natural(Kc, 0, "nat_k")
                wait(ch_dve, "b")
                natural(Bc, 1, "nat_b")
                wait(ch_dve, "a")
                natural(AR[:, :, 0], 2, "nat_a")
                natural(Vc, 3, "nat_v")
                for i in range(2):
                    for m, src, bank in (("k", Kc, 4), ("b", Bc, 6)):
                        if i:
                            wait(ch_dve, f"mask_{m}0")
                        for j in range(2):
                            for e in range(2):
                                rows, p = slice(e * HD, (e + 1) * HD), 2 * i + j
                                last = pe.matmul(PS[0:C, bank + e, j * 2 * C:(j + 1) * 2 * C], src[rows, p],
                                                 AR[rows, p].rearrange("p a b -> p (a b)"), start=True,
                                                 stop=True)
                        ch_pe.done(last, f"prod_{m}{i}")
                wait(ch_dve, "mask_k1")
                wait(ch_dve, "nat_v")
                for h in range(NH):
                    last = pe.matmul(PS[0:C, 3, h * HD:(h + 1) * HD], MK[0:C, h, 0], Vn[0:C, vcols(h)],
                                     start=True, stop=True)
                ch_pe.done(last, "z")
                wait(ch_dve, "xt_init")
                wait(ch_act, "nat_k")
                wait(ch_dve, "nat_b")
                for q in range(2):
                    for j in range(4):
                        last = pe.transpose(PS[0:C, q, j * C:(j + 1) * C], XTr[0:C, 4 * q + j], ident[0:C, 0:C])
                    ch_pe.done(last, f"x_{q}")
                for lv in LEVELS:
                    for q in range(2):
                        if q == 0:
                            pe.wait_ge(ch_pool.sem, ch_pool.after(c, f"bm_{lv}"))
                        if lv == 1:
                            wait(ch_act, f"x_{q}")
                        else:
                            wait(ch_dve, f"x_{lv - 1}_{q}_xt")
                        for j in range(4):
                            h = 4 * q + j
                            last = pe.matmul(PS[0:C, q, j * C:(j + 1) * C], Bm[lv % 2][0:C, h], Xm[0:C, h],
                                             start=True, stop=True)
                        ch_pe.done(last, f"t1_{lv}_{q}")
                    for q in range(2):
                        wait(ch_act, f"t1_{lv}_{q}")
                        if lv == 1 and q == 0:
                            wait(ch_act, "nat_a")
                        for j in range(4):
                            h = 4 * q + j
                            if lv < N_LV - 1:
                                pe.matmul(PS[0:C, 2 + q, j * C:(j + 1) * C], XTr[0:C, h], T1[0:C, h],
                                          start=True, stop=True)
                            last = pe.matmul(PS[0:C, 4 + q, j * C:(j + 1) * C], T1[0:C, h], XTr[0:C, h],
                                             start=True, stop=True)
                        ch_pe.done(last, f"t2_{lv}_{q}")
                wait(ch_dve, f"x_{N_LV - 1}_1_xt")
                for h in range(NH):
                    e, p = h // HP, h % HP
                    last = pe.matmul(PS[e * HD:(e + 1) * HD, 0, p * C:(p + 1) * C], An[0:C, vcols(h)],
                                     XTr[0:C, h], start=True, stop=True)
                ch_pe.done(last, "wt")
                wait(ch_act, "wt")
                wait(ch_act, "z")
                for h in range(NH):
                    e, p, rows = h // HP, h % HP, hrows(h)
                    out = PS[0:C, 6 + e, p * HD:(p + 1) * HD]
                    pe.matmul(out, XTr[0:C, h], Zm[0:C, h * HD:(h + 1) * HD], start=True, stop=False)
                    last = pe.matmul(out, WT[rows, p], St[rows, p], start=False, stop=True)
                ch_pe.done(last, "u")
                wait(ch_act, "nu")
                for h in range(NH):
                    e, p, rows = h // HP, h % HP, hrows(h)
                    out = PS[0:C, 2 + e, p * HD:(p + 1) * HD]
                    pe.matmul(out, AR[rows, p, 1], St[rows, p], start=True, stop=False)
                    pe.matmul(out, MK[0:C, h, 1], Vn[0:C, vcols(h)], start=False, stop=False)
                    last = pe.matmul(out, MB[0:C, h, 1], NU[0:C, h * HD:(h + 1) * HD], start=False, stop=True)
                ch_pe.done(last, "y")
                for h in range(NH):
                    p, rows = h % HP, hrows(h)
                    out = PS[rows, 1, p * HD:(p + 1) * HD]
                    pe.matmul(out, ident[rows, rows], St[rows, p], start=True, stop=False)
                    pe.matmul(out, Kn[0:C, vcols(h)], Vn[0:C, vcols(h)], start=False, stop=False)
                    last = pe.matmul(out, Bn[0:C, vcols(h)], NU[0:C, h * HD:(h + 1) * HD], start=False, stop=True)
                ch_pe.done(last, "s")
                wait(ch_dve, "norm")
                for p in range(HP):
                    last = pe.transpose(PS[:, 0, p * C:(p + 1) * C], Yc[0:C, p * P:(p + 1) * P], ident[0:C, 0:C])
                ch_pe.done(last, "yt")

            pe.wait_ge(ch_act.sem, ch_act.before(NC))
            pe.wait_ge(ds_act, 1)
            for kind in range(6):
                last = pe.transpose(PS[0:HP * DEC, kind // 4, kind % 4 * P:(kind % 4 + 1) * P],
                                    d_col[:, kind].rearrange("p a b -> p (a b)"), ident)
            last.then_inc(ds_pe, 1)
            pe.wait_ge(ds_dve, 4)
            for p in range(HP):
                last = pe.transpose(PS[:, 2, p * DEC:(p + 1) * DEC], dYn[0:DEC, p * P:(p + 1) * P],
                                    ident[0:DEC, 0:DEC])
            last.then_inc(ds_pe, 1)
            for p in range(HP):
                s = p % 2
                if p == 0:
                    pe.wait_ge(ds_act, 3 + HP)
                if p >= 2:
                    pe.wait_ge(o_done, p - 1)
                for g in range(NG):
                    last = pe.matmul(PS[:, 3 * s + g, 0:G], wg[:, p * P:(p + 1) * P],
                                     RW[:, 13, g * G:(g + 1) * G], start=True, stop=True)
                last.then_inc(o_pe, 1)
            pe.wait_ge(o_done, HP)
            if debug == 'rw':
                return

            pe.wait_ge(h_back, 16)
            with pe.Fori(0, KT) as n:
                pe_unit(pe, 2 * n + V_GATE0, 0, HT)
                pe_unit(pe, 2 * n + V_GATE0, 1, HT)
                pe_unit(pe, 2 * n + V_GATE0 + 1, 0, RW, HP)
                pe_unit(pe, 2 * n + V_GATE0 + 1, 1, FX, HP)
            pe.wait_ge(mg_ready, KT)
            with pe.Fori(V_OUT0, V_OUT0 + PV_OUT) as v:
                pe_unit(pe, v, 0, MG)
                pe_unit(pe, v, 1, MG)
            pe.wait_ge(evac[0], V_FF0)
            pe_norm(pe, 1)
            pe.wait_ge(h_ready, 2 * KT)
            with pe.Fori(0, FF_CH) as c:
                with pe.Fori(0, KT // 2) as j:
                    pe_unit(pe, KT * c + j + V_FF0, 0, HT)
                    pe_unit(pe, KT * c + j + V_FF0, 1, HT)
                with pe.Fori(0, KT // 2) as j:
                    pe.wait_ge(ff_ready, KT * c + (KT + 2))
                    pe_unit(pe, KT * c + j + (V_FF0 + KT // 2), 0, FH)
                    pe_unit(pe, KT * c + j + (V_FF0 + KT // 2), 1, FH)
            pe.wait_ge(evac[0], PAIRS)
            pe_norm(pe, 2)

        @block.scalar
        def _(act):
            order = Order(act, act_order)
            act.wait_ge(consts_in, 80)
            act.wait_ge(x_in, 64)
            act_norm(act, 0)

            def keep(v, s, dst):
                act.wait_ge(unit_done, 2 * v + s + 1)
                act.copy(g3(dst), grp(s)).then_inc(evac[s], 1)

            with act.Fori(0, PV_FOX) as v:
                for s in range(2):
                    keep(v, s, FX[:, bass.ds(2 * v + s, 1), :].rearrange("p o n -> p (o n)"))
            act.wait_ge(f_ready, 1)
            order(act.activation(g3(f_neg[0:NH]), PS[0:NH, 0:3, 0:G], ACT.Identity,
                                 bias=par[0:NH, V_BF:V_BF + 1]))
            order(act.activation(f_t[0:NH], f_neg[0:NH], ACT.Abs))
            order(act.activation(f_t[0:NH], f_t[0:NH], ACT.Exp, scale=-1.0))
            act.activation(f_t[0:NH], f_t[0:NH], ACT.Ln,
                           bias=cst[0:NH, C_ONE:C_ONE + 1]).then_inc(f_read, 1)
            for t in range(NC):
                act.wait_ge(vt_ready, t + 1)
                act.copy(vnat[0:C, t, :], PS[0:C, 6 + t % 2, :]).then_inc(vt_read, 1)

            with act.Fori(0, HP) as i:
                def exps(j):
                    hl, qt = tiles[j]
                    bank = 0 if j % 2 else 3
                    n = (qt + 1) * C
                    act.wait_ge(max_ready, N_IT * i + j + 1)
                    if j >= 2:
                        act.wait_ge(pt_done, N_GR * i + gr_before[j - 1])
                    if j >= 4:
                        act.wait_ge(o_read, N_IT * i + j - 3)
                    act.activation(Pm[0:C, j % 2, 0:n], sflat(bank, n), ACT.Exp,
                                   bias=rowmax[0:C, j % 2:j % 2 + 1],
                                   accum_out=rowsum[0:C, j % 4:j % 4 + 1]).then_inc(p_ready, 1)

                def blocks(j):
                    hl, qt = tiles[j]
                    for g in range(groups[j]):
                        n = gr_before[j] + g
                        if n % 2 == 0:
                            act.wait_ge(pt_done, N_GR * i + n + 1)
                            if g == 0 or g == 1:
                                if j >= 2:
                                    act.wait_ge(pv_done, N_IT * i + j - 1)
                            m = min(4, qt + 1 - 4 * g)
                            act.copy(PTm[0:C, j % 2, 4 * g:4 * g + m, :],
                                     PS[0:C, 5, 0:m * C].rearrange("p (a b) -> p a b", a=m))\
                               .then_inc(pt_read[0], 1)

                exps(0)
                for j in range(N_IT):
                    if j + 1 < N_IT:
                        exps(j + 1)
                    blocks(j)
            for t in range(NC):
                act.wait_ge(ot_ready, t + 1)
                act.copy(FX[:, 0:HP, t * C:(t + 1) * C],
                         PS[:, 6 + t % 2, 0:HP * C].rearrange("p (a b) -> p a b", a=HP)).then_inc(ot_read, 1)
            act.wait_ge(da_step, 4)
            act.activation(da_s.rearrange("p b g h -> p (b g h)"), da_s.rearrange("p b g h -> p (b g h)"),
                           ACT.Exp).then_inc(da_exp, 1)
            act.activation(da_po, da_po, ACT.Exp).then_inc(da_exp, 1)
            if debug == 'fox':
                return

            act.wait_ge(da_step, 6)
            with act.Fori(V_RW0, V_RW0 + PV_RW) as v:
                for s in range(2):
                    keep(v, s, RW[:, bass.ds(2 * v + (s - 2 * V_RW0), 1), :].rearrange("p o n -> p (o n)"))
            act.wait_ge(mixed, RW_T)
            act.activation(RW[0:HD, 12, :], RW[0:HD, 12, :], ACT.Tanh).then_inc(pa, 1)
            act.activation(RW[:, 13, :], RW[:, 13, :], ACT.Sigmoid).then_inc(pa, 1)
            act.wait_ge(kv_stored, 16)
            for p in range(HP):
                for m, dst, par0 in ((0, LW, V_W0), (1, BB, V_A0)):
                    act.wait_ge(pp, 2 * p + m + 1)
                    act.activation(g3(dst[:, p]), grp(m), ACT.Sigmoid,
                                   bias=par[:, par0 + p:par0 + p + 1]).then_inc(pa, 1)
            for p in range(HP):
                act.wait_ge(pp, 2 * HP + 2 * p + 1)
                act.activation(g3(ptmp[0]), grp(0), ACT.Sqrt).then_inc(pa, 1)
            act.wait_ge(pd, 3 * HP)
            act.sem_inc(ch_act.sem, 1)
            with act.Fori(0, NC) as c:
                def wait(steps, name):
                    act.wait_ge(steps.sem, steps.after(c, name))

                here = bass.ds(c * C, C)
                act.wait_ge(ch_pe.sem, ch_pe.before(c))
                act.wait_ge(ch_dve.sem, ch_dve.before(c))
                ch_act.done(act.copy(Vc, RW[:, 2 * HP:3 * HP, here]), "v")
                wait(ch_dve, "scan_3")
                ch_act.done(act.activation(E1, Lc, ACT.Exp), "e1")
                ch_act.done(act.activation(E3, Lc, ACT.Exp, scale=-1.0), "e3")
                wait(ch_dve, "lm")
                ch_act.done(act.activation(E2, Lm, ACT.Exp), "e2")
                wait(ch_pe, "nat_k")
                ch_act.done(act.copy(Kn[0:C], PS[0:C, 0, :]), "nat_k")
                wait(ch_pe, "nat_a")
                ch_act.done(act.copy(An[0:C], PS[0:C, 2, :]), "nat_a")
                wait(ch_pe, "z")
                ch_act.done(act.copy(Zm[0:C], PS[0:C, 3, :]), "z")

                def quad(ap, q):
                    return ap[0:C, 4 * q:4 * q + 4].rearrange("p a b -> p (a b)")

                for q in range(2):
                    wait(ch_pe, f"x_{q}")
                    ch_act.done(act.copy(quad(Xm, q), PS[0:C, q, 0:4 * C]), f"x_{q}")
                for lv in LEVELS:
                    for q in range(2):
                        wait(ch_pe, f"t1_{lv}_{q}")
                        if lv > 1:
                            wait(ch_pe, f"t2_{lv - 1}_{q}")
                        ch_act.done(act.copy(quad(T1, q), PS[0:C, q, 0:4 * C]), f"t1_{lv}_{q}")
                wait(ch_pe, "wt")
                ch_act.done(act.copy(WT, PS[:, 0, 0:HP * C].rearrange("p (a b) -> p a b", a=HP)), "wt")
                wait(ch_pe, "u")
                ch_act.done(act.mul(NU[0:C].rearrange("p (e n) -> p e n", e=2), PS[0:C, 6:8, 0:HP * HD],
                                    -1.0), "nu")
                wait(ch_dve, "var")
                ch_act.done(act.activation(gst[0:C, 2], gst[0:C, 1], ACT.Ln, scale=1.0 / HD,
                                           bias=par[0:C, V_GEPS:V_GEPS + 1]), "ln")
                wait(ch_act, "ln")
                ch_act.done(act.activation(gst[0:C, 3], gst[0:C, 2], ACT.Exp, scale=-0.5), "rstd")
                wait(ch_pe, "yt")
                for p in range(HP):
                    ch_act.done(act.activation(RW[:, p, here], PS[:, 0, p * C:(p + 1) * C], ACT.Identity,
                                               scale=par[:, V_LW + p:V_LW + p + 1],
                                               bias=par[:, V_LB + p:V_LB + p + 1]), f"y_{p}")
            act.wait_ge(ch_pe.sem, ch_pe.before(NC))
            for kind, src in ((1, KK), (2, BB), (3, RW[:, HP:2 * HP]), (4, RW[:, 0:HP]), (5, RW[:, 2 * HP:3 * HP])):
                order(act.copy(d_col[:, kind], src[:, :, TP:TS]))
            act.activation(d_col[:, 0], LW[:, :, TP:TS], ACT.Exp).then_inc(ds_act, 1)
            act.wait_ge(ds_pe, 1)
            act.copy(d_nat[0:HP * DEC].rearrange("p k c -> p (k c)"),
                     PS[0:HP * DEC, 0:2, :].rearrange("p a b -> p (a b)")[:, 0:6 * P]).then_inc(ds_act, 1)
            act.wait_ge(ds_var, 1)
            order(act.activation(dst4[0:DEC, 2], dst4[0:DEC, 1], ACT.Ln, scale=1.0 / HD,
                                 bias=par[0:DEC, V_GEPS:V_GEPS + 1]))
            act.activation(dst4[0:DEC, 3], dst4[0:DEC, 2], ACT.Exp, scale=-0.5).then_inc(ds_act, 1)
            act.wait_ge(ds_pe, 2)
            for p in range(HP):
                act.activation(RW[:, p, TP:TS], PS[:, 2, p * DEC:(p + 1) * DEC], ACT.Identity,
                               scale=par[:, V_LW + p:V_LW + p + 1],
                               bias=par[:, V_LB + p:V_LB + p + 1]).then_inc(ds_act, 1)
            if debug == 'rw':
                return
            act.wait_ge(o_done, HP)
            with act.Fori(0, KT) as n:
                for s in range(2):
                    act.wait_ge(unit_done, 4 * n + (2 * V_GATE0 + s + 1))
                    act.wait_ge(sg_used, 2 * n + (s + 1))
                    act.activation(g3(SG[s]), grp(s), ACT.Sigmoid).then_inc(evac[s], 1)
            act.wait_ge(xr_ready, KT)
            act_norm(act, 1)
            with act.Fori(0, FF_CH) as c:
                with act.Fori(0, KT // 2) as j:
                    for s in range(2):
                        act.wait_ge(unit_done, 2 * KT * c + 2 * j + (2 * V_FF0 + s + 1))
                        act.wait_ge(ff_ready, KT * c + 2 * j + (s + 1))
                        act.activation(g3(RL[s]), grp(s), ACT.Relu).then_inc(evac[s], 1)
            act.wait_ge(evac[0], PAIRS)
            act.wait_ge(evac[1], PAIRS)
            act_norm(act, 2)

        @block.vector
        def _(dve):
            order = Order(dve, dve_order)
            dve.wait_ge(consts_in, 80)
            dve.wait_ge(x_in, 64)
            dve_norm(dve, 0, V_NM, order)
            order(dve.memset(f_ones[0:NH], 1.0))
            dve.wait_ge(f_read, 1)
            order(dve.tensor_scalar(f_u[0:NH], f_neg[0:NH], 0.0, None, ALU.min))
            order(dve.tensor_tensor(lfT[0:NH], f_u[0:NH], f_t[0:NH], ALU.subtract))
            order(dve.tensor_tensor_scan(f_c[0:NH], f_ones[0:NH], lfT[0:NH, 0:TP], 0.0, ALU.mult, ALU.add))
            dve.tensor_scalar(f_c[0:NH], f_c[0:NH], -1.0, None, ALU.mult).then_inc(lf_ready, 1)
            dve.wait_ge(cneg_stored, 16)
            dve.wait_ge(evac[0], PV_FOX)
            dve.wait_ge(evac[1], PV_FOX)
            order(dve.memset(qa[HD:HD + 1, :, :], 1.0))

            with dve.Fori(0, HP) as i:
                def maxes(j):
                    hl, qt = tiles[j]
                    bank = 0 if j % 2 else 3
                    dve.wait_ge(s_done, N_IT * i + j + 1)
                    diag = sflat(bank, C, qt * C)
                    order(dve.tensor_tensor(diag, diag, cst[0:C, C_AM:C_AM + C], ALU.add))
                    dve.tensor_reduce(rowmax[0:C, j % 2:j % 2 + 1], sflat(bank, (qt + 1) * C), AX.X, ALU.max,
                                      negate=True).then_inc(max_ready, 1)

                def blocks(j):
                    hl, qt = tiles[j]
                    for g in range(groups[j]):
                        n = gr_before[j] + g
                        if n % 2 == 1:
                            dve.wait_ge(pt_done, N_GR * i + n + 1)
                            if j >= 2:
                                dve.wait_ge(pv_done, N_IT * i + j - 1)
                            m = min(4, qt + 1 - 4 * g)
                            dve.tensor_copy(PTm[0:C, j % 2, 4 * g:4 * g + m, :],
                                            PS[0:C, 6, 0:m * C].rearrange("p (a b) -> p a b", a=m))\
                               .then_inc(pt_read[1], 1)

                def output(j):
                    hl, qt = tiles[j]
                    dve.wait_ge(pv_done, N_IT * i + j + 1)
                    order(dve.reciprocal(rowinv[0:C, j % 2:j % 2 + 1], rowsum[0:C, j % 4:j % 4 + 1]))
                    dve.tensor_scalar(onat[0:C, qt, bass.ds(i * P + hl * HD, HD)], PS[0:C, 7, 0:HD],
                                      rowinv[0:C, j % 2:j % 2 + 1], None, ALU.mult).then_inc(o_read, 1)

                order.enter(i, 2 * N_IT + 2)
                dve.sem_inc(qk_free, 1)
                for hl in range(2):
                    half = slice(hl * HD, (hl + 1) * HD)
                    order(dve.tensor_scalar(qa[0:HD, hl, :],
                                            FX[half, bass.ds(i, 1), 0:TP].rearrange("p o n -> p (o n)"),
                                            SCALE, None, ALU.mult))
                    ins = dve.tensor_copy(ka[0:HD, hl, :],
                                          FX[half, bass.ds(i + HP, 1), 0:TP].rearrange("p o n -> p (o n)"))
                    ins.then_inc(qk_staged, 1)
                maxes(0)
                for j in range(N_IT):
                    if j + 1 < N_IT:
                        maxes(j + 1)
                    blocks(j)
                    if j:
                        output(j - 1)
                output(N_IT - 1)
                order.leave(HP)

            dve.wait_ge(ot_read, NC)
            order(dve.memset(qbd, 0.0))
            for e in range(2):
                half = slice(e * HD, (e + 1) * HD)
                order(dve.tensor_scalar(qbd[half, :, :, e], FX[half, 0:HP, TP:TS], SCALE, None, ALU.mult))
            order(dve.tensor_tensor(qkbd, qbd, FX[:, HP:2 * HP, TP:TS].unsqueeze(3)
                                    .to_broadcast([P, HP, DEC, 2]), ALU.mult))
            dve.tensor_tensor(lfd[0:NH], lfT[0:NH, TP:TS].unsqueeze(2).to_broadcast([NH, DEC, NH]),
                              ident[0:NH, 0:NH].unsqueeze(1).to_broadcast([NH, DEC, NH]), ALU.mult)\
               .then_inc(da_step, 1)
            dve.wait_ge(da_ready, 1)
            order(dve.tensor_copy(da_bias.rearrange("p b g h -> p (b g h)"), PS[:, 7, :]))
            dve.wait_ge(kp_used, DEC)
            flat_s = da_s.rearrange("p b g h -> p (b g h)")
            order(dve.tensor_tensor(flat_s, PS[:, 6, :], da_bias.rearrange("p b g h -> p (b g h)"), ALU.add))
            dve.tensor_reduce(da_mx.rearrange("p (b h) -> p b h", b=DEC), da_s.rearrange("p b g h -> p b h g"),
                              AX.X, ALU.max).then_inc(da_step, 1)
            dve.wait_ge(da_ready, 3)
            order(dve.tensor_reduce(da_c1[0:DEC * NH], PS[0:DEC * NH, 4, 0:P], AX.X, ALU.max))
            dve.tensor_scalar(da_dg[0:DEC * NH], ident[0:DEC * NH, 0:DEC * NH], da_c1[0:DEC * NH], None,
                              ALU.mult).then_inc(da_step, 1)
            dve.wait_ge(da_ready, 4)
            order(dve.tensor_copy(da_own, PS[:, 5, 0:DEC * NH]))
            order(dve.tensor_tensor(da_mx, PS[:, 4, 256:256 + DEC * NH], da_own, ALU.max))
            order(dve.tensor_tensor(da_po, da_own, da_mx, ALU.subtract))
            dve.tensor_tensor(da_s, da_s, da_mx.rearrange("p (b h) -> p b h", b=DEC).unsqueeze(2)
                              .to_broadcast([P, DEC, NPG, NH]), ALU.subtract).then_inc(da_step, 1)
            dve.wait_ge(da_exp, 2)
            dve.tensor_reduce(da_den.rearrange("p (b h) -> p b h", b=DEC), da_s.rearrange("p b g h -> p b h g"),
                              AX.X, ALU.add).then_inc(da_step, 1)
            dve.wait_ge(da_ready, 5)
            order(dve.tensor_tensor(da_mx, PS[:, 4, 384:384 + DEC * NH], da_po, ALU.add))
            order(dve.reciprocal(da_mx, da_mx))
            dve.wait_ge(vp_used, DEC)

            def by_pair(ap, e):
                return ap.rearrange("p (b a e) -> p a b e", b=DEC, a=HP)[e * HD:(e + 1) * HD, :, :, e]

            for e in range(2):
                half = slice(e * HD, (e + 1) * HD)
                pv = PS[half, 7, 0:2 * DEC * HP].rearrange("p (a b e) -> p a b e", a=HP, b=DEC)[:, :, :, e]
                order(dve.tensor_tensor(da_o[half], by_pair(da_po, e), FX[half, 2 * HP:3 * HP, TP:TS], ALU.mult))
                order(dve.tensor_tensor(da_o[half], da_o[half], pv, ALU.add))
                last = dve.tensor_tensor(FX[half, 0:HP, TP:TS], da_o[half], by_pair(da_mx, e), ALU.mult)
                if e == 0:
                    order(last)
            last.then_inc(da_step, 1)
            if debug == 'fox':
                return

            mix = Order(dve, mix_order)
            dve.wait_ge(da_step, 6)
            dve.wait_ge(lora_in, 16)
            mix(dve.memset(mtmp[:, TS:TT], 0.0))
            with dve.Fori(0, PV_RW) as i:
                mix.enter(i, 8)
                for s in range(2):
                    tile = bass.ds(2 * i + s, 1)

                    def cut(a, b):
                        return RW[:, tile, a:b].rearrange("p o n -> p (o n)")

                    dve.wait_ge(evac[s], i + (V_RW0 + 1))
                    mix(dve.tensor_copy(sh_out[:, tile, :], RW[:, tile, TP - 1:TS]))
                    mix(dve.tensor_tensor(mtmp[:, 1:TP], cut(0, TP - 1), cut(1, TP), ALU.subtract))
                    mix(dve.tensor_scalar(mtmp[:, 0:1], cut(0, 1), -1.0, None, ALU.mult))
                    mix(dve.tensor_tensor(mtmp[:, TP:TS], sh_in[:, tile, :].rearrange("p o n -> p (o n)"),
                                          cut(TP, TS), ALU.subtract))
                    dve.scalar_tensor_tensor(cut(0, TT), mtmp, par[:, bass.ds(2 * i + (V_MU + s), 1)],
                                             cut(0, TT), ALU.mult, ALU.add).then_inc(mixed, 1)
                    dve.wait_ge(mixed, 2 * i + (s + 1))
                mix.leave(PV_RW)
            for p in range(HP):
                r_, k_, v_ = RW[:, p, :], RW[:, HP + p, :], RW[:, 2 * HP + p, :]
                if p == 0:
                    dve.wait_ge(kv_stored, 16)
                    dve.wait_ge(pa, 10)
                order(dve.tensor_scalar(LW[:, p], LW[:, p], -E_HALF, None, ALU.mult))
                order(dve.tensor_scalar(KK[:, p], k_, par[:, V_KK + p:V_KK + p + 1], None, ALU.mult))
                dve.tensor_tensor(ptmp[0], KK[:, p], KK[:, p], ALU.mult).then_inc(pd, 1)
                order(dve.tensor_scalar(mtmp, BB[:, p], 1.0, par[:, V_KA + p:V_KA + p + 1],
                                        ALU.subtract, ALU.mult))
                order(dve.scalar_tensor_tensor(k_, mtmp, 1.0, k_, ALU.add, ALU.mult))
                dve.scalar_tensor_tensor(ptmp[1], r_, par[:, V_RK + p:V_RK + p + 1], k_, ALU.mult, ALU.mult)\
                   .then_inc(pd, 1)
                dve.wait_ge(pa, 11 + p)
                order(dve.tensor_scalar(ptmp[0], ptmp[0], 1e-12, None, ALU.max))
                order(dve.reciprocal(ptmp[0], ptmp[0]))
                order(dve.tensor_tensor(KK[:, p], KK[:, p], ptmp[0], ALU.mult))
                order(dve.tensor_tensor(BB[:, p], KK[:, p], BB[:, p], ALU.mult))
                dve.wait_ge(pp, 2 * HP + 2 * p + 2)
                dve.tensor_tensor(g3(BON[:, p]), grp(1), g3(v_), ALU.mult).then_inc(pd, 1)
                dve.wait_ge(pd, 3 * p + 3)

            order(dve.memset(St, 0.0))
            dve.wait_ge(h_stored, 16)
            dve.wait_ge(sh_stored, 16)
            dve.sem_inc(ch_dve.sem, 1)
            with dve.Fori(0, NC) as c:
                def wait(steps, name):
                    dve.wait_ge(steps.sem, steps.after(c, name))

                def done(ins, name):
                    ch_dve.done(ins, name)
                    dve.wait_ge(ch_dve.sem, ch_dve.after(c, name))

                here = bass.ds(c * C, C)
                dve.wait_ge(ch_pe.sem, ch_pe.before(c))
                for p in range(HP):
                    done(dve.tensor_tensor_scan(Lc[:, p], ones[:, 0:C], LW[:, p, here], 0.0, ALU.mult, ALU.add),
                         f"scan_{p}")
                done(dve.tensor_tensor(Lm, Lc, LW[:, :, here], ALU.subtract), "lm")
                wait(ch_act, "e1")
                done(dve.tensor_tensor(AR[:, :, 1], RW[:, 0:HP, here], E1, ALU.mult), "r")
                wait(ch_act, "e3")
                done(dve.tensor_tensor(Kc, RW[:, HP:2 * HP, here], E3, ALU.mult), "k")
                done(dve.tensor_tensor(Bc, BB[:, :, here], E3, ALU.mult), "b")
                wait(ch_act, "e2")
                done(dve.tensor_tensor(AR[:, :, 0], KK[:, :, here], E2, ALU.mult), "a")
                wait(ch_pe, "nat_b")
                done(dve.tensor_copy(Bn[0:C], PS[0:C, 1, :]), "nat_b")
                wait(ch_pe, "nat_v")
                done(dve.tensor_copy(Vn[0:C], PS[0:C, 3, :]), "nat_v")
                cm = cst[0:C, C_CM:C_CM + 2 * C].unsqueeze(1).unsqueeze(1).to_broadcast([C, 2, 2, 2 * C])
                for i in range(2):
                    for m, dst, bank in (("k", MK, 4), ("b", MB, 6)):
                        wait(ch_pe, f"prod_{m}{i}")
                        done(dve.tensor_tensor(
                            dst[0:C].rearrange("p (e a) x t -> p e a (x t)", e=2)[:, :, 2 * i:2 * i + 2],
                            PS[0:C, bank:bank + 2, 0:4 * C].rearrange("p e (a n) -> p e a n", a=2),
                            cm, ALU.mult), f"mask_{m}{i}")
                wait(ch_pool, "bm_0")
                done(dve.tensor_tensor(XTr[0:C], ident[0:C, 0:C].unsqueeze(1).to_broadcast([C, NH, C]),
                                       Bm[0][0:C], ALU.subtract), "xt_init")

                def quad(ap, q):
                    return ap[0:C, 4 * q:4 * q + 4].rearrange("p a b -> p (a b)")

                for lv in LEVELS:
                    for q in range(2):
                        wait(ch_pe, f"t2_{lv}_{q}")
                        if lv < N_LV - 1:
                            done(dve.tensor_tensor(quad(Xm, q), quad(Xm, q), PS[0:C, 2 + q, 0:4 * C],
                                                   ALU.subtract), f"x_{lv}_{q}_x")
                        done(dve.tensor_tensor(quad(XTr, q), quad(XTr, q), PS[0:C, 4 + q, 0:4 * C],
                                               ALU.subtract), f"x_{lv}_{q}_xt")

                def heads(ap):
                    return ap.rearrange("p (h v) -> p h v", h=NH)

                def spread(ap):
                    return ap.unsqueeze(2).to_broadcast([C, NH, HD])

                def by_head(ap):
                    return ap.rearrange("p (e a v) -> p e a v", e=2, a=HP)

                def spread4(k):
                    return gst[0:C, k].rearrange("p (e a) -> p e a", e=2).unsqueeze(3).to_broadcast([C, 2, HP, HD])

                y = PS[0:C, 2:4, 0:HP * HD].rearrange("p e (a v) -> p e a v", a=HP)
                ych = Yc[0:C].rearrange("p (a e v) -> p e a v", a=HP, e=2)
                wait(ch_pe, "y")
                done(dve.tensor_reduce(gst[0:C, 0].rearrange("p (e a) -> p e a", e=2), y, AX.X, ALU.add), "sum")
                done(dve.tensor_scalar(gst[0:C, 0], gst[0:C, 0], 1.0 / HD, None, ALU.mult), "mean")
                wait(ch_pe, "s")
                done(dve.tensor_tensor(St, PS[:, 1, 0:HP * HD].rearrange("p (a b) -> p a b", a=HP),
                                       E1[:, :, C - 1:C].to_broadcast([P, HP, HD]), ALU.mult), "state")
                done(dve.tensor_tensor(ych, y, spread4(0), ALU.subtract), "center")
                done(dve.tensor_tensor(by_head(Zm[0:C]), ych, ych, ALU.mult), "sq")
                done(dve.tensor_reduce(gst[0:C, 1].rearrange("p (e a) -> p e a", e=2), by_head(Zm[0:C]), AX.X,
                                       ALU.add), "var")
                wait(ch_act, "rstd")
                done(dve.tensor_tensor(ych, ych, spread4(3), ALU.mult), "norm")

            def on_keys(ap):
                return ap.unsqueeze(3).to_broadcast([P, DEC // 2, NH, HD])

            dve.wait_ge(ds_load, 16 * 11)
            order(dve.tensor_tensor(dT, dS, dKK, ALU.mult))
            order(dve.tensor_reduce(dU, dT, AX.X, ALU.add))
            dve.sem_inc(ds_dve, 1)
            order(dve.tensor_tensor(dS, dS, dW, ALU.mult))
            order(dve.tensor_tensor(dT, dB, on_keys(dU), ALU.mult))
            order(dve.tensor_tensor(dS, dS, dT, ALU.subtract))
            order(dve.tensor_tensor(dT, dK, on_keys(dV), ALU.mult))
            dve.tensor_tensor(dS, dS, dT, ALU.add).then_inc(ds_dve, 1)
            dve.wait_ge(ds_dve, 2)
            dve.wait_ge(ds_load, 16 * 13)
            order(dve.tensor_tensor(dT, dS, dR, ALU.mult))
            dve.tensor_reduce(dU, dT, AX.X, ALU.add).then_inc(ds_dve, 1)
            dve.wait_ge(ds_yb, 16)

            def heads(ap):
                return ap.rearrange("p (h v) -> p h v", h=NH)

            def spread(ap):
                return ap.unsqueeze(2).to_broadcast([DEC, NH, HD])

            order(dve.tensor_reduce(dst4[0:DEC, 0], heads(dYn[0:DEC]), AX.X, ALU.add))
            order(dve.tensor_scalar(dst4[0:DEC, 0], dst4[0:DEC, 0], 1.0 / HD, None, ALU.mult))
            order(dve.tensor_tensor(heads(dYn[0:DEC]), heads(dYn[0:DEC]), spread(dst4[0:DEC, 0]), ALU.subtract))
            order(dve.tensor_tensor(dSQ[0:DEC], dYn[0:DEC], dYn[0:DEC], ALU.mult))
            order(dve.tensor_reduce(dst4[0:DEC, 1], heads(dSQ[0:DEC]), AX.X, ALU.add))
            dve.sem_inc(ds_var, 1)
            dve.wait_ge(ds_act, 3)
            dve.tensor_tensor(heads(dYn[0:DEC]), heads(dYn[0:DEC]), spread(dst4[0:DEC, 3]), ALU.mult)\
               .then_inc(ds_dve, 1)
            dve.wait_ge(ds_act, 3 + HP)
            for p in range(HP):
                order(dve.tensor_tensor(RW[:, p, :], RW[:, p, :], BON[:, p, :], ALU.add))
                dve.wait_ge(o_pe, p + 1)
                dve.tensor_tensor(g3(RW[:, p, :]), g3(RW[:, p, :]), grp(p % 2), ALU.mult).then_inc(o_done, 1)
                dve.wait_ge(o_done, p + 1)
            if debug == 'rw':
                return

            dve.sem_inc(sg_used, 2)
            with dve.Fori(0, KT) as n:
                for s in range(2):
                    dst = MG[:, bass.ds(n, 1), :].rearrange("p o n -> p (o n)") if s == 0 else gtmp
                    dve.wait_ge(evac[s], 2 * n + (V_GATE0 + 1))
                    dve.wait_ge(unit_done, 4 * n + (2 * V_GATE0 + 3 + s))
                    dve.tensor_tensor(g3(dst), g3(SG[s]), grp(s), ALU.mult).then_inc(evac[s], 1)
                    dve.wait_ge(evac[s], 2 * n + (V_GATE0 + 2))
                    dve.sem_inc(sg_used, 1)
                dst = MG[:, bass.ds(n, 1), :].rearrange("p o n -> p (o n)")
                dve.tensor_tensor(dst, dst, gtmp, ALU.add).then_inc(mg_ready, 1)
                dve.wait_ge(mg_ready, n + 1)
            dve.wait_ge(x_back, 16)
            with dve.Fori(0, PV_OUT) as j:
                for s in range(2):
                    dst = g3(XT[:, bass.ds(2 * j + s, 1), :].rearrange("p o n -> p (o n)"))
                    dve.wait_ge(unit_done, 2 * j + (2 * V_OUT0 + s + 1))
                    dve.tensor_tensor(dst, dst, grp(s), ALU.add).then_inc(evac[s], 1)
            dve.wait_ge(evac[0], V_FF0)
            dve.wait_ge(evac[1], V_FF0)
            dve.sem_inc(xr_ready, KT)
            dve_norm(dve, 1, V_NF, order)
            dve.sem_inc(ff_ready, 2)
            with dve.Fori(0, FF_CH) as c:
                with dve.Fori(0, KT // 2) as j:
                    for s in range(2):
                        dve.wait_ge(evac[s], KT * c + j + (V_FF0 + 1))
                        dve.tensor_tensor(FH[:, bass.ds(2 * j + s, 1), :].rearrange("p o n -> p (o n)"),
                                          RL[s], RL[s], ALU.mult).then_inc(ff_ready, 1)
                with dve.Fori(0, PV_OUT) as j:
                    for s in range(2):
                        dst = g3(XT[:, bass.ds(2 * j + s, 1), :].rearrange("p o n -> p (o n)"))
                        dve.wait_ge(unit_done, 2 * KT * c + 2 * j + (2 * V_FF0 + KT + s + 1))
                        dve.tensor_tensor(dst, dst, grp(s), ALU.add).then_inc(evac[s], 1)
            dve.wait_ge(evac[0], PAIRS)
            dve.wait_ge(evac[1], PAIRS)
            dve_norm(dve, 2, V_NL, order)
            dve.sem_inc(lastn, KT)

        @block.gpsimd
        def _(pool):
            if debug == 'fox':
                return
            pool.sem_inc(ch_pool.sem, 1)
            with pool.Fori(0, NC) as c:
                pool.wait_ge(ch_dve.sem, ch_dve.after(c, "mask_b1"))
                for lv in range(N_LV):
                    if lv == 2:
                        pool.wait_ge(ch_dve.sem, ch_dve.after(c, "xt_init"))
                    if lv > 2:
                        pool.wait_ge(ch_pe.sem, ch_pe.after(c, f"t1_{lv - 2}_1"))
                    mask = cst[0:C, C_LV + lv * C:C_LV + (lv + 1) * C].unsqueeze(1).to_broadcast([C, NH, C])
                    ch_pool.done(pool.tensor_tensor(Bm[lv % 2][0:C], MB[0:C, :, 0], mask, ALU.mult), f"bm_{lv}")


def _tiles(w):
    k, n = w.shape
    return w.reshape(k // P, P, n // P, P).transpose(2, 1, 0, 3).reshape(n // P, P, k)


def _constants():
    import numpy as np
    z = np.zeros((P, C_ALL), np.float32)
    i, j, t = np.arange(P)[:, None], np.arange(P)[None], np.arange(C)[None]
    z[:, C_ID:C_ID + P] = i == j
    z[:, C_ONE:C_ONE + P] = 1
    z[:, C_BLK:C_BLK + P] = i // HD == j // HD
    z[:, C_SUF:C_SUF + P] = i > j
    z[:, C_AM:C_AM + C] = np.where(t <= i, 0, -1e30)
    z[:, C_CM:C_CM + C] = i < t
    z[:, C_CM + C:C_CM + 2 * C] = i <= t
    for level in range(N_LV):
        n = 1 << level
        z[:, C_LV + level * C:C_LV + (level + 1) * C] = (i // n % 2 == 0) & (t // n == i // n + 1)
    return z


def lay_out(inp):
    import numpy as np
    f = np.float32
    x = np.concatenate([inp["meta_tokens"], inp["x_prompt"][0], inp["x_sample"][:, 0],
                        np.zeros((TT - TS, D), f)])
    xt = x.T.reshape(KT, P, TT).transpose(1, 0, 2)
    w = inp["w_in"][0]
    n_rw, n_fox = RW_T * P, 3 * NH * HD
    w_rw, w_fox = w[:, :n_rw], w[:, n_rw:n_rw + n_fox]
    w_f, w_g = w[:, n_rw + n_fox:n_rw + n_fox + NH], w[:, n_rw + n_fox + NH:]
    gr, gf = _tiles(w_g[:, :D]), _tiles(w_g[:, D:])
    pad = np.zeros((KT, P, D - NH * HD), f)
    br = np.concatenate([_tiles(inp["w_br_rwkv"][0]), pad], 2)
    bf = np.concatenate([_tiles(inp["w_br_fox"][0]), pad], 2)
    merge = np.stack([gr, gf, br, bf], 1).reshape(4 * KT, P, D)
    up = _tiles(inp["w_ffn_up"][0])
    ff = []
    for c in range(FF_CH):
        ff += [up[c * KT:(c + 1) * KT], _tiles(inp["w_ffn_down"][0][c * D:(c + 1) * D])]
    wu = np.concatenate([_tiles(w_fox), _tiles(w_rw), merge, _tiles(inp["w_out"][0])] + ff)

    def cols(v):
        return v.reshape(-1, P).T

    bfg = np.zeros((P, 1), f)
    bfg[:NH, 0] = inp["b_forget"][0]
    par = np.concatenate([cols(inp["norm_mix"][0]), cols(inp["norm_ffn"][0]), cols(inp["norm_final"]),
                          cols(inp["mu_shift"][0]), cols(inp["w0"][0]), cols(inp["a0"][0]), cols(inp["k_k"][0]),
                          cols(inp["k_a"][0]), cols(inp["r_k"][0]), cols(inp["ln_x_w"][0]),
                          cols(inp["ln_x_b"][0]), np.full((P, 1), 1e-6, f), np.full((P, 1), 64e-5, f), bfg,
                          np.zeros((P, 1), f)], 1)
    kp = inp["cache_k"][0].reshape(POOL, PAGE, HP, P).transpose(0, 3, 2, 1)
    vp = np.concatenate([inp["cache_v"][0].reshape(POOL, PAGE, NH * HD), inp["cache_logf"][0]], 2)
    st = inp["state_wkv"][0].reshape(2, DEC // 2, NH, HD, HD).transpose(0, 3, 1, 2, 4).reshape(P, -1)
    sh = inp["state_shift"][0].reshape(DEC, RW_T, P).transpose(2, 1, 0)
    return {"xt": xt, "wu": wu, "cst": _constants(), "par": par,
            "wf": w_f.reshape(KT, P, NH).transpose(1, 0, 2),
            "wl": np.concatenate([inp["w_decay_up"][0], inp["w_a_up"][0]]), "wg": inp["w_g_up"][0],
            "page_table": inp["page_table"].reshape(1, -1), "kp": kp, "vp": vp, "st": st, "sh": sh}


_OUTS = {"o_y": (P, KT, TT), "o_kv": (P, 2 * HP, TT), "o_lf": (NH, TT), "o_sh": (P, RW_T, DEC + 1),
         "o_sp": (P, HP, HD), "o_ss": (P, DEC // 2 * NH * HD)}


def give_back(o):
    y = o["o_y"].transpose(2, 1, 0).reshape(TT, D)
    kv = o["o_kv"].transpose(2, 1, 0).reshape(TT, 2, NH, HD)
    lf = o["o_lf"].T
    sh = o["o_sh"].transpose(2, 1, 0).reshape(DEC + 1, RW_T * P)
    sp = o["o_sp"].reshape(2, HD, HP, HD).transpose(2, 0, 3, 1).reshape(NH, HD, HD)
    ss = o["o_ss"].reshape(2, HD, DEC // 2, NH, HD).transpose(0, 2, 3, 1, 4).reshape(DEC, NH, HD, HD)
    return (y[T_META:TP][None], y[TP:TS][:, None], sh[0:1][None], sp[None, None],
            kv[:TP, 0][None, None], kv[:TP, 1][None, None], lf[:TP][None, None], sh[1:][None], ss[None],
            kv[TP:TS, 0][None, :, None], kv[TP:TS, 1][None, :, None], lf[TP:TS][None, :, None])


def kernel(**inputs):
    import numpy as np
    import concourse.bacc as bacc
    from concourse.bass_utils import run_bass_kernel_spmd

    nc = bacc.Bacc("TRN2", target_bir_lowering=False, num_devices=1, dynamic_dma_scratch_size=1024)
    arrays, aps = {}, {}
    for name, a in lay_out({k: np.asarray(v) for k, v in inputs.items()}).items():
        a = np.ascontiguousarray(a)
        arrays["in_" + name] = a
        aps[name] = nc.dram_tensor("in_" + name, a.shape, mybir.dt.from_np(a.dtype), kind="ExternalInput").ap()
    for name, shape in _OUTS.items():
        aps[name] = nc.dram_tensor("out_" + name, shape, F32, kind="ExternalOutput").ap()
    build(nc, aps)
    r = run_bass_kernel_spmd(nc, [arrays], core_ids=[0])
    got = {name: np.asarray(r.results[0]["out_" + name]) for name in _OUTS}
    return tuple(np.ascontiguousarray(a) for a in give_back(got))
```

```python
from contextlib import ExitStack

import concourse.bass as bass
from concourse import mybir
from concourse.alu_op_type import AluOpType as ALU

F32 = mybir.dt.float32
I32 = mybir.dt.int32
ACT = mybir.ActivationFunctionType
AX = mybir.AxisListType

P = 128
D = 1024
KT = D // P
T_META, SEQ, DEC = 16, 1024, 8
TP = T_META + SEQ
TS = TP + DEC
TT = 1050
NG, G = 3, TT // 3
C = 104
NC = TP // C
HD = 64
NH = 8
HP = NH // 2
PAGE, NPG, POOL = 128, 8, 80
VW = NH * HD + NH
FF_CH = 4
RW_T = 14
SCALE = HD ** -0.5
E_HALF = 0.6065306597126334

C_ID, C_ONE, C_BLK, C_SUF = 0, 128, 256, 384
C_AM = 512
C_CM = C_AM + C
C_LV = C_CM + 2 * C
N_LV = 7
C_ALL = C_LV + N_LV * C
V_NM, V_NF, V_NL, V_MU, V_W0, V_A0, V_KK, V_KA, V_RK, V_LW, V_LB, V_EPS, V_GEPS, V_BF = (
    0, 8, 16, 24, 38, 42, 46, 50, 54, 58, 62, 66, 67, 68)
V_ALL = 70

PV_RW, PV_FOX, PV_GATE, PV_BR, PV_OUT, PV_FF = 7, 6, 8, 8, 4, 32
V_FOX0 = PV_RW
V_GATE0 = V_FOX0 + PV_FOX
V_BR0 = V_GATE0 + PV_GATE
V_OUT0 = V_BR0 + PV_BR
V_FF0 = V_OUT0 + PV_OUT
PAIRS = V_FF0 + PV_FF
PV_FILL = PV_FOX + PV_GATE
C_FOX = PV_FOX

SB_COLS = 56900


class Order:

    def __init__(self, eng, sem):
        self.eng, self.sem, self.base, self.n = eng, sem, 0, 0

    def __call__(self, ins):
        self.n += 1
        ins.then_inc(self.sem, 1)
        self.eng.wait_ge(self.sem, self.base + self.n)

    def enter(self, i, per):
        self.outer, self.per = self.base + self.n, per
        self.base, self.n = self.outer + i * per, 0

    def leave(self, count):
        assert self.n == self.per, ("steps in the loop's body", self.n, self.per)
        self.base, self.n = self.outer + count * self.per, 0


class Steps:

    def __init__(self, sem, names):
        self.sem, self.names, self.next = sem, names, 0

    def after(self, c, name):
        return c * len(self.names) + (self.names.index(name) + 2)

    def before(self, c):
        return c * len(self.names) + 1

    def done(self, ins, name):
        assert self.names[self.next] == name, (self.names[self.next], name)
        self.next = (self.next + 1) % len(self.names)
        ins.then_inc(self.sem, 1)


def build(nc, A):
    with ExitStack() as ctx:
        def sem(name):
            return ctx.enter_context(nc.semaphore(name))

        SB = ctx.enter_context(nc.sbuf_tensor("sb", [P, SB_COLS], F32))
        PT_SB = ctx.enter_context(nc.sbuf_tensor("page_ids", [1, DEC * NPG], I32))
        PS = ctx.enter_context(nc.psum_tensor("ps", [P, 8, 512], F32))
        chunk_dram = nc.dram_tensor("chunk_dram", [P, NC, 6, HP, C], F32, kind="Internal").ap()
        bg_dram = nc.dram_tensor("bg_dram", [P, 2 * HP, TT], F32, kind="Internal").ap()
        gate_dram = nc.dram_tensor("gate_dram", [2 * KT, P, TT], F32, kind="Internal").ap()
        cneg_dram = nc.dram_tensor("cneg_dram", [NH, TP], F32, kind="Internal").ap()
        samp_dram = nc.dram_tensor("samp_dram", [6, DEC, NH * HD], F32, kind="Internal").ap()
        ysamp_dram = nc.dram_tensor("ysamp_dram", [DEC, NH, HD], F32, kind="Internal").ap()

        def view(at, *dims):
            n = 1
            for d in dims:
                n *= d
            assert at + n <= SB_COLS, (at, n)
            v = SB[:, at:at + n]
            if len(dims) == 2:
                v = v.rearrange("p (a b) -> p a b", a=dims[0])
            if len(dims) == 3:
                v = v.rearrange("p (a b c) -> p a b c", a=dims[0], b=dims[1])
            if len(dims) == 4:
                v = v.rearrange("p (a b c d) -> p a b c d", a=dims[0], b=dims[1], c=dims[2])
            return v

        class Region:

            def __init__(self, at, n):
                self.at, self.end = at, at + n

            def take(self, *dims):
                n = 1
                for d in dims:
                    n *= d
                v = view(self.at, *dims)
                self.at += n
                assert self.at <= self.end, (self.at, self.end)
                return v

        whole = Region(0, SB_COLS)
        cst = whole.take(C_ALL)
        par = whole.take(V_ALL)
        W = whole.take(2, D)
        wl = whole.take(512)
        wg = whole.take(512)
        wf = whole.take(KT, NH)
        lfT = whole.take(TT)
        HT = whole.take(KT, TT)
        FX = whole.take(12, TT)
        ar = whole.at
        ar_n = SB_COLS - ar
        XT = view(ar, KT, TT)
        RW = view(ar, RW_T, TT)
        YT = view(SB_COLS - HP * TT, HP, TT)
        d_col = view(SB_COLS - HP * TT - 6 * HP * DEC, 6, HP, DEC)
        ar_end = SB_COLS - HP * TT - 6 * HP * DEC

        ident = cst[:, C_ID:C_ID + P]
        ones = cst[:, C_ONE:C_ONE + P]
        blk = cst[:, C_BLK:C_BLK + P]
        suf = cst[:, C_SUF:C_SUF + P]

        def grp(slot):
            return PS[:, 3 * slot:3 * slot + 3, 0:G]

        def g3(ap):
            return ap.rearrange("p (g n) -> p g n", g=NG)

        consts_in, x_in, state_in = sem("consts_in"), sem("x_in"), sem("state_in")
        w_in = [sem("w_in0"), sem("w_in1")]
        unit_done = sem("unit_done")
        evac = [sem("evac0"), sem("evac1")]
        act_order, dve_order = sem("act_order"), sem("dve_order")
        out_stored, kv_stored, sh_stored = sem("out_stored"), sem("kv_stored"), sem("sh_stored")
        sp_stored = sem("sp_stored")
        sq_ready, sq_added = sem("sq_ready"), sem("sq_added")
        ssum_ready, rms_ready, h_ready = sem("ssum_ready"), sem("rms_ready"), sem("h_ready")
        sub_done, sub_read = sem("sub_done"), sem("sub_read")

        r_norm = Region(ar + KT * TT, 4 * TT)
        sq = r_norm.take(2, TT)
        sqsum = r_norm.take(TT)
        rstd = r_norm.take(TT)

        def pe_unit(pe, v, s, x, nk=KT, late=True):
            pe.wait_ge(w_in[s], 16 * (v + 1))
            if not isinstance(v, int) or v > 0:
                pe.wait_ge(evac[s], v - PV_FILL if late else v)
            for k in range(nk):
                for g in range(NG):
                    last = pe.matmul(PS[:, 3 * s + g, 0:G], W[:, s, k * P:(k + 1) * P],
                                     x[:, k, g * G:(g + 1) * G], start=(k == 0), stop=(k == nk - 1))
            last.then_inc(unit_done, 1)

        def pe_norm(pe, n):
            pe.wait_ge(sq_added, KT * (n + 1))
            for g in range(NG):
                last = pe.matmul(PS[:, g, 0:G], ones, sqsum[:, g * G:(g + 1) * G], start=True, stop=True)
            last.then_inc(ssum_ready, 1)

        def act_norm(act, n):
            for k in range(KT):
                if KT * n + k >= 2:
                    act.wait_ge(sq_added, KT * n + k - 1)
                act.activation(sq[:, k % 2], XT[:, k, :], ACT.Square).then_inc(sq_ready, 1)
            act.wait_ge(ssum_ready, n + 1)
            act.activation(g3(rstd), grp(0), ACT.Sqrt, scale=1.0 / D,
                           bias=par[:, V_EPS:V_EPS + 1]).then_inc(rms_ready, 1)

        def dve_norm(dve, n, gain, order):
            for k in range(KT):
                dve.wait_ge(sq_ready, KT * n + k + 1)
                if k:
                    dve.wait_ge(sq_added, KT * n + k)
                    dve.tensor_tensor(sqsum, sqsum, sq[:, k % 2], ALU.add).then_inc(sq_added, 1)
                else:
                    dve.tensor_copy(sqsum, sq[:, 0]).then_inc(sq_added, 1)
            dve.wait_ge(rms_ready, n + 1)
            order(dve.reciprocal(rstd, rstd))
            for k in range(KT):
                dve.scalar_tensor_tensor(HT[:, k, :], XT[:, k, :], par[:, gain + k:gain + k + 1], rstd,
                                         ALU.mult, ALU.mult).then_inc(h_ready, 1)
            dve.wait_ge(h_ready, KT * (n + 1))

        class Filler:

            def __init__(self, pe, v):
                self.pe, self.v = pe, v
                self.left = [(s, g, k) for s in range(2) for g in range(NG) for k in range(KT)]

            def run(self, n=None):
                for s, g, k in self.left[:n]:
                    m = NG * s + g
                    if k == 0:
                        if g == 0:
                            self.pe.wait_ge(w_in[s], 16 * self.v + 16)
                        self.pe.wait_ge(sub_read, 2 * NG * self.v + (m + 1 - 2 * NG * V_FOX0))
                    last = self.pe.matmul(PS[:, 6 + m % 2, 0:G], W[:, s, k * P:(k + 1) * P],
                                          HT[:, k, g * G:(g + 1) * G], start=(k == 0), stop=(k == KT - 1))
                    if k == KT - 1:
                        last.then_inc(unit_done if g == NG - 1 else sub_done, 1)
                self.left = self.left[n:] if n is not None else []

        def act_fill(act, v, m, dst):
            s, g = divmod(m, NG)
            if g == NG - 1:
                act.wait_ge(unit_done, 2 * v + (s + 1))
            else:
                act.wait_ge(sub_done, 4 * v + (2 * s + g + 1 - 4 * V_FOX0))
            act.copy(dst, PS[:, 6 + m % 2, 0:G]).then_inc(sub_read, 1)

        f_ready, f_read, lf_ready = sem("f_ready"), sem("f_read"), sem("lf_ready")
        cneg_stored, cneg_in = sem("cneg_stored"), [sem("cneg_in0"), sem("cneg_in1")]
        vt_ready, vt_read = sem("vt_ready"), sem("vt_read")
        qk_free, qk_staged = sem("qk_free"), sem("qk_staged")
        s_done, max_ready, p_ready = sem("s_done"), sem("max_ready"), sem("p_ready")
        pt_done, pt_read = sem("pt_done"), [sem("pt_read0"), sem("pt_read1")]
        pv_done, o_read = sem("pv_done"), sem("o_read")
        ot_ready, ot_read = sem("ot_ready"), sem("ot_read")

        r_att = Region(ar, ar_end - ar)
        qa = r_att.take(2, TP)
        ka = r_att.take(2, TP)
        Pm = r_att.take(2, TP)
        PTm = r_att.take(2, NC, C)
        onat = r_att.take(NC, 512)
        rowmax = r_att.take(2)
        rowsum = r_att.take(4)
        rowinv = r_att.take(2)
        vnat = view(ar_end - NC * 512, NC, 512)
        r_f = Region(ar_end - NC * 512 - 2 * TT, 2 * TT)
        f_neg, f_t = r_f.take(TT), r_f.take(TT)
        f_c, f_ones = f_neg[:, 0:TP], f_t[:, 0:TP]
        tiles = [(hl, qt) for hl in range(2) for qt in range(NC)]
        N_IT = len(tiles)
        groups = [-(-(qt + 1) // 4) for _, qt in tiles]
        N_GR = sum(groups)
        assert N_GR % 2 == 0
        gr_before = [sum(groups[:j]) for j in range(N_IT)]

        ids_in = sem("ids_in")
        kp_in = [sem("kp_in0"), sem("kp_in1")]
        vp_in = [sem("vp_in0"), sem("vp_in1")]
        lfp_in = sem("lfp_in")
        da_ready = sem("da_ready")
        da_step = sem("da_step")
        da_exp = sem("da_exp")
        kp_used, vp_used = sem("kp_used"), sem("vp_used")
        r_da = Region(ar, ar_end - ar)
        Vp = r_da.take(2, NPG, VW)
        Kp = r_da.take(2, NPG, HP, PAGE)
        lfp = r_da.take(DEC, NPG, NH)
        qbd = r_da.take(HP, DEC, 2)
        qkbd = r_da.take(HP, DEC, 2)
        lfd = r_da.take(DEC, NH)
        da_bias = r_da.take(DEC, NPG, NH)
        da_s = r_da.take(DEC, NPG, NH)
        da_own = r_da.take(DEC * NH)
        da_mx = r_da.take(DEC * NH)
        da_c1 = r_da.take(1)
        da_dg = r_da.take(DEC * NH)
        da_po = r_da.take(DEC * NH)
        da_den = r_da.take(DEC * NH)
        da_o = r_da.take(HP, DEC)

        mixed, mix_order = sem("mixed"), sem("mix_order")
        lora_in = sem("lora_in")
        pp, pa, pd = sem("prep_pe"), sem("prep_act"), sem("prep_dve")
        LW, KK, BB = FX[:, 0:HP, :], FX[:, HP:2 * HP, :], FX[:, 2 * HP:3 * HP, :]
        r_rw = Region(ar + RW_T * TT, ar_end - ar - RW_T * TT)
        BG = r_rw.take(2 * HP, TT)
        BON, GT = BG[:, 0:HP], BG[:, HP:2 * HP]
        sh_in = r_rw.take(RW_T, DEC)
        sh_out = r_rw.take(RW_T, DEC + 1)
        mtmp = r_rw.take(TT)
        ptmp = [YT[:, 0, :], YT[:, 1, :]]

        d_col_ready = sem("d_col_ready")
        prep_stored, bg_stored, bg_back = sem("prep_stored"), sem("bg_stored"), sem("bg_back")
        st_in, g_stored, g_back = sem("st_in"), [sem("g_stored0"), sem("g_stored1")], [sem("g_back0"), sem("g_back1")]

        r_ch = Region(ar, ar_end - ar)
        CH = r_ch.take(6, HP, C)
        SGs = r_ch.take(2, TT)
        Lc, Lm = r_ch.take(HP, C), r_ch.take(HP, C)
        E1, E2, E3 = r_ch.take(HP, C), r_ch.take(HP, C), r_ch.take(HP, C)
        AR = r_ch.take(HP, 2, C)
        Kc, Bc, Vc = r_ch.take(HP, C), r_ch.take(HP, C), r_ch.take(HP, C)
        Kn, Bn, An, Vn = r_ch.take(512), r_ch.take(512), r_ch.take(512), r_ch.take(512)
        Xm, XTr = r_ch.take(NH, C), r_ch.take(NH, C)
        r_c2 = r_ch
        MK = r_c2.take(NH, 2, C)
        MB = r_c2.take(NH, 2, C)
        T1 = r_c2.take(NH, C)
        Bm = r_c2.take(NH, C), r_c2.take(NH, C)
        Zm = r_c2.take(512)
        WT = r_c2.take(HP, C)
        NU = r_c2.take(512)
        St = r_ch.take(HP, HD)
        Yc = r_c2.take(512)
        gst = r_c2.take(4, NH)

        LEVELS = range(1, N_LV)
        ch_pe = Steps(sem("ch_pe"), ["nat_k", "nat_b", "nat_a", "nat_v"]
                      + [f"prod_{m}{i}" for i in range(2) for m in "kb"] + ["z", "x_0", "x_1"]
                      + [f"{t}_{lv}_{q}" for lv in LEVELS for t in ("t1", "t2") for q in range(2)]
                      + ["wt", "u", "y", "s", "yt"])
        ch_act = Steps(sem("ch_act"), ["v", "e1", "e3", "e2", "nat_k", "nat_a", "z", "x_0", "x_1"]
                       + [f"t1_{lv}_{q}" for lv in LEVELS for q in range(2)]
                       + ["wt", "nu", "ln", "rstd"] + [f"y_{p}" for p in range(HP)])
        ch_dve = Steps(sem("ch_dve"), [f"scan_{p}" for p in range(HP)] + ["lm", "r", "k", "b", "a", "nat_b", "nat_v"]
                       + [f"mask_{m}{i}" for i in range(2) for m in "kb"] + ["xt_init"]
                       + [f"x_{lv}_{q}_{t}" for lv in LEVELS for q in range(2)
                          for t in (("x", "xt") if lv < N_LV - 1 else ("xt",))]
                       + ["sum", "mean", "state", "center", "sq", "var", "norm"])
        ch_pool = Steps(sem("ch_pool"), [f"bm_{lv}" for lv in range(N_LV)])

        ds_pe, ds_act, ds_dve = sem("ds_pe"), sem("ds_act"), sem("ds_dve")
        ds_store, ds_load = sem("ds_store"), sem("ds_load")
        ds_y, ds_yb, ds_var = sem("ds_y"), sem("ds_yb"), sem("ds_var")
        o_pe, o_done = sem("o_pe"), sem("o_done")
        r_ds = Region(ar, ar_end - ar)
        SGs2 = r_ds.take(6 * HP * C + 2 * TT)
        dS = r_ds.take(DEC // 2, NH, HD)
        dW, dT = r_ds.take(DEC // 2, NH, HD), r_ds.take(DEC // 2, NH, HD)
        dKK, dB, dK = (r_ds.take(DEC // 2, NH, HD) for _ in range(3))
        dR = dKK
        dV, dU = r_ds.take(DEC // 2, NH), r_ds.take(DEC // 2, NH)
        d_nat = view(r_ds.at, 6, P)
        dYn, dSQ = r_ds.take(512), r_ds.take(512)
        dst4 = r_ds.take(4, NH)
        assert r_ds.at <= ar_end - NC * 512 - 2 * TT
        BGb = view(ar + 6 * HP * C + 2 * TT, 2 * HP, TT)

        sg_ready, sg_used, mg_ready = sem("sg_ready"), sem("sg_used"), sem("mg_ready")
        ff_ready, x_back, xr_ready = sem("ff_ready"), sem("x_back"), sem("xr_ready")
        MG = FX[:, HP:3 * HP, :]
        r_m = Region(ar + KT * TT, 5 * TT + 2 * TT)
        GR = r_m.take(2, TT)
        SG = r_m.take(2, TT)
        gtmp = r_m.take(TT)
        FH = view(ar + 12 * TT, KT, TT)
        RL = [view(ar + (20 + s) * TT, TT) for s in range(2)]
        lastn = sem("y_ready")

        def sflat(bank, n, c0=0):
            return PS[0:C, bank:bank + 3 if bank == 0 else bank + 2, :].rearrange("p a b -> p (a b)")[:, c0:c0 + n]

        block = ctx.enter_context(nc.Block())

        @block.sync
        def _(sp):
            def load_w(v, s, wait=True):
                if wait:
                    sp.wait_ge(unit_done, 2 * v + s - 1)
                sp.dma_start(W[:, s, :], A["wu"][bass.ds(2 * v + s, 1), :, :].rearrange("o p n -> (o p) n")
                             if not isinstance(v, int) else A["wu"][2 * v + s]).then_inc(w_in[s], 16)

            def load_pairs(v0, v1):
                with sp.Fori(v0, v1) as v:
                    load_w(v, 0)
                    load_w(v, 1)

            for n in range(4):
                sp.dma_start(XT[:, 2 * n:2 * n + 2, :], A["xt"][:, 2 * n:2 * n + 2, :]).then_inc(x_in, 16)
            sp.dma_start(cst, A["cst"]).then_inc(consts_in, 16)
            sp.dma_start(par, A["par"]).then_inc(consts_in, 16)
            load_w(0, 0, wait=False)
            load_w(0, 1, wait=False)
            sp.dma_start(wf, A["wf"]).then_inc(consts_in, 16)
            sp.dma_start(wl, A["wl"]).then_inc(consts_in, 16)
            sp.dma_start(wg, A["wg"]).then_inc(consts_in, 16)
            sp.dma_start(PT_SB[:, :], A["page_table"]).then_inc(ids_in, 16)
            sp.wait_ge(h_ready, KT)
            sp.dma_start(sh_in, A["sh"]).then_inc(lora_in, 16)
            load_pairs(1, V_FOX0 + 1)
            sp.wait_ge(mixed, RW_T)
            sp.dma_start(A["o_sh"], sh_out).then_inc(sh_stored, 16)

            def keep_tile(kind, p, src):
                sp.dma_start(chunk_dram[:, :, kind, p, :], src[:, p, 0:TP].rearrange("p (c t) -> p c t", c=NC))\
                  .then_inc(prep_stored, 16)

            for p in range(HP):
                sp.wait_ge(pd, 3 * p + 3)
                for kind, src in enumerate((RW[:, 0:HP], RW[:, HP:2 * HP], RW[:, 2 * HP:3 * HP], LW, KK, BB)):
                    keep_tile(kind, p, src)
            sp.wait_ge(pa, 2 + 4 * HP)
            sp.dma_start(bg_dram, BG).then_inc(bg_stored, 16)

            def load_chunk(c):
                src = chunk_dram[:, c] if isinstance(c, int) else chunk_dram[:, bass.ds(c, 1)]\
                    .rearrange("p o a b t -> p (o a) b t")
                sp.dma_start(CH, src).then_inc(st_in, 16)

            def sp_chunk(c, gates, more):
                if more:
                    sp.wait_ge(ch_dve.sem, ch_dve.after(c, "a"))
                    sp.wait_ge(ch_act.sem, ch_act.after(c, "v"))
                    load_chunk(c + 1)
                for s in range(2):
                    if gates:
                        sp_gate(c - C_FOX, s)
                    load_w(c + (V_FOX0 + 1), s)

            def sp_gate(x, s):
                sp.wait_ge(sub_read, 2 * NG * x + (2 * NG * PV_FOX + NG * s + NG + 2))
                dst = gate_dram[2 * x + s] if isinstance(x, int) else gate_dram[bass.ds(2 * x + s, 1)]\
                    .rearrange("o p n -> (o p) n")
                sp.dma_start(dst, SGs[:, s]).then_inc(g_stored[s], 16)

            sp.wait_ge(prep_stored, 16 * 6 * HP)
            sp.wait_ge(bg_stored, 16)
            sp.wait_ge(sh_stored, 16)
            sp.wait_ge(d_col_ready, 1)
            load_chunk(0)
            with sp.Fori(0, C_FOX) as c:
                sp_chunk(c, False, True)
            with sp.Fori(C_FOX, NC - 1) as c:
                sp_chunk(c, True, True)
            sp_chunk(NC - 1, True, False)

            sp.wait_ge(ch_pe.sem, ch_pe.before(NC))
            sp.wait_ge(ch_dve.sem, ch_dve.before(NC))
            sp.dma_start(A["o_sp"], St).then_inc(sp_stored, 16)
            sp.dma_start(dS.rearrange("p b h k -> p (b h k)"), A["st"]).then_inc(ds_load, 16)
            sp.wait_ge(ds_act, 1)
            for p in range(HP):
                sp.dma_start(samp_dram[:, :, p * P:(p + 1) * P].rearrange("k b c -> b k c"),
                             d_nat[p * DEC:(p + 1) * DEC]).then_inc(ds_store, 16)
            sp.wait_ge(ds_store, 16 * HP)

            def spread(dst, kind):
                for e in range(2):
                    sp.dma_start(dst[e * HD:(e + 1) * HD].rearrange("p b h k -> p (b h k)"),
                                 samp_dram[kind, e * (DEC // 2):(e + 1) * (DEC // 2), :]
                                 .rearrange("b n -> (b n)").partition_broadcast(HD)).then_inc(ds_load, 16)

            for dst, kind in ((dKK, 1), (dW, 0), (dB, 2), (dK, 3)):
                spread(dst, kind)
            for e in range(2):
                sp.dma_start(dV[e * HD:(e + 1) * HD],
                             samp_dram[5, e * (DEC // 2):(e + 1) * (DEC // 2), :]
                             .rearrange("b (h v) -> v b h", h=NH),
                             allow_slow_non_contiguous=True).then_inc(ds_load, 16)
            x = NC - C_FOX
            for s in range(2):
                sp_gate(x, s)
                load_w(x + (V_GATE0 + 1), s)
            sp.wait_ge(ds_dve, 1)
            spread(dR, 4)
            sp.wait_ge(ds_dve, 2)
            sp.dma_start(A["o_ss"], dS.rearrange("p b h k -> p (b h k)")).then_inc(out_stored, 16)
            sp.wait_ge(ds_dve, 3)
            for e in range(2):
                sp.dma_start(ysamp_dram[e * (DEC // 2):(e + 1) * (DEC // 2)].rearrange("b h v -> v b h"),
                             dU[e * HD:(e + 1) * HD], allow_slow_non_contiguous=True).then_inc(ds_y, 16)
            sp.wait_ge(ds_y, 32)
            sp.dma_start(dYn[0:DEC], ysamp_dram.rearrange("b h v -> b (h v)")).then_inc(ds_yb, 16)
            with sp.Fori(NC - C_FOX + 1, PV_GATE) as x:
                for s in range(2):
                    sp_gate(x, s)
                    load_w(x + (V_GATE0 + 1), s)
            sp.wait_ge(ds_dve, 4)
            sp.wait_ge(out_stored, 16)
            sp.wait_ge(ds_pe, 2)
            sp.dma_start(BGb, bg_dram).then_inc(bg_back, 16)
            sp.wait_ge(lf_ready, 1)
            sp.dma_start(cneg_dram, f_c[0:NH, :]).then_inc(cneg_stored, 16)
            sp.dma_start(A["o_lf"], lfT[0:NH, :]).then_inc(out_stored, 16)
            sp.dma_start(A["o_kv"], FX[:, HP:3 * HP, :]).then_inc(kv_stored, 16)
            sp.wait_ge(cneg_stored, 16)
            with sp.Fori(0, HP) as i:
                for hl in range(2):
                    if hl == 0:
                        sp.wait_ge(qk_free, i + 1)
                    sp.dma_start(ka[HD:HD + 1, hl, :], cneg_dram[bass.ds(2 * i + hl, 1), :])\
                      .then_inc(cneg_in[hl], 16)
            sp.wait_ge(ids_in, 16)
            sp.wait_ge(ot_read, NC)

            def page_id(i, s, pg):
                at = bass.ds(i * (2 * NPG) + (s * NPG + pg), 1)
                return sp.value_load(PT_SB[0:1, at], min_val=0, max_val=POOL - 1)

            def load_keys(i, s):
                for pg in range(NPG):
                    page = page_id(i, s, pg)
                    sp.dma_start(Kp[:, s, pg, :, :],
                                 A["kp"][bass.ds(page, 1), :, :, :].rearrange("o p h t -> (o p) h t"))\
                      .then_inc(kp_in[s], 16)
                    sp.dma_start(lfp[:, bass.ds(2 * i + s, 1), pg, :].rearrange("p o h -> p (o h)"),
                                 A["vp"][bass.ds(page, 1), :, NH * HD:VW].rearrange("o p h -> (o p) h"))\
                      .then_inc(lfp_in, 16)

            def load_values(i, s):
                for pg in range(NPG):
                    page = page_id(i, s, pg)
                    sp.dma_start(Vp[:, s, pg, :],
                                 A["vp"][bass.ds(page, 1), :, :].rearrange("o p n -> (o p) n"))\
                      .then_inc(vp_in[s], 16)

            for load, used in ((load_keys, kp_used), (load_values, vp_used)):
                load(0, 0)
                load(0, 1)
                with sp.Fori(1, DEC // 2) as i:
                    for s in range(2):
                        sp.wait_ge(used, 2 * i + s - 1)
                        load(i, s)
            sp.wait_ge(da_step, 6)
            sp.dma_start(XT, A["xt"]).then_inc(x_back, 16)

            def gates_back(n):
                for s in range(2):
                    src = gate_dram[2 * n + s] if isinstance(n, int) else gate_dram[bass.ds(2 * n + s, 1)]\
                        .rearrange("o p n -> (o p) n")
                    sp.dma_start(GR[:, s], src).then_inc(g_back[s], 16)

            gates_back(0)
            with sp.Fori(1, KT) as n:
                sp.wait_ge(sg_ready, 2 * n)
                gates_back(n)
                load_w(n + V_BR0, 0)
                load_w(n + V_BR0, 1)
            load_pairs(V_OUT0, PAIRS)
            for k in range(KT):
                sp.wait_ge(lastn, k + 1)
                sp.dma_start(A["o_y"][:, k, :], HT[:, k, :]).then_inc(out_stored, 16)
            sp.wait_ge(kv_stored, 16)
            sp.wait_ge(sp_stored, 16)
            sp.wait_ge(out_stored, 16 * (2 + KT))

        @block.tensor
        def _(pe):
            pe.wait_ge(consts_in, 80)
            pe_norm(pe, 0)
            pe.wait_ge(h_ready, KT)
            pe_unit(pe, 0, 0, HT)
            pe_unit(pe, 0, 1, HT)
            with pe.Fori(1, PV_RW) as v:
                pe_unit(pe, v, 0, HT, late=False)
                pe_unit(pe, v, 1, HT, late=False)
            pe.wait_ge(evac[0], PV_RW)
            pe.wait_ge(evac[1], PV_RW)
            pe.wait_ge(pa, 2)
            for p in range(HP):
                for m in range(2):
                    if p:
                        pe.wait_ge(pa, 2 + 2 * p - 1 + m)
                    rows = slice(m * HD, (m + 1) * HD)
                    for g in range(NG):
                        last = pe.matmul(PS[:, 3 * m + g, 0:G], wl[rows, p * P:(p + 1) * P],
                                         RW[rows, 12, g * G:(g + 1) * G], start=True, stop=True)
                    last.then_inc(pp, 1)
            for p in range(HP):
                for m in range(2):
                    if p == 0:
                        pe.wait_ge(pa, 10)
                    pe.wait_ge(pd, 3 * p + 1 + m)
                    if p and m == 0:
                        pe.wait_ge(pa, 10 + p)
                    if p and m == 1:
                        pe.wait_ge(pd, 3 * p)
                    for g in range(NG):
                        last = pe.matmul(PS[:, 3 * m + g, 0:G], blk, ptmp[m][:, g * G:(g + 1) * G],
                                         start=True, stop=True)
                    last.then_inc(pp, 1)

            for p in range(HP):
                if p == 0:
                    pe.wait_ge(pa, 2 + 3 * HP)
                else:
                    pe.wait_ge(pa, 2 + 3 * HP + p)
                for g in range(NG):
                    last = pe.matmul(PS[:, g, 0:G], wg[:, p * P:(p + 1) * P],
                                     RW[:, 13, g * G:(g + 1) * G], start=True, stop=True)
                last.then_inc(pp, 1)

            pe.wait_ge(pd, 3 * HP)
            pe.wait_ge(pa, 2 + 4 * HP)
            pe.sem_inc(ch_pe.sem, 1)

            def pe_chunk(c):
                fill = Filler(pe, c + V_FOX0)

                def wait(steps, name):
                    pe.wait_ge(steps.sem, steps.after(c, name))

                def natural(src, bank, name):
                    for p in range(HP):
                        last = pe.transpose(PS[0:C, bank, p * P:(p + 1) * P], src[:, p], ident)
                    ch_pe.done(last, name)

                def vcols(h):
                    at = h % HP * P + h // HP * HD
                    return slice(at, at + HD)

                def hrows(h):
                    return slice(h // HP * HD, (h // HP + 1) * HD)

                fill.run(16)
                wait(ch_dve, "k")
                pe.wait_ge(ch_act.sem, ch_act.before(c))
                natural(Kc, 0, "nat_k")
                wait(ch_dve, "b")
                natural(Bc, 1, "nat_b")
                wait(ch_dve, "a")
                natural(AR[:, :, 0], 2, "nat_a")
                natural(Vc, 3, "nat_v")
                for i in range(2):
                    for m, src, bank in (("k", Kc, 4), ("b", Bc, 0)):
                        if i:
                            wait(ch_dve, f"mask_{m}0")
                        elif m == "b":
                            wait(ch_act, "nat_k")
                            wait(ch_dve, "nat_b")
                        for j in range(2):
                            for e in range(2):
                                rows, p = slice(e * HD, (e + 1) * HD), 2 * i + j
                                last = pe.matmul(PS[0:C, bank + e, j * 2 * C:(j + 1) * 2 * C], src[rows, p],
                                                 AR[rows, p].rearrange("p a b -> p (a b)"), start=True,
                                                 stop=True)
                        ch_pe.done(last, f"prod_{m}{i}")
                fill.run(4)
                wait(ch_dve, "mask_k1")
                wait(ch_dve, "nat_v")
                for h in range(NH):
                    last = pe.matmul(PS[0:C, 3, h * HD:(h + 1) * HD], MK[0:C, h, 0], Vn[0:C, vcols(h)],
                                     start=True, stop=True)
                ch_pe.done(last, "z")
                fill.run(4)
                wait(ch_dve, "xt_init")
                for q in range(2):
                    for j in range(4):
                        last = pe.transpose(PS[0:C, q, j * C:(j + 1) * C], XTr[0:C, 4 * q + j], ident[0:C, 0:C])
                    ch_pe.done(last, f"x_{q}")
                for lv in LEVELS:
                    for q in range(2):
                        if q == 0:
                            pe.wait_ge(ch_pool.sem, ch_pool.after(c, f"bm_{lv}"))
                        if lv == 1:
                            wait(ch_act, f"x_{q}")
                        else:
                            wait(ch_dve, f"x_{lv - 1}_{q}_xt")
                        for j in range(4):
                            h = 4 * q + j
                            last = pe.matmul(PS[0:C, q, j * C:(j + 1) * C], Bm[lv % 2][0:C, h], Xm[0:C, h],
                                             start=True, stop=True)
                        ch_pe.done(last, f"t1_{lv}_{q}")
                    fill.run(1)
                    for q in range(2):
                        wait(ch_act, f"t1_{lv}_{q}")
                        if lv == 1 and q == 0:
                            wait(ch_act, "nat_a")
                        for j in range(4):
                            h = 4 * q + j
                            if lv < N_LV - 1:
                                pe.matmul(PS[0:C, 2 + q, j * C:(j + 1) * C], XTr[0:C, h], T1[0:C, h],
                                          start=True, stop=True)
                            last = pe.matmul(PS[0:C, 4 + q, j * C:(j + 1) * C], T1[0:C, h], XTr[0:C, h],
                                             start=True, stop=True)
                        ch_pe.done(last, f"t2_{lv}_{q}")
                    fill.run(1)
                fill.run(2)
                wait(ch_dve, f"x_{N_LV - 1}_1_xt")
                for h in range(NH):
                    e, p = h // HP, h % HP
                    last = pe.matmul(PS[e * HD:(e + 1) * HD, 0, p * C:(p + 1) * C], An[0:C, vcols(h)],
                                     XTr[0:C, h], start=True, stop=True)
                ch_pe.done(last, "wt")
                fill.run(2)
                wait(ch_act, "wt")
                wait(ch_act, "z")
                for h in range(NH):
                    e, p, rows = h // HP, h % HP, hrows(h)
                    out = PS[0:C, 4 + e, p * HD:(p + 1) * HD]
                    pe.matmul(out, XTr[0:C, h], Zm[0:C, h * HD:(h + 1) * HD], start=True, stop=False)
                    last = pe.matmul(out, WT[rows, p], St[rows, p], start=False, stop=True)
                ch_pe.done(last, "u")
                fill.run(2)
                wait(ch_act, "nu")
                for h in range(NH):
                    e, p, rows = h // HP, h % HP, hrows(h)
                    out = PS[0:C, 2 + e, p * HD:(p + 1) * HD]
                    pe.matmul(out, AR[rows, p, 1], St[rows, p], start=True, stop=False)
                    pe.matmul(out, MK[0:C, h, 1], Vn[0:C, vcols(h)], start=False, stop=False)
                    last = pe.matmul(out, MB[0:C, h, 1], NU[0:C, h * HD:(h + 1) * HD], start=False, stop=True)
                ch_pe.done(last, "y")
                for h in range(NH):
                    p, rows = h % HP, hrows(h)
                    out = PS[rows, 1, p * HD:(p + 1) * HD]
                    pe.matmul(out, ident[rows, rows], St[rows, p], start=True, stop=False)
                    pe.matmul(out, Kn[0:C, vcols(h)], Vn[0:C, vcols(h)], start=False, stop=False)
                    last = pe.matmul(out, Bn[0:C, vcols(h)], NU[0:C, h * HD:(h + 1) * HD], start=False, stop=True)
                ch_pe.done(last, "s")
                fill.run()
                wait(ch_dve, "norm")
                for p in range(HP):
                    last = pe.transpose(PS[:, 0, p * C:(p + 1) * C], Yc[0:C, p * P:(p + 1) * P], ident[0:C, 0:C])
                ch_pe.done(last, "yt")

            with pe.Fori(0, C_FOX) as c:
                pe_chunk(c)
            with pe.Fori(C_FOX, NC) as c:
                pe_chunk(c)

            pe.wait_ge(ch_act.sem, ch_act.before(NC))
            for kind in range(6):
                last = pe.transpose(PS[0:HP * DEC, kind // 4, kind % 4 * P:(kind % 4 + 1) * P],
                                    d_col[:, kind].rearrange("p a b -> p (a b)"), ident)
            last.then_inc(ds_pe, 1)
            pe.wait_ge(ds_act, 1)
            for k in range(KT):
                for g in range(NG):
                    last = pe.matmul(PS[0:NH, g, 0:G], wf[:, k, :], HT[:, k, g * G:(g + 1) * G],
                                     start=(k == 0), stop=(k == KT - 1))
            last.then_inc(f_ready, 1)
            for t in range(NC):
                if t >= 2:
                    pe.wait_ge(vt_read, t - 1)
                for hp in range(HP):
                    last = pe.transpose(PS[0:C, 3 + t % 2, hp * P:(hp + 1) * P],
                                        FX[:, 2 * HP + hp, t * C:(t + 1) * C], ident)
                last.then_inc(vt_ready, 1)

            with pe.Fori(V_GATE0 + (NC - C_FOX), V_BR0) as v:
                Filler(pe, v).run()
            pe.wait_ge(ds_dve, 4)
            for p in range(HP):
                last = pe.transpose(PS[:, 2, p * DEC:(p + 1) * DEC], dYn[0:DEC, p * P:(p + 1) * P],
                                    ident[0:DEC, 0:DEC])
            last.then_inc(ds_pe, 1)
            pe.wait_ge(vt_read, NC)
            pe.wait_ge(f_read, 1)
            pe.wait_ge(sub_read, 2 + 2 * NG * PV_FILL)
            pe.wait_ge(ds_act, 2 + HP)
            with pe.Fori(0, HP) as i:
                def scores(j):
                    hl, qt = tiles[j]
                    if qt == 0:
                        pe.wait_ge(qk_staged, 2 * i + hl + 1)
                        pe.wait_ge(cneg_in[hl], 16 * i + 16)
                    bank = 0 if j % 2 else 3
                    if j >= 2:
                        pe.wait_ge(p_ready, N_IT * i + j - 1)
                    for c0 in range(0, (qt + 1) * C, 512):
                        n = min(512, (qt + 1) * C - c0)
                        last = pe.matmul(PS[0:C, bank + c0 // 512, 0:n],
                                         qa[0:HD + 1, hl, qt * C:(qt + 1) * C],
                                         ka[0:HD + 1, hl, c0:c0 + n], start=True, stop=True)
                    last.then_inc(s_done, 1)

                def transposed(j):
                    hl, qt = tiles[j]
                    pe.wait_ge(p_ready, N_IT * i + j + 1)
                    for g in range(groups[j]):
                        n = gr_before[j] + g
                        slot = n % 2
                        if n >= 2:
                            pe.wait_ge(pt_read[slot], (N_GR // 2) * i + n // 2)
                        for b in range(4 * g, min(4 * g + 4, qt + 1)):
                            last = pe.transpose(PS[0:C, 5 + slot, (b - 4 * g) * C:(b - 4 * g + 1) * C],
                                                Pm[0:C, j % 2, b * C:(b + 1) * C], ident[0:C, 0:C])
                        last.then_inc(pt_done, 1)

                def values(j):
                    hl, qt = tiles[j]
                    end = gr_before[j] + groups[j]
                    pe.wait_ge(pt_read[0], (N_GR // 2) * i + (end + 1) // 2)
                    if end >= 2:
                        pe.wait_ge(pt_read[1], (N_GR // 2) * i + end // 2)
                    if j:
                        pe.wait_ge(o_read, N_IT * i + j)
                    for b in range(qt + 1):
                        last = pe.matmul(PS[0:C, 7, 0:HD], PTm[0:C, j % 2, b, :],
                                         vnat[0:C, b, bass.ds(i * P + hl * HD, HD)],
                                         start=(b == 0), stop=(b == qt))
                    last.then_inc(pv_done, 1)

                scores(0)
                for j in range(N_IT):
                    if j + 1 < N_IT:
                        scores(j + 1)
                    transposed(j)
                    if j:
                        values(j - 1)
                values(N_IT - 1)
            for t in range(NC):
                pe.wait_ge(o_read, N_IT * HP)
                if t >= 2:
                    pe.wait_ge(ot_read, t - 1)
                for hp in range(HP):
                    last = pe.transpose(PS[:, 6 + t % 2, hp * C:(hp + 1) * C],
                                        onat[0:C, t, hp * P:(hp + 1) * P], ident[0:C, 0:C])
                last.then_inc(ot_ready, 1)
            pe.wait_ge(ot_read, NC)

            pe.wait_ge(da_step, 1)
            with pe.Fori(0, DEC // 2) as i:
                for s in range(2):
                    pe.wait_ge(kp_in[s], 16 * NPG * i + 16 * NPG)
                    for pg in range(NPG):
                        for hp in range(HP):
                            last = pe.matmul(
                                PS[:, 6, bass.ds(i * 2 * NPG * NH + (s * NPG + pg) * NH + 2 * hp, 2)],
                                Kp[:, s, pg, hp, :],
                                qbd[:, hp, bass.ds(2 * i + s, 1), :].rearrange("p o h -> p (o h)"),
                                start=True, stop=True)
                    last.then_inc(kp_used, 1)
            pe.wait_ge(lfp_in, 16 * NPG * DEC)
            bias4 = PS[:, 7, :].rearrange("p (b g h) -> p b g h", b=DEC, g=NPG)
            pe.matmul(PS[:, 7, :], suf, lfp.rearrange("p b g h -> p (b g h)"), start=True, stop=False)
            for s in range(1, NPG):
                pe.matmul(bias4[:, :, 0:NPG - s, :], ones, lfp[:, :, s:NPG, :], start=False, stop=False)
            last = pe.matmul(bias4, ones[0:NH, :],
                             lfd[0:NH].unsqueeze(2).to_broadcast([NH, DEC, NPG, NH]), start=False, stop=True)
            last.then_inc(da_ready, 1)
            last = pe.matmul(PS[:, 5, 0:DEC * NH].rearrange("p (b a h) -> p a b h", b=DEC, a=HP), ones,
                             qkbd, start=True, stop=True)
            last.then_inc(da_ready, 1)
            pe.wait_ge(da_step, 2)
            pe.transpose(PS[0:DEC * NH, 4, 0:P], da_mx, ident).then_inc(da_ready, 1)
            pe.wait_ge(da_step, 3)
            pe.matmul(PS[:, 4, 256:256 + DEC * NH], ones[0:DEC * NH, :], da_dg[0:DEC * NH], start=True,
                      stop=True).then_inc(da_ready, 1)
            pe.wait_ge(da_step, 5)
            pe.matmul(PS[:, 4, 384:384 + DEC * NH], ones, da_den, start=True, stop=True)\
              .then_inc(da_ready, 1)
            with pe.Fori(0, DEC // 2) as i:
                for s in range(2):
                    pe.wait_ge(vp_in[s], 16 * NPG * i + 16 * NPG)
                    for hp in range(HP):
                        for pg in range(NPG):
                            last = pe.matmul(
                                PS[:, 7, bass.ds(i * 4 + 2 * s + 2 * DEC * hp, 2)],
                                Vp[:, s, pg, hp * P:(hp + 1) * P],
                                da_s[:, bass.ds(2 * i + s, 1), pg, 2 * hp:2 * hp + 2]
                                .rearrange("p o h -> p (o h)"),
                                start=(pg == 0), stop=(pg == NPG - 1))
                    last.then_inc(vp_used, 1)
            pe.wait_ge(da_step, 6)
            with pe.Fori(V_BR0, V_OUT0) as v:
                pe_unit(pe, v, 0, YT, HP)
                pe_unit(pe, v, 1, FX, HP)
            pe.wait_ge(mg_ready, KT)
            with pe.Fori(V_OUT0, V_OUT0 + PV_OUT) as v:
                pe_unit(pe, v, 0, MG)
                pe_unit(pe, v, 1, MG)
            pe.wait_ge(evac[0], V_FF0 - PV_FILL)
            pe_norm(pe, 1)
            pe.wait_ge(h_ready, 2 * KT)
            with pe.Fori(0, FF_CH) as c:
                with pe.Fori(0, KT // 2) as j:
                    pe_unit(pe, KT * c + j + V_FF0, 0, HT)
                    pe_unit(pe, KT * c + j + V_FF0, 1, HT)
                with pe.Fori(0, KT // 2) as j:
                    pe.wait_ge(ff_ready, KT * c + (KT + 2))
                    pe_unit(pe, KT * c + j + (V_FF0 + KT // 2), 0, FH)
                    pe_unit(pe, KT * c + j + (V_FF0 + KT // 2), 1, FH)
            pe.wait_ge(evac[0], PAIRS - PV_FILL)
            pe_norm(pe, 2)

        @block.scalar
        def _(act):
            order = Order(act, act_order)
            act.wait_ge(consts_in, 80)
            act.wait_ge(x_in, 64)
            act_norm(act, 0)

            def keep(v, s, dst):
                act.wait_ge(unit_done, 2 * v + s + 1)
                act.copy(g3(dst), grp(s)).then_inc(evac[s], 1)

            act.wait_ge(h_ready, KT)
            with act.Fori(0, PV_RW) as v:
                for s in range(2):
                    keep(v, s, RW[:, bass.ds(2 * v + s, 1), :].rearrange("p o n -> p (o n)"))
            act.wait_ge(mixed, RW_T)
            act.activation(RW[0:HD, 12, :], RW[0:HD, 12, :], ACT.Tanh).then_inc(pa, 1)
            act.activation(RW[:, 13, :], RW[:, 13, :], ACT.Sigmoid).then_inc(pa, 1)
            for p in range(HP):
                for m, dst, par0 in ((0, LW, V_W0), (1, BB, V_A0)):
                    act.wait_ge(pp, 2 * p + m + 1)
                    act.activation(g3(dst[:, p]), grp(m), ACT.Sigmoid,
                                   bias=par[:, par0 + p:par0 + p + 1]).then_inc(pa, 1)
            for p in range(HP):
                act.wait_ge(pp, 2 * HP + 2 * p + 1)
                act.activation(g3(ptmp[0]), grp(0), ACT.Sqrt).then_inc(pa, 1)
            for p in range(HP):
                act.wait_ge(pp, 4 * HP + p + 1)
                act.copy(g3(GT[:, p]), grp(0)).then_inc(pa, 1)
            act.wait_ge(pd, 3 * HP)
            for kind, src in ((1, KK), (2, BB), (3, RW[:, HP:2 * HP]), (4, RW[:, 0:HP]), (5, RW[:, 2 * HP:3 * HP])):
                order(act.copy(d_col[:, kind], src[:, :, TP:TS]))
            order(act.activation(d_col[:, 0], LW[:, :, TP:TS], ACT.Exp))
            act.sem_inc(d_col_ready, 1)
            act.wait_ge(prep_stored, 16 * 6 * HP)
            act.wait_ge(bg_stored, 16)
            act.wait_ge(sh_stored, 16)
            act.sem_inc(sub_read, 2)
            act.sem_inc(g_stored[0], 16)
            act.sem_inc(g_stored[1], 16)
            act.sem_inc(ch_act.sem, 1)

            def gate_out(x, m):
                s, g = divmod(m, NG)
                if g == 0:
                    act.wait_ge(g_stored[s], 16 * x + 16)
                act_fill(act, x + V_GATE0, m, SGs[:, s, g * G:(g + 1) * G])

            def act_chunk(c, gates):
                def out(m):
                    if gates:
                        gate_out(c - C_FOX, m)
                    else:
                        s, g = divmod(m, NG)
                        act_fill(act, c + V_FOX0, m, FX[:, bass.ds(2 * c + s, 1), g * G:(g + 1) * G]
                                 .rearrange("p o n -> p (o n)"))

                def wait(steps, name):
                    act.wait_ge(steps.sem, steps.after(c, name))

                here = bass.ds(c * C, C)
                act.wait_ge(ch_pe.sem, ch_pe.before(c))
                act.wait_ge(ch_dve.sem, ch_dve.before(c))
                act.wait_ge(st_in, 16 * c + 16)
                ch_act.done(act.copy(Vc, CH[:, 2]), "v")
                wait(ch_dve, "scan_3")
                ch_act.done(act.activation(E1, Lc, ACT.Exp), "e1")
                ch_act.done(act.activation(E3, Lc, ACT.Exp, scale=-1.0), "e3")
                wait(ch_dve, "lm")
                ch_act.done(act.activation(E2, Lm, ACT.Exp), "e2")
                out(0)
                out(1)
                wait(ch_pe, "nat_k")
                ch_act.done(act.copy(Kn[0:C], PS[0:C, 0, :]), "nat_k")
                wait(ch_pe, "nat_a")
                ch_act.done(act.copy(An[0:C], PS[0:C, 2, :]), "nat_a")
                wait(ch_pe, "z")
                ch_act.done(act.copy(Zm[0:C], PS[0:C, 3, :]), "z")

                def quad(ap, q):
                    return ap[0:C, 4 * q:4 * q + 4].rearrange("p a b -> p (a b)")

                for q in range(2):
                    wait(ch_pe, f"x_{q}")
                    ch_act.done(act.copy(quad(Xm, q), PS[0:C, q, 0:4 * C]), f"x_{q}")
                out(2)
                for lv in LEVELS:
                    for q in range(2):
                        wait(ch_pe, f"t1_{lv}_{q}")
                        if lv > 1:
                            wait(ch_pe, f"t2_{lv - 1}_{q}")
                        ch_act.done(act.copy(quad(T1, q), PS[0:C, q, 0:4 * C]), f"t1_{lv}_{q}")
                    if lv == 4:
                        out(3)
                wait(ch_pe, "wt")
                ch_act.done(act.copy(WT, PS[:, 0, 0:HP * C].rearrange("p (a b) -> p a b", a=HP)), "wt")
                out(4)
                wait(ch_pe, "u")
                ch_act.done(act.mul(NU[0:C].rearrange("p (e n) -> p e n", e=2), PS[0:C, 4:6, 0:HP * HD],
                                    -1.0), "nu")
                wait(ch_dve, "var")
                ch_act.done(act.activation(gst[0:C, 2], gst[0:C, 1], ACT.Ln, scale=1.0 / HD,
                                           bias=par[0:C, V_GEPS:V_GEPS + 1]), "ln")
                wait(ch_act, "ln")
                ch_act.done(act.activation(gst[0:C, 3], gst[0:C, 2], ACT.Exp, scale=-0.5), "rstd")
                out(5)
                wait(ch_pe, "yt")
                for p in range(HP):
                    ch_act.done(act.activation(YT[:, p, here], PS[:, 0, p * C:(p + 1) * C], ACT.Identity,
                                               scale=par[:, V_LW + p:V_LW + p + 1],
                                               bias=par[:, V_LB + p:V_LB + p + 1]), f"y_{p}")
            with act.Fori(0, C_FOX) as c:
                act_chunk(c, False)
            with act.Fori(C_FOX, NC) as c:
                act_chunk(c, True)
            act.wait_ge(ch_pe.sem, ch_pe.before(NC))
            act.wait_ge(ds_pe, 1)
            act.copy(d_nat[0:HP * DEC].rearrange("p k c -> p (k c)"),
                     PS[0:HP * DEC, 0:2, :].rearrange("p a b -> p (a b)")[:, 0:6 * P]).then_inc(ds_act, 1)
            act.wait_ge(f_ready, 1)
            act.wait_ge(sp_stored, 16)
            order(act.activation(g3(f_neg[0:NH]), PS[0:NH, 0:3, 0:G], ACT.Identity,
                                 bias=par[0:NH, V_BF:V_BF + 1]))
            order(act.activation(f_t[0:NH], f_neg[0:NH], ACT.Abs))
            order(act.activation(f_t[0:NH], f_t[0:NH], ACT.Exp, scale=-1.0))
            act.activation(f_t[0:NH], f_t[0:NH], ACT.Ln,
                           bias=cst[0:NH, C_ONE:C_ONE + 1]).then_inc(f_read, 1)
            for t in range(NC):
                act.wait_ge(vt_ready, t + 1)
                act.copy(vnat[0:C, t, :], PS[0:C, 3 + t % 2, :]).then_inc(vt_read, 1)

            with act.Fori(NC - C_FOX, PV_GATE) as x:
                for m in range(2 * NG):
                    gate_out(x, m)
            act.wait_ge(ds_var, 1)
            order(act.activation(dst4[0:DEC, 2], dst4[0:DEC, 1], ACT.Ln, scale=1.0 / HD,
                                 bias=par[0:DEC, V_GEPS:V_GEPS + 1]))
            act.activation(dst4[0:DEC, 3], dst4[0:DEC, 2], ACT.Exp, scale=-0.5).then_inc(ds_act, 1)
            act.wait_ge(ds_pe, 2)
            for p in range(HP):
                act.activation(YT[:, p, TP:TS], PS[:, 2, p * DEC:(p + 1) * DEC], ACT.Identity,
                               scale=par[:, V_LW + p:V_LW + p + 1],
                               bias=par[:, V_LB + p:V_LB + p + 1]).then_inc(ds_act, 1)
            with act.Fori(0, HP) as i:
                def exps(j):
                    hl, qt = tiles[j]
                    bank = 0 if j % 2 else 3
                    n = (qt + 1) * C
                    act.wait_ge(max_ready, N_IT * i + j + 1)
                    if j >= 2:
                        act.wait_ge(pt_done, N_GR * i + gr_before[j - 1])
                    if j >= 4:
                        act.wait_ge(o_read, N_IT * i + j - 3)
                    act.activation(Pm[0:C, j % 2, 0:n], sflat(bank, n), ACT.Exp,
                                   bias=rowmax[0:C, j % 2:j % 2 + 1],
                                   accum_out=rowsum[0:C, j % 4:j % 4 + 1]).then_inc(p_ready, 1)

                def blocks(j):
                    hl, qt = tiles[j]
                    for g in range(groups[j]):
                        n = gr_before[j] + g
                        if n % 2 == 0:
                            act.wait_ge(pt_done, N_GR * i + n + 1)
                            if g == 0 or g == 1:
                                if j >= 2:
                                    act.wait_ge(pv_done, N_IT * i + j - 1)
                            m = min(4, qt + 1 - 4 * g)
                            act.copy(PTm[0:C, j % 2, 4 * g:4 * g + m, :],
                                     PS[0:C, 5, 0:m * C].rearrange("p (a b) -> p a b", a=m))\
                               .then_inc(pt_read[0], 1)

                exps(0)
                for j in range(N_IT):
                    if j + 1 < N_IT:
                        exps(j + 1)
                    blocks(j)
            for t in range(NC):
                act.wait_ge(ot_ready, t + 1)
                act.copy(FX[:, 0:HP, t * C:(t + 1) * C],
                         PS[:, 6 + t % 2, 0:HP * C].rearrange("p (a b) -> p a b", a=HP)).then_inc(ot_read, 1)
            act.wait_ge(da_step, 4)
            act.activation(da_s.rearrange("p b g h -> p (b g h)"), da_s.rearrange("p b g h -> p (b g h)"),
                           ACT.Exp).then_inc(da_exp, 1)
            act.activation(da_po, da_po, ACT.Exp).then_inc(da_exp, 1)
            with act.Fori(0, KT) as n:
                for s in range(2):
                    act.wait_ge(g_back[s], 16 * n + 16)
                    act.wait_ge(sg_used, 2 * n + (s + 1))
                    act.activation(SG[:, s], GR[:, s], ACT.Sigmoid).then_inc(sg_ready, 1)
            act.wait_ge(xr_ready, KT)
            act_norm(act, 1)
            with act.Fori(0, FF_CH) as c:
                with act.Fori(0, KT // 2) as j:
                    for s in range(2):
                        act.wait_ge(unit_done, 2 * KT * c + 2 * j + (2 * V_FF0 + s + 1))
                        act.wait_ge(ff_ready, KT * c + 2 * j + (s + 1))
                        act.activation(g3(RL[s]), grp(s), ACT.Relu).then_inc(evac[s], 1)
            act.wait_ge(evac[0], PAIRS - PV_FILL)
            act.wait_ge(evac[1], PAIRS - PV_FILL)
            act_norm(act, 2)

        @block.vector
        def _(dve):
            order = Order(dve, dve_order)
            dve.wait_ge(consts_in, 80)
            dve.wait_ge(x_in, 64)
            dve_norm(dve, 0, V_NM, order)
            mix = Order(dve, mix_order)
            dve.wait_ge(lora_in, 16)
            mix(dve.memset(mtmp[:, TS:TT], 0.0))
            with dve.Fori(0, PV_RW) as i:
                mix.enter(i, 8)
                for s in range(2):
                    tile = bass.ds(2 * i + s, 1)

                    def cut(a, b):
                        return RW[:, tile, a:b].rearrange("p o n -> p (o n)")

                    dve.wait_ge(evac[s], i + 1)
                    mix(dve.tensor_copy(sh_out[:, tile, :], RW[:, tile, TP - 1:TS]))
                    mix(dve.tensor_tensor(mtmp[:, 1:TP], cut(0, TP - 1), cut(1, TP), ALU.subtract))
                    mix(dve.tensor_scalar(mtmp[:, 0:1], cut(0, 1), -1.0, None, ALU.mult))
                    mix(dve.tensor_tensor(mtmp[:, TP:TS], sh_in[:, tile, :].rearrange("p o n -> p (o n)"),
                                          cut(TP, TS), ALU.subtract))
                    dve.scalar_tensor_tensor(cut(0, TT), mtmp, par[:, bass.ds(2 * i + (V_MU + s), 1)],
                                             cut(0, TT), ALU.mult, ALU.add).then_inc(mixed, 1)
                    dve.wait_ge(mixed, 2 * i + (s + 1))
                mix.leave(PV_RW)
            for p in range(HP):
                r_, k_, v_ = RW[:, p, :], RW[:, HP + p, :], RW[:, 2 * HP + p, :]
                if p == 0:
                    dve.wait_ge(pa, 10)
                order(dve.tensor_scalar(LW[:, p], LW[:, p], -E_HALF, None, ALU.mult))
                order(dve.tensor_scalar(KK[:, p], k_, par[:, V_KK + p:V_KK + p + 1], None, ALU.mult))
                dve.tensor_tensor(ptmp[0], KK[:, p], KK[:, p], ALU.mult).then_inc(pd, 1)
                order(dve.tensor_scalar(mtmp, BB[:, p], 1.0, par[:, V_KA + p:V_KA + p + 1],
                                        ALU.subtract, ALU.mult))
                order(dve.scalar_tensor_tensor(k_, mtmp, 1.0, k_, ALU.add, ALU.mult))
                dve.scalar_tensor_tensor(ptmp[1], r_, par[:, V_RK + p:V_RK + p + 1], k_, ALU.mult, ALU.mult)\
                   .then_inc(pd, 1)
                dve.wait_ge(pa, 11 + p)
                order(dve.tensor_scalar(ptmp[0], ptmp[0], 1e-12, None, ALU.max))
                order(dve.reciprocal(ptmp[0], ptmp[0]))
                order(dve.tensor_tensor(KK[:, p], KK[:, p], ptmp[0], ALU.mult))
                order(dve.tensor_tensor(BB[:, p], KK[:, p], BB[:, p], ALU.mult))
                dve.wait_ge(pp, 2 * HP + 2 * p + 2)
                dve.tensor_tensor(g3(BON[:, p]), grp(1), g3(v_), ALU.mult).then_inc(pd, 1)
                dve.wait_ge(pd, 3 * p + 3)

            dve.wait_ge(prep_stored, 16 * 6 * HP)
            dve.wait_ge(bg_stored, 16)
            dve.wait_ge(sh_stored, 16)
            dve.wait_ge(d_col_ready, 1)
            order(dve.memset(St, 0.0))
            order(dve.memset(YT[:, :, TS:TT], 0.0))
            dve.sem_inc(ch_dve.sem, 1)
            with dve.Fori(0, NC) as c:
                def wait(steps, name):
                    dve.wait_ge(steps.sem, steps.after(c, name))

                def done(ins, name):
                    ch_dve.done(ins, name)
                    dve.wait_ge(ch_dve.sem, ch_dve.after(c, name))

                dve.wait_ge(ch_pe.sem, ch_pe.before(c))
                dve.wait_ge(st_in, 16 * c + 16)
                for p in range(HP):
                    done(dve.tensor_tensor_scan(Lc[:, p], ones[:, 0:C], CH[:, 3, p], 0.0, ALU.mult, ALU.add),
                         f"scan_{p}")
                done(dve.tensor_tensor(Lm, Lc, CH[:, 3], ALU.subtract), "lm")
                wait(ch_act, "e1")
                done(dve.tensor_tensor(AR[:, :, 1], CH[:, 0], E1, ALU.mult), "r")
                wait(ch_act, "e3")
                done(dve.tensor_tensor(Kc, CH[:, 1], E3, ALU.mult), "k")
                done(dve.tensor_tensor(Bc, CH[:, 5], E3, ALU.mult), "b")
                wait(ch_act, "e2")
                done(dve.tensor_tensor(AR[:, :, 0], CH[:, 4], E2, ALU.mult), "a")
                wait(ch_pe, "nat_b")
                done(dve.tensor_copy(Bn[0:C], PS[0:C, 1, :]), "nat_b")
                wait(ch_pe, "nat_v")
                done(dve.tensor_copy(Vn[0:C], PS[0:C, 3, :]), "nat_v")
                cm = cst[0:C, C_CM:C_CM + 2 * C].unsqueeze(1).unsqueeze(1).to_broadcast([C, 2, 2, 2 * C])
                for i in range(2):
                    for m, dst, bank in (("k", MK, 4), ("b", MB, 0)):
                        wait(ch_pe, f"prod_{m}{i}")
                        done(dve.tensor_tensor(
                            dst[0:C].rearrange("p (e a) x t -> p e a (x t)", e=2)[:, :, 2 * i:2 * i + 2],
                            PS[0:C, bank:bank + 2, 0:4 * C].rearrange("p e (a n) -> p e a n", a=2),
                            cm, ALU.mult), f"mask_{m}{i}")
                wait(ch_pool, "bm_0")
                done(dve.tensor_tensor(XTr[0:C], ident[0:C, 0:C].unsqueeze(1).to_broadcast([C, NH, C]),
                                       Bm[0][0:C], ALU.subtract), "xt_init")

                def quad(ap, q):
                    return ap[0:C, 4 * q:4 * q + 4].rearrange("p a b -> p (a b)")

                for lv in LEVELS:
                    for q in range(2):
                        wait(ch_pe, f"t2_{lv}_{q}")
                        if lv < N_LV - 1:
                            done(dve.tensor_tensor(quad(Xm, q), quad(Xm, q), PS[0:C, 2 + q, 0:4 * C],
                                                   ALU.subtract), f"x_{lv}_{q}_x")
                        done(dve.tensor_tensor(quad(XTr, q), quad(XTr, q), PS[0:C, 4 + q, 0:4 * C],
                                               ALU.subtract), f"x_{lv}_{q}_xt")

                def heads(ap):
                    return ap.rearrange("p (h v) -> p h v", h=NH)

                def spread(ap):
                    return ap.unsqueeze(2).to_broadcast([C, NH, HD])

                def by_head(ap):
                    return ap.rearrange("p (e a v) -> p e a v", e=2, a=HP)

                def spread4(k):
                    return gst[0:C, k].rearrange("p (e a) -> p e a", e=2).unsqueeze(3).to_broadcast([C, 2, HP, HD])

                y = PS[0:C, 2:4, 0:HP * HD].rearrange("p e (a v) -> p e a v", a=HP)
                ych = Yc[0:C].rearrange("p (a e v) -> p e a v", a=HP, e=2)
                wait(ch_pe, "y")
                done(dve.tensor_reduce(gst[0:C, 0].rearrange("p (e a) -> p e a", e=2), y, AX.X, ALU.add), "sum")
                done(dve.tensor_scalar(gst[0:C, 0], gst[0:C, 0], 1.0 / HD, None, ALU.mult), "mean")
                wait(ch_pe, "s")
                done(dve.tensor_tensor(St, PS[:, 1, 0:HP * HD].rearrange("p (a b) -> p a b", a=HP),
                                       E1[:, :, C - 1:C].to_broadcast([P, HP, HD]), ALU.mult), "state")
                done(dve.tensor_tensor(ych, y, spread4(0), ALU.subtract), "center")
                done(dve.tensor_tensor(by_head(Zm[0:C]), ych, ych, ALU.mult), "sq")
                done(dve.tensor_reduce(gst[0:C, 1].rearrange("p (e a) -> p e a", e=2), by_head(Zm[0:C]), AX.X,
                                       ALU.add), "var")
                wait(ch_act, "rstd")
                done(dve.tensor_tensor(ych, ych, spread4(3), ALU.mult), "norm")

            def on_keys(ap):
                return ap.unsqueeze(3).to_broadcast([P, DEC // 2, NH, HD])

            dve.wait_ge(ds_load, 16 * 11)
            order(dve.tensor_tensor(dT, dS, dKK, ALU.mult))
            order(dve.tensor_reduce(dU, dT, AX.X, ALU.add))
            dve.sem_inc(ds_dve, 1)
            order(dve.tensor_tensor(dS, dS, dW, ALU.mult))
            order(dve.tensor_tensor(dT, dB, on_keys(dU), ALU.mult))
            order(dve.tensor_tensor(dS, dS, dT, ALU.subtract))
            order(dve.tensor_tensor(dT, dK, on_keys(dV), ALU.mult))
            dve.tensor_tensor(dS, dS, dT, ALU.add).then_inc(ds_dve, 1)
            dve.wait_ge(ds_dve, 2)
            dve.wait_ge(ds_load, 16 * 13)
            order(dve.tensor_tensor(dT, dS, dR, ALU.mult))
            dve.tensor_reduce(dU, dT, AX.X, ALU.add).then_inc(ds_dve, 1)
            dve.wait_ge(ds_yb, 16)

            def heads(ap):
                return ap.rearrange("p (h v) -> p h v", h=NH)

            def spread(ap):
                return ap.unsqueeze(2).to_broadcast([DEC, NH, HD])

            order(dve.tensor_reduce(dst4[0:DEC, 0], heads(dYn[0:DEC]), AX.X, ALU.add))
            order(dve.tensor_scalar(dst4[0:DEC, 0], dst4[0:DEC, 0], 1.0 / HD, None, ALU.mult))
            order(dve.tensor_tensor(heads(dYn[0:DEC]), heads(dYn[0:DEC]), spread(dst4[0:DEC, 0]), ALU.subtract))
            order(dve.tensor_tensor(dSQ[0:DEC], dYn[0:DEC], dYn[0:DEC], ALU.mult))
            order(dve.tensor_reduce(dst4[0:DEC, 1], heads(dSQ[0:DEC]), AX.X, ALU.add))
            dve.sem_inc(ds_var, 1)
            dve.wait_ge(ds_act, 2)
            dve.tensor_tensor(heads(dYn[0:DEC]), heads(dYn[0:DEC]), spread(dst4[0:DEC, 3]), ALU.mult)\
               .then_inc(ds_dve, 1)
            dve.wait_ge(f_read, 1)
            order(dve.tensor_scalar(lfT[0:NH], f_neg[0:NH], 0.0, None, ALU.min))
            order(dve.tensor_tensor(lfT[0:NH], lfT[0:NH], f_t[0:NH], ALU.subtract))
            order(dve.memset(f_ones[0:NH], 1.0))
            order(dve.tensor_tensor_scan(f_c[0:NH], f_ones[0:NH], lfT[0:NH, 0:TP], 0.0, ALU.mult, ALU.add))
            dve.tensor_scalar(f_c[0:NH], f_c[0:NH], -1.0, None, ALU.mult).then_inc(lf_ready, 1)

            dve.wait_ge(bg_back, 16)
            dve.wait_ge(ds_act, 2 + HP)
            order(dve.tensor_tensor(YT, YT, BGb[:, 0:HP], ALU.add))
            dve.tensor_tensor(YT, YT, BGb[:, HP:2 * HP], ALU.mult).then_inc(o_done, 1)
            dve.wait_ge(o_done, 1)
            dve.wait_ge(cneg_stored, 16)
            order(dve.memset(qa[HD:HD + 1, :, :], 1.0))
            with dve.Fori(0, HP) as i:
                def maxes(j):
                    hl, qt = tiles[j]
                    bank = 0 if j % 2 else 3
                    dve.wait_ge(s_done, N_IT * i + j + 1)
                    diag = sflat(bank, C, qt * C)
                    order(dve.tensor_tensor(diag, diag, cst[0:C, C_AM:C_AM + C], ALU.add))
                    dve.tensor_reduce(rowmax[0:C, j % 2:j % 2 + 1], sflat(bank, (qt + 1) * C), AX.X, ALU.max,
                                      negate=True).then_inc(max_ready, 1)

                def blocks(j):
                    hl, qt = tiles[j]
                    for g in range(groups[j]):
                        n = gr_before[j] + g
                        if n % 2 == 1:
                            dve.wait_ge(pt_done, N_GR * i + n + 1)
                            if j >= 2:
                                dve.wait_ge(pv_done, N_IT * i + j - 1)
                            m = min(4, qt + 1 - 4 * g)
                            dve.tensor_copy(PTm[0:C, j % 2, 4 * g:4 * g + m, :],
                                            PS[0:C, 6, 0:m * C].rearrange("p (a b) -> p a b", a=m))\
                               .then_inc(pt_read[1], 1)

                def output(j):
                    hl, qt = tiles[j]
                    dve.wait_ge(pv_done, N_IT * i + j + 1)
                    order(dve.reciprocal(rowinv[0:C, j % 2:j % 2 + 1], rowsum[0:C, j % 4:j % 4 + 1]))
                    dve.tensor_scalar(onat[0:C, qt, bass.ds(i * P + hl * HD, HD)], PS[0:C, 7, 0:HD],
                                      rowinv[0:C, j % 2:j % 2 + 1], None, ALU.mult).then_inc(o_read, 1)

                order.enter(i, 2 * N_IT + 2)
                dve.sem_inc(qk_free, 1)
                for hl in range(2):
                    half = slice(hl * HD, (hl + 1) * HD)
                    order(dve.tensor_scalar(qa[0:HD, hl, :],
                                            FX[half, bass.ds(i, 1), 0:TP].rearrange("p o n -> p (o n)"),
                                            SCALE, None, ALU.mult))
                    ins = dve.tensor_copy(ka[0:HD, hl, :],
                                          FX[half, bass.ds(i + HP, 1), 0:TP].rearrange("p o n -> p (o n)"))
                    ins.then_inc(qk_staged, 1)
                maxes(0)
                for j in range(N_IT):
                    if j + 1 < N_IT:
                        maxes(j + 1)
                    blocks(j)
                    if j:
                        output(j - 1)
                output(N_IT - 1)
                order.leave(HP)

            dve.wait_ge(ot_read, NC)
            order(dve.memset(qbd, 0.0))
            for e in range(2):
                half = slice(e * HD, (e + 1) * HD)
                order(dve.tensor_scalar(qbd[half, :, :, e], FX[half, 0:HP, TP:TS], SCALE, None, ALU.mult))
            order(dve.tensor_tensor(qkbd, qbd, FX[:, HP:2 * HP, TP:TS].unsqueeze(3)
                                    .to_broadcast([P, HP, DEC, 2]), ALU.mult))
            dve.tensor_tensor(lfd[0:NH], lfT[0:NH, TP:TS].unsqueeze(2).to_broadcast([NH, DEC, NH]),
                              ident[0:NH, 0:NH].unsqueeze(1).to_broadcast([NH, DEC, NH]), ALU.mult)\
               .then_inc(da_step, 1)
            dve.wait_ge(da_ready, 1)
            order(dve.tensor_copy(da_bias.rearrange("p b g h -> p (b g h)"), PS[:, 7, :]))
            dve.wait_ge(kp_used, DEC)
            flat_s = da_s.rearrange("p b g h -> p (b g h)")
            order(dve.tensor_tensor(flat_s, PS[:, 6, :], da_bias.rearrange("p b g h -> p (b g h)"), ALU.add))
            dve.tensor_reduce(da_mx.rearrange("p (b h) -> p b h", b=DEC), da_s.rearrange("p b g h -> p b h g"),
                              AX.X, ALU.max).then_inc(da_step, 1)
            dve.wait_ge(da_ready, 3)
            order(dve.tensor_reduce(da_c1[0:DEC * NH], PS[0:DEC * NH, 4, 0:P], AX.X, ALU.max))
            dve.tensor_scalar(da_dg[0:DEC * NH], ident[0:DEC * NH, 0:DEC * NH], da_c1[0:DEC * NH], None,
                              ALU.mult).then_inc(da_step, 1)
            dve.wait_ge(da_ready, 4)
            order(dve.tensor_copy(da_own, PS[:, 5, 0:DEC * NH]))
            order(dve.tensor_tensor(da_mx, PS[:, 4, 256:256 + DEC * NH], da_own, ALU.max))
            order(dve.tensor_tensor(da_po, da_own, da_mx, ALU.subtract))
            dve.tensor_tensor(da_s, da_s, da_mx.rearrange("p (b h) -> p b h", b=DEC).unsqueeze(2)
                              .to_broadcast([P, DEC, NPG, NH]), ALU.subtract).then_inc(da_step, 1)
            dve.wait_ge(da_exp, 2)
            dve.tensor_reduce(da_den.rearrange("p (b h) -> p b h", b=DEC), da_s.rearrange("p b g h -> p b h g"),
                              AX.X, ALU.add).then_inc(da_step, 1)
            dve.wait_ge(da_ready, 5)
            order(dve.tensor_tensor(da_mx, PS[:, 4, 384:384 + DEC * NH], da_po, ALU.add))
            order(dve.reciprocal(da_mx, da_mx))
            dve.wait_ge(vp_used, DEC)

            def by_pair(ap, e):
                return ap.rearrange("p (b a e) -> p a b e", b=DEC, a=HP)[e * HD:(e + 1) * HD, :, :, e]

            for e in range(2):
                half = slice(e * HD, (e + 1) * HD)
                pv = PS[half, 7, 0:2 * DEC * HP].rearrange("p (a b e) -> p a b e", a=HP, b=DEC)[:, :, :, e]
                order(dve.tensor_tensor(da_o[half], by_pair(da_po, e), FX[half, 2 * HP:3 * HP, TP:TS], ALU.mult))
                order(dve.tensor_tensor(da_o[half], da_o[half], pv, ALU.add))
                last = dve.tensor_tensor(FX[half, 0:HP, TP:TS], da_o[half], by_pair(da_mx, e), ALU.mult)
                if e == 0:
                    order(last)
            last.then_inc(da_step, 1)
            dve.sem_inc(sg_used, 2)
            with dve.Fori(0, KT) as n:
                for s in range(2):
                    dst = MG[:, bass.ds(n, 1), :].rearrange("p o n -> p (o n)") if s == 0 else gtmp
                    dve.wait_ge(sg_ready, 2 * n + (s + 1))
                    dve.wait_ge(unit_done, 2 * n + (2 * V_BR0 + s + 1))
                    dve.tensor_tensor(g3(dst), g3(SG[:, s]), grp(s), ALU.mult).then_inc(evac[s], 1)
                    dve.wait_ge(evac[s], n + (V_BR0 - PV_FILL + 1))
                    dve.sem_inc(sg_used, 1)
                dst = MG[:, bass.ds(n, 1), :].rearrange("p o n -> p (o n)")
                dve.tensor_tensor(dst, dst, gtmp, ALU.add).then_inc(mg_ready, 1)
                dve.wait_ge(mg_ready, n + 1)
            dve.wait_ge(x_back, 16)
            with dve.Fori(0, PV_OUT) as j:
                for s in range(2):
                    dst = g3(XT[:, bass.ds(2 * j + s, 1), :].rearrange("p o n -> p (o n)"))
                    dve.wait_ge(unit_done, 2 * j + (2 * V_OUT0 + s + 1))
                    dve.tensor_tensor(dst, dst, grp(s), ALU.add).then_inc(evac[s], 1)
            dve.wait_ge(evac[0], V_FF0 - PV_FILL)
            dve.wait_ge(evac[1], V_FF0 - PV_FILL)
            dve.sem_inc(xr_ready, KT)
            dve_norm(dve, 1, V_NF, order)
            dve.sem_inc(ff_ready, 2)
            with dve.Fori(0, FF_CH) as c:
                with dve.Fori(0, KT // 2) as j:
                    for s in range(2):
                        dve.wait_ge(evac[s], KT * c + j + (V_FF0 - PV_FILL + 1))
                        dve.tensor_tensor(FH[:, bass.ds(2 * j + s, 1), :].rearrange("p o n -> p (o n)"),
                                          RL[s], RL[s], ALU.mult).then_inc(ff_ready, 1)
                with dve.Fori(0, PV_OUT) as j:
                    for s in range(2):
                        dst = g3(XT[:, bass.ds(2 * j + s, 1), :].rearrange("p o n -> p (o n)"))
                        dve.wait_ge(unit_done, 2 * KT * c + 2 * j + (2 * V_FF0 + KT + s + 1))
                        dve.tensor_tensor(dst, dst, grp(s), ALU.add).then_inc(evac[s], 1)
            dve.wait_ge(evac[0], PAIRS - PV_FILL)
            dve.wait_ge(evac[1], PAIRS - PV_FILL)
            dve_norm(dve, 2, V_NL, order)
            dve.sem_inc(lastn, KT)

        @block.gpsimd
        def _(pool):
            pool.sem_inc(ch_pool.sem, 1)
            with pool.Fori(0, NC) as c:
                pool.wait_ge(ch_dve.sem, ch_dve.after(c, "mask_b1"))
                for lv in range(N_LV):
                    if lv == 2:
                        pool.wait_ge(ch_dve.sem, ch_dve.after(c, "xt_init"))
                    if lv > 2:
                        pool.wait_ge(ch_pe.sem, ch_pe.after(c, f"t1_{lv - 2}_1"))
                    mask = cst[0:C, C_LV + lv * C:C_LV + (lv + 1) * C].unsqueeze(1).to_broadcast([C, NH, C])
                    ch_pool.done(pool.tensor_tensor(Bm[lv % 2][0:C], MB[0:C, :, 0], mask, ALU.mult), f"bm_{lv}")


def _tiles(w):
    k, n = w.shape
    return w.reshape(k // P, P, n // P, P).transpose(2, 1, 0, 3).reshape(n // P, P, k)


def _constants():
    import numpy as np
    z = np.zeros((P, C_ALL), np.float32)
    i, j, t = np.arange(P)[:, None], np.arange(P)[None], np.arange(C)[None]
    z[:, C_ID:C_ID + P] = i == j
    z[:, C_ONE:C_ONE + P] = 1
    z[:, C_BLK:C_BLK + P] = i // HD == j // HD
    z[:, C_SUF:C_SUF + P] = i > j
    z[:, C_AM:C_AM + C] = np.where(t <= i, 0, -1e30)
    z[:, C_CM:C_CM + C] = i < t
    z[:, C_CM + C:C_CM + 2 * C] = i <= t
    for level in range(N_LV):
        n = 1 << level
        z[:, C_LV + level * C:C_LV + (level + 1) * C] = (i // n % 2 == 0) & (t // n == i // n + 1)
    return z


def lay_out(inp):
    import numpy as np
    f = np.float32
    x = np.concatenate([inp["meta_tokens"], inp["x_prompt"][0], inp["x_sample"][:, 0],
                        np.zeros((TT - TS, D), f)])
    xt = x.T.reshape(KT, P, TT).transpose(1, 0, 2)
    w = inp["w_in"][0]
    n_rw, n_fox = RW_T * P, 3 * NH * HD
    w_rw, w_fox = w[:, :n_rw], w[:, n_rw:n_rw + n_fox]
    w_f, w_g = w[:, n_rw + n_fox:n_rw + n_fox + NH], w[:, n_rw + n_fox + NH:]
    gr, gf = _tiles(w_g[:, :D]), _tiles(w_g[:, D:])
    pad = np.zeros((KT, P, D - NH * HD), f)
    br = np.concatenate([_tiles(inp["w_br_rwkv"][0]), pad], 2)
    bf = np.concatenate([_tiles(inp["w_br_fox"][0]), pad], 2)
    gates = np.stack([gr, gf], 1).reshape(2 * KT, P, D)
    branches = np.stack([br, bf], 1).reshape(2 * KT, P, D)
    up = _tiles(inp["w_ffn_up"][0])
    ff = []
    for c in range(FF_CH):
        ff += [up[c * KT:(c + 1) * KT], _tiles(inp["w_ffn_down"][0][c * D:(c + 1) * D])]
    wu = np.concatenate([_tiles(w_rw), _tiles(w_fox), gates, branches, _tiles(inp["w_out"][0])] + ff)

    def cols(v):
        return v.reshape(-1, P).T

    bfg = np.zeros((P, 1), f)
    bfg[:NH, 0] = inp["b_forget"][0]
    par = np.concatenate([cols(inp["norm_mix"][0]), cols(inp["norm_ffn"][0]), cols(inp["norm_final"]),
                          cols(inp["mu_shift"][0]), cols(inp["w0"][0]), cols(inp["a0"][0]), cols(inp["k_k"][0]),
                          cols(inp["k_a"][0]), cols(inp["r_k"][0]), cols(inp["ln_x_w"][0]),
                          cols(inp["ln_x_b"][0]), np.full((P, 1), 1e-6, f), np.full((P, 1), 64e-5, f), bfg,
                          np.zeros((P, 1), f)], 1)
    kp = inp["cache_k"][0].reshape(POOL, PAGE, HP, P).transpose(0, 3, 2, 1)
    vp = np.concatenate([inp["cache_v"][0].reshape(POOL, PAGE, NH * HD), inp["cache_logf"][0]], 2)
    st = inp["state_wkv"][0].reshape(2, DEC // 2, NH, HD, HD).transpose(0, 3, 1, 2, 4).reshape(P, -1)
    sh = inp["state_shift"][0].reshape(DEC, RW_T, P).transpose(2, 1, 0)
    return {"xt": xt, "wu": wu, "cst": _constants(), "par": par,
            "wf": w_f.reshape(KT, P, NH).transpose(1, 0, 2),
            "wl": np.concatenate([inp["w_decay_up"][0], inp["w_a_up"][0]]), "wg": inp["w_g_up"][0],
            "page_table": inp["page_table"].reshape(1, -1), "kp": kp, "vp": vp, "st": st, "sh": sh}


_OUTS = {"o_y": (P, KT, TT), "o_kv": (P, 2 * HP, TT), "o_lf": (NH, TT), "o_sh": (P, RW_T, DEC + 1),
         "o_sp": (P, HP, HD), "o_ss": (P, DEC // 2 * NH * HD)}


def give_back(o):
    y = o["o_y"].transpose(2, 1, 0).reshape(TT, D)
    kv = o["o_kv"].transpose(2, 1, 0).reshape(TT, 2, NH, HD)
    lf = o["o_lf"].T
    sh = o["o_sh"].transpose(2, 1, 0).reshape(DEC + 1, RW_T * P)
    sp = o["o_sp"].reshape(2, HD, HP, HD).transpose(2, 0, 3, 1).reshape(NH, HD, HD)
    ss = o["o_ss"].reshape(2, HD, DEC // 2, NH, HD).transpose(0, 2, 3, 1, 4).reshape(DEC, NH, HD, HD)
    return (y[T_META:TP][None], y[TP:TS][:, None], sh[0:1][None], sp[None, None],
            kv[:TP, 0][None, None], kv[:TP, 1][None, None], lf[:TP][None, None], sh[1:][None], ss[None],
            kv[TP:TS, 0][None, :, None], kv[TP:TS, 1][None, :, None], lf[TP:TS][None, :, None])


def kernel(**inputs):
    import numpy as np
    import concourse.bacc as bacc
    from concourse.bass_utils import run_bass_kernel_spmd

    nc = bacc.Bacc("TRN2", target_bir_lowering=False, num_devices=1, dynamic_dma_scratch_size=1024)
    arrays, aps = {}, {}
    for name, a in lay_out({k: np.asarray(v) for k, v in inputs.items()}).items():
        a = np.ascontiguousarray(a)
        arrays["in_" + name] = a
        aps[name] = nc.dram_tensor("in_" + name, a.shape, mybir.dt.from_np(a.dtype), kind="ExternalInput").ap()
    for name, shape in _OUTS.items():
        aps[name] = nc.dram_tensor("out_" + name, shape, F32, kind="ExternalOutput").ap()
    build(nc, aps)
    r = run_bass_kernel_spmd(nc, [arrays], core_ids=[0])
    got = {name: np.asarray(r.results[0]["out_" + name]) for name in _OUTS}
    return tuple(np.ascontiguousarray(a) for a in give_back(got))
```

```python
from contextlib import ExitStack

import numpy as np

import concourse.bass as bass
from concourse import mybir
from concourse.alu_op_type import AluOpType as ALU

F32 = mybir.dt.float32
F32R = mybir.dt.float32r
I32 = mybir.dt.int32
ACT = mybir.ActivationFunctionType
AX = mybir.AxisListType

P = 128
D = 1024
KT = D // P
T_META, SEQ, DEC = 16, 1024, 8
TP = T_META + SEQ
TS = TP + DEC
TT = 1050
NG, G = 3, TT // 3
C = 104
NC = TP // C
HD = 64
NH = 8
HP = NH // 2
PAGE, NPG, POOL = 128, 8, 80
VW = NH * HD + NH
FF_CH = 4
RW_T = 14
SCALE = HD ** -0.5
E_HALF = 0.6065306597126334

C_ID, C_ONE, C_BLK, C_SUF = 0, 128, 256, 384
C_AM = 512
C_CM = C_AM + C
C_LV = C_CM + 2 * C
N_LV = 7
C_ALL = C_LV + N_LV * C
V_NM, V_NF, V_NL, V_MU, V_W0, V_A0, V_KK, V_KA, V_RK, V_LW, V_LB, V_EPS, V_GEPS, V_BF = (
    0, 8, 16, 24, 38, 42, 46, 50, 54, 58, 62, 66, 67, 68)
V_ALL = 70

PV_RW, PV_FOX, PV_GATE, PV_BR, PV_OUT, PV_FF = 7, 6, 8, 8, 4, 32
V_FOX0 = PV_RW
V_GATE0 = V_FOX0 + PV_FOX
V_BR0 = V_GATE0 + PV_GATE
V_OUT0 = V_BR0 + PV_BR
V_FF0 = V_OUT0 + PV_OUT
PAIRS = V_FF0 + PV_FF
PV_FILL = PV_FOX + PV_GATE
C_FOX = PV_FOX

SB_COLS = 56904


class Order:

    def __init__(self, eng, sem):
        self.eng, self.sem, self.base, self.n = eng, sem, 0, 0

    def __call__(self, ins):
        self.n += 1
        ins.then_inc(self.sem, 1)
        self.eng.wait_ge(self.sem, self.base + self.n)

    def enter(self, i, per, first=0):
        self.outer, self.per = self.base + self.n, per
        self.base, self.n = i * per + (self.outer - first * per), 0

    def leave(self, count):
        assert self.n == self.per, ("steps in the loop's body", self.n, self.per)
        self.base, self.n = self.outer + count * self.per, 0


class Steps:

    def __init__(self, sem, names):
        self.sem, self.names, self.next = sem, names, 0

    def after(self, c, name):
        return c * len(self.names) + (self.names.index(name) + 2)

    def before(self, c):
        return c * len(self.names) + 1

    def done(self, ins, name):
        assert self.names[self.next] == name, (self.names[self.next], name)
        self.next = (self.next + 1) % len(self.names)
        ins.then_inc(self.sem, 1)


def build(nc, A):
    with ExitStack() as ctx:
        def sem(name):
            return ctx.enter_context(nc.semaphore(name))

        ctx.enter_context(nc.sbuf_tensor("sb", [P, SB_COLS], F32))
        sb_at = nc.sbuf_base - 4 * SB_COLS
        PT_SB = ctx.enter_context(nc.sbuf_tensor("page_ids", [1, DEC * NPG], I32))
        PS = ctx.enter_context(nc.psum_tensor("ps", [P, 8, 512], F32))
        chunk_dram = nc.dram_tensor("chunk_dram", [P, NC, 6, HP, C], F32, kind="Internal").ap()
        bg_dram = nc.dram_tensor("bg_dram", [P, 2 * HP, TT], F32, kind="Internal").ap()
        gate_dram = nc.dram_tensor("gate_dram", [2 * KT, P, TT], F32, kind="Internal").ap()
        cneg_dram = nc.dram_tensor("cneg_dram", [NH, TP], F32, kind="Internal").ap()
        samp_dram = nc.dram_tensor("samp_dram", [6, DEC, NH * HD], F32, kind="Internal").ap()
        ysamp_dram = nc.dram_tensor("ysamp_dram", [DEC, NH, HD], F32, kind="Internal").ap()

        def own(name, at, *dims, dtype=F32):
            assert at + int(np.prod(dims)) <= SB_COLS
            return nc.alloc_sbuf_tensor_at(name, [P, *dims], dtype, offset=sb_at + 4 * at).ap()

        placed = 0

        def keep_tensor(name, *dims):
            nonlocal placed
            at, placed = placed, placed + -(-int(np.prod(dims)) // 8) * 8
            return own(name, at, *dims)

        cst = keep_tensor("constants", C_ALL)
        W = keep_tensor("weights", 2, D)
        wl = keep_tensor("lora_weights", 512)
        wg = keep_tensor("gate_weights", 512)
        wf = keep_tensor("forget_weights", KT, NH)
        par = keep_tensor("params", V_ALL)
        lfT = keep_tensor("log_forget", TT)
        ht_at = placed
        HT = keep_tensor("normed", KT, TT)
        FX = keep_tensor("fox", 12, TT)
        ar = placed
        rw_end = ar + -(-RW_T * TT // 8) * 8
        arena = own("arena", ar, SB_COLS - ar)

        def view(at, *dims):
            n = int(np.prod(dims))
            assert ar <= at and at + n <= SB_COLS, (at, n)
            v = arena[:, at - ar:at - ar + n]
            if len(dims) == 2:
                v = v.rearrange("p (a b) -> p a b", a=dims[0])
            if len(dims) == 3:
                v = v.rearrange("p (a b c) -> p a b c", a=dims[0], b=dims[1])
            if len(dims) == 4:
                v = v.rearrange("p (a b c d) -> p a b c d", a=dims[0], b=dims[1], c=dims[2])
            return v

        class Region:

            def __init__(self, at, n):
                self.at, self.end = at, at + n

            def take(self, *dims):
                n = 1
                for d in dims:
                    n *= d
                v = view(self.at, *dims)
                self.at += n
                assert self.at <= self.end, (self.at, self.end)
                return v

        XT = view(ar, KT, TT)
        RW = view(ar, RW_T, TT)
        YT = view(SB_COLS - HP * TT, HP, TT)
        d_col = view(SB_COLS - HP * TT - 6 * HP * DEC, 6, HP, DEC)
        ar_end = SB_COLS - HP * TT - 6 * HP * DEC

        ident = cst[:, C_ID:C_ID + P]
        ones = cst[:, C_ONE:C_ONE + P]
        blk = cst[:, C_BLK:C_BLK + P]
        suf = cst[:, C_SUF:C_SUF + P]

        def grp(slot):
            return PS[:, 3 * slot:3 * slot + 3, 0:G]

        def g3(ap):
            return ap.rearrange("p (g n) -> p g n", g=NG)

        consts_in, x_in = sem("consts_in"), sem("x_in")
        w_in = [sem("w_in0"), sem("w_in1")]
        unit_done = sem("unit_done")
        evac = [sem("evac0"), sem("evac1")]
        act_order, dve_order = sem("act_order"), sem("dve_order")
        out_stored, kv_stored, sh_stored = sem("out_stored"), sem("kv_stored"), sem("sh_stored")
        sp_stored = sem("sp_stored")
        sq_ready, sq_added = sem("sq_ready"), sem("sq_added")
        ssum_ready, rms_ready, h_ready = sem("ssum_ready"), sem("rms_ready"), sem("h_ready")
        sub_done, sub_read = sem("sub_done"), sem("sub_read")

        w_hi, w_split = [sem("w_hi0"), sem("w_hi1")], [sem("w_split0"), sem("w_split1")]
        h_hi, h_raw = sem("h_hi"), sem("h_raw")

        norms = []
        for n in range(2):
            norms.append((own(f"squares{n}", ar + KT * TT, 2, TT), view(ar + (KT + 2) * TT, TT),
                          view(ar + (KT + 3) * TT, TT)))
        norms.append((own("squares2", ht_at + 2 * KT * TT, 2, TT), FX[:, 10, :], FX[:, 11, :]))

        HS = own("h_split", ht_at, 2, KT, TT, dtype=F32R)
        FS = own("ff_split", ar + KT * TT, 2, KT, TT, dtype=F32R)
        WS = own("w_split", ar + 3 * KT * TT, 2, 2, D, dtype=F32R)

        def pe_unit(pe, v, s, x, nk=KT, late=True):
            pe.wait_ge(w_in[s], 16 * (v + 1))
            if not isinstance(v, int) or v > 0:
                pe.wait_ge(evac[s], v - PV_FILL if late else v)
            for k in range(nk):
                for g in range(NG):
                    last = pe.matmul(PS[:, 3 * s + g, 0:G], W[:, s, k * P:(k + 1) * P],
                                     x[:, k, g * G:(g + 1) * G], start=(k == 0), stop=(k == nk - 1))
            last.then_inc(unit_done, 1)

        H0 = [own("h0_high", ht_at + KT * TT, KT, TT, dtype=F32R), own("h0_low", rw_end, KT, TT, dtype=F32R)]
        WS0 = own("w0_split", ht_at + 2 * KT * TT, 2, 2, D, dtype=F32R)
        h0_hi, h0_ready = sem("h0_hi"), sem("h0_ready")
        RWKV, FFN = (WS0, 0, 0), (WS, PV_RW - V_FF0, PV_FILL)

        def halves(x):
            return x[:, 0], x[:, 1]

        def pe_unit_split(pe, v, s, x, ready=None, of=FFN):
            ws, shift, filled = of
            pe.wait_ge(w_split[s], v + (shift + 1))
            if not isinstance(v, int) or v > 0:
                pe.wait_ge(evac[s], v - filled if filled else v)
            for k in range(KT):
                if ready is not None:
                    ready(k)
                for wh, xh in ((0, 0), (0, 1), (1, 0)):
                    for g in range(NG):
                        last = pe.matmul(PS[:, 3 * s + g, 0:G], ws[:, s, wh, k * P:(k + 1) * P],
                                         x[xh][:, k, g * G:(g + 1) * G], start=(k == 0 and wh + xh == 0),
                                         stop=(k == KT - 1 and wh == 1))
            last.then_inc(unit_done, 1)

        def act_split(act, v, s, of=FFN):
            act.wait_ge(w_in[s], 16 * (v + 1))
            if not isinstance(v, int) or v > 0:
                act.wait_ge(unit_done, 2 * v + s - 1)
            act.copy(of[0][:, s, 0], W[:, s]).then_inc(w_hi[s], 1)

        def dve_split(dve, v, s, of=FFN):
            dve.wait_ge(w_hi[s], v + (of[1] + 1))
            dve.tensor_tensor(of[0][:, s, 1], W[:, s], of[0][:, s, 0], ALU.subtract).then_inc(w_split[s], 1)

        def pe_norm(pe, n):
            sqsum = norms[n][1]
            pe.wait_ge(sq_added, KT * (n + 1))
            for g in range(NG):
                last = pe.matmul(PS[:, g, 0:G], ones, sqsum[:, g * G:(g + 1) * G], start=True, stop=True)
            last.then_inc(ssum_ready, 1)

        def act_square(act, n, k, slot):
            if n or k >= 2:
                act.wait_ge(sq_added, k + (KT * n - 1))
            act.activation(norms[n][0][:, slot],
                           XT[:, k, :] if isinstance(k, int) else
                           XT[:, bass.ds(k, 1), :].rearrange("p o n -> p (o n)"), ACT.Square)\
               .then_inc(sq_ready, 1)

        def act_rms(act, n):
            act.wait_ge(ssum_ready, n + 1)
            act.activation(g3(norms[n][2]), grp(0), ACT.Sqrt, scale=1.0 / D,
                           bias=par[:, V_EPS:V_EPS + 1]).then_inc(rms_ready, 1)

        def dve_add_square(dve, n, k, slot):
            sq, sqsum, rstd = norms[n]
            dve.wait_ge(sq_ready, k + (KT * n + 1))
            if n or k:
                dve.wait_ge(sq_added, k + KT * n)
            dve.tensor_tensor(sqsum, sqsum, sq[:, slot], ALU.add).then_inc(sq_added, 1)

        def dve_rms(dve, n, order):
            dve.wait_ge(rms_ready, n + 1)
            order(dve.reciprocal(norms[n][2], norms[n][2]))

        def normed(dve, n, k, gain, dst):
            return dve.scalar_tensor_tensor(dst, XT[:, k, :], par[:, gain + k:gain + k + 1], norms[n][2],
                                            ALU.mult, ALU.mult)

        class Filler:

            def __init__(self, pe, v):
                self.pe, self.v = pe, v
                self.left = [(s, g, k) for s in range(2) for g in range(NG) for k in range(KT)]

            def run(self, n=None):
                for s, g, k in self.left[:n]:
                    m = NG * s + g
                    if k == 0:
                        if g == 0:
                            self.pe.wait_ge(w_in[s], 16 * self.v + 16)
                        self.pe.wait_ge(sub_read, 2 * NG * self.v + (m + 1 - 2 * NG * V_FOX0))
                    last = self.pe.matmul(PS[:, 6 + m % 2, 0:G], W[:, s, k * P:(k + 1) * P],
                                          HT[:, k, g * G:(g + 1) * G], start=(k == 0), stop=(k == KT - 1))
                    if k == KT - 1:
                        last.then_inc(unit_done if g == NG - 1 else sub_done, 1)
                self.left = self.left[n:] if n is not None else []

        def act_fill(act, v, m, dst):
            s, g = divmod(m, NG)
            if g == NG - 1:
                act.wait_ge(unit_done, 2 * v + (s + 1))
            else:
                act.wait_ge(sub_done, 4 * v + (2 * s + g + 1 - 4 * V_FOX0))
            act.copy(dst, PS[:, 6 + m % 2, 0:G]).then_inc(sub_read, 1)

        f_ready, f_read, lf_ready = sem("f_ready"), sem("f_read"), sem("lf_ready")
        cneg_stored, cneg_in = sem("cneg_stored"), [sem("cneg_in0"), sem("cneg_in1")]
        vt_ready, vt_read = sem("vt_ready"), sem("vt_read")
        qk_free, qk_staged = sem("qk_free"), sem("qk_staged")
        s_done, max_ready, p_ready = sem("s_done"), sem("max_ready"), sem("p_ready")
        pt_done, pt_read = sem("pt_done"), [sem("pt_read0"), sem("pt_read1")]
        pv_done, o_read = sem("pv_done"), sem("o_read")
        dg_ready, v_staged = sem("dg_ready"), sem("v_staged")

        r_att = Region(ar, ar_end - ar)
        qa = r_att.take(2, TP)
        ka = r_att.take(2, TP)
        Pm = r_att.take(2, TP)
        PTm = r_att.take(2, NC, C)
        vst = r_att.take(NC, P)
        dg = r_att.take(2, C)
        rowmax = r_att.take(2)
        rowsum = r_att.take(4)
        rowinv = r_att.take(2)
        vnat = view(ar_end - NC * 512, NC, 512)
        r_f = Region(ar_end - NC * 512 - 2 * TT, 2 * TT)
        f_neg, f_t = r_f.take(TT), r_f.take(TT)
        f_c, f_ones = f_neg[:, 0:TP], f_t[:, 0:TP]
        tiles = [(hl, qt) for hl in range(2) for qt in range(NC)]
        N_IT = len(tiles)
        groups = [-(-(qt + 1) // 4) for _, qt in tiles]
        N_GR = sum(groups)
        assert N_GR % 2 == 0
        gr_before = [sum(groups[:j]) for j in range(N_IT)]

        ids_in = sem("ids_in")
        kp_in = [sem("kp_in0"), sem("kp_in1")]
        vp_in = [sem("vp_in0"), sem("vp_in1")]
        lfp_in = sem("lfp_in")
        da_ready = sem("da_ready")
        da_step = sem("da_step")
        da_exp = sem("da_exp")
        kp_used, vp_used = sem("kp_used"), sem("vp_used")
        r_da = Region(r_att.at, ar_end - NC * 512 - r_att.at)
        slots = HT.rearrange("p a b -> p (a b)")
        Kp = [slots[:, s * NPG * VW:s * NPG * VW + NPG * HP * PAGE]
              .rearrange("p (g h t) -> p g h t", g=NPG, h=HP) for s in range(2)]
        Vp = [slots[:, s * NPG * VW:(s + 1) * NPG * VW].rearrange("p (g n) -> p g n", g=NPG) for s in range(2)]
        DA_COL = P
        DA_AT = (4, 8, 12, 16)
        NDA = len(DA_AT)
        da_pv = r_da.take(HP, DEC, 2)
        lfp = r_da.take(DEC, NPG, NH)
        qbd = r_da.take(HP, DEC, 2)
        qkbd = r_da.take(HP, DEC, 2)
        lfd = r_da.take(DEC, NH)
        da_bias = r_da.take(DEC, NPG, NH)
        da_s = r_da.take(DEC, NPG, NH)
        da_own = r_da.take(DEC * NH)
        da_mx = r_da.take(DEC * NH)
        da_c1 = r_da.take(1)
        da_dg = r_da.take(DEC * NH)
        da_po = r_da.take(DEC * NH)
        da_den = r_da.take(DEC * NH)
        da_o = r_da.take(HP, DEC)

        mixed, mix_order = sem("mixed"), sem("mix_order")
        lora_in = sem("lora_in")
        pp, pa, pd = sem("prep_pe"), sem("prep_act"), sem("prep_dve")
        LW, KK, BB = FX[:, 0:HP, :], FX[:, HP:2 * HP, :], FX[:, 2 * HP:3 * HP, :]
        r_rw = Region(rw_end, ar_end - rw_end)
        BG = r_rw.take(2 * HP, TT)
        BON, GT = BG[:, 0:HP], BG[:, HP:2 * HP]
        sh_in = r_rw.take(RW_T, DEC)
        sh_out = r_rw.take(RW_T, DEC + 1)
        mtmp = r_rw.take(TT)
        ptmp = [YT[:, 0, :], YT[:, 1, :]]

        d_col_ready = sem("d_col_ready")
        prep_stored, bg_stored, bg_back = sem("prep_stored"), sem("bg_stored"), sem("bg_back")
        st_in, g_stored, g_back = sem("st_in"), [sem("g_stored0"), sem("g_stored1")], [sem("g_back0"), sem("g_back1")]

        r_ch = Region(ar, ar_end - ar)
        CH = r_ch.take(6, HP, C)
        SGs = r_ch.take(2, TT)
        Lc, Lm = r_ch.take(HP, C), r_ch.take(HP, C)
        E1, E2, E3 = r_ch.take(HP, C), r_ch.take(HP, C), r_ch.take(HP, C)
        AR = r_ch.take(HP, 2, C)
        Kc, Bc, Vc = r_ch.take(HP, C), r_ch.take(HP, C), r_ch.take(HP, C)
        Kn, Bn, An, Vn = r_ch.take(512), r_ch.take(512), r_ch.take(512), r_ch.take(512)
        Xm, XTr = r_ch.take(NH, C), r_ch.take(NH, C)
        r_c2 = r_ch
        MK = r_c2.take(NH, 2, C)
        MB = r_c2.take(NH, 2, C)
        T1 = r_c2.take(NH, C)
        Bm = r_c2.take(NH, C), r_c2.take(NH, C)
        Zm = r_c2.take(512)
        WT = r_c2.take(HP, C)
        NU = r_c2.take(512)
        St = r_ch.take(HP, HD)
        Yc = r_c2.take(512)
        gst = r_c2.take(4, NH)

        LEVELS = range(1, N_LV)
        ch_pe = Steps(sem("ch_pe"), ["nat_k", "nat_b", "nat_a", "nat_v"]
                      + [f"prod_{m}{i}" for i in range(2) for m in "kb"] + ["z", "x_0", "x_1"]
                      + [f"{t}_{lv}_{q}" for lv in LEVELS for t in ("t1", "t2") for q in range(2)]
                      + ["wt", "u", "y", "s", "yt"])
        ch_act = Steps(sem("ch_act"), ["v", "e1", "e3", "e2", "nat_k", "nat_a", "z", "x_0", "x_1"]
                       + [f"t1_{lv}_{q}" for lv in LEVELS for q in range(2)]
                       + ["wt", "nu", "ln", "rstd"] + [f"y_{p}" for p in range(HP)])
        ch_dve = Steps(sem("ch_dve"), [f"scan_{p}" for p in range(HP)] + ["lm", "r", "k", "b", "a", "nat_b", "nat_v"]
                       + [f"mask_{m}{i}" for i in range(2) for m in "kb"] + ["xt_init"]
                       + [f"x_{lv}_{q}_{t}" for lv in LEVELS for q in range(2)
                          for t in (("x", "xt") if lv < N_LV - 1 else ("xt",))]
                       + ["sum", "mean", "state", "center", "sq", "var", "norm"])
        ch_pool = Steps(sem("ch_pool"), [f"bm_{lv}" for lv in range(N_LV)])

        ds_pe, ds_act, ds_dve = sem("ds_pe"), sem("ds_act"), sem("ds_dve")
        ds_store, ds_load = sem("ds_store"), sem("ds_load")
        ds_y, ds_yb, ds_var = sem("ds_y"), sem("ds_yb"), sem("ds_var")
        o_pe, o_done = sem("o_pe"), sem("o_done")
        r_ds = Region(ar, ar_end - ar)
        r_ds.take(6 * HP * C + 2 * TT)
        dS = r_ds.take(DEC // 2, NH, HD)
        dW, dT = r_ds.take(DEC // 2, NH, HD), r_ds.take(DEC // 2, NH, HD)
        dKK, dB, dK = (r_ds.take(DEC // 2, NH, HD) for _ in range(3))
        dR = dKK
        dV, dU = r_ds.take(DEC // 2, NH), r_ds.take(DEC // 2, NH)
        d_nat = view(r_ds.at, 6, P)
        dYn, dSQ = r_ds.take(512), r_ds.take(512)
        dst4 = r_ds.take(4, NH)
        assert r_ds.at <= ar_end - NC * 512 - 2 * TT
        BGb = view(ar_end - NC * 512 - 2 * HP * TT, 2 * HP, TT)
        assert r_da.at <= ar_end - NC * 512 - 2 * HP * TT

        sg_ready, sg_used, mg_ready = sem("sg_ready"), sem("sg_used"), sem("mg_ready")
        ff_raw, ff_hi, ff_ready, x_back = sem("ff_raw"), sem("ff_hi"), sem("ff_ready"), sem("x_back")
        MG = FX[:, HP:3 * HP, :]
        r_m = Region(ar + KT * TT, 5 * TT + 2 * TT)
        GR = r_m.take(2, TT)
        SG = r_m.take(2, TT)
        gtmp = r_m.take(TT)
        RL = [norms[2][0][:, s] for s in range(2)]

        def sflat(bank, n, c0=0):
            return PS[0:C, bank:bank + 3 if bank == 0 else bank + 2, :].rearrange("p a b -> p (a b)")[:, c0:c0 + n]

        block = ctx.enter_context(nc.Block())

        @block.sync
        def _(sp):
            def load_w(v, s, wait=True):
                if wait:
                    sp.wait_ge(unit_done, 2 * v + s - 1)
                sp.dma_start(W[:, s, :], A["wu"][bass.ds(2 * v + s, 1), :, :].rearrange("o p n -> (o p) n")
                             if not isinstance(v, int) else A["wu"][2 * v + s]).then_inc(w_in[s], 16)

            def load_pairs(v0, v1):
                with sp.Fori(v0, v1) as v:
                    load_w(v, 0)
                    load_w(v, 1)

            for n in range(4):
                sp.dma_start(XT[:, 2 * n:2 * n + 2, :], A["xt"][:, 2 * n:2 * n + 2, :]).then_inc(x_in, 16)
            sp.dma_start(cst, A["cst"]).then_inc(consts_in, 16)
            sp.dma_start(par, A["par"]).then_inc(consts_in, 16)
            load_w(0, 0, wait=False)
            load_w(0, 1, wait=False)
            sp.dma_start(wf, A["wf"]).then_inc(consts_in, 16)
            sp.dma_start(wl, A["wl"]).then_inc(consts_in, 16)
            sp.dma_start(wg, A["wg"]).then_inc(consts_in, 16)
            sp.dma_start(PT_SB[:, :], A["page_table"]).then_inc(ids_in, 16)
            sp.wait_ge(h_ready, KT)
            sp.dma_start(sh_in, A["sh"]).then_inc(lora_in, 16)
            load_pairs(1, V_FOX0 + 1)
            sp.wait_ge(mixed, RW_T)
            sp.dma_start(A["o_sh"], sh_out).then_inc(sh_stored, 16)

            def keep_tile(kind, p, src):
                sp.dma_start(chunk_dram[:, :, kind, p, :], src[:, p, 0:TP].rearrange("p (c t) -> p c t", c=NC))\
                  .then_inc(prep_stored, 16)

            for p in range(HP):
                sp.wait_ge(pd, 3 * p + 3)
                for kind, src in enumerate((RW[:, 0:HP], RW[:, HP:2 * HP], RW[:, 2 * HP:3 * HP], LW, KK, BB)):
                    keep_tile(kind, p, src)
            sp.wait_ge(pa, 2 + 4 * HP)
            sp.dma_start(bg_dram, BG).then_inc(bg_stored, 16)

            def load_chunk(c):
                src = chunk_dram[:, c] if isinstance(c, int) else chunk_dram[:, bass.ds(c, 1)]\
                    .rearrange("p o a b t -> p (o a) b t")
                sp.dma_start(CH, src).then_inc(st_in, 16)

            def sp_chunk(c, gates, more):
                if more:
                    sp.wait_ge(ch_dve.sem, ch_dve.after(c, "a"))
                    sp.wait_ge(ch_act.sem, ch_act.after(c, "v"))
                    load_chunk(c + 1)
                for s in range(2):
                    if gates:
                        sp_gate(c - C_FOX, s)
                    load_w(c + (V_FOX0 + 1), s)

            def sp_gate(x, s):
                sp.wait_ge(sub_read, 2 * NG * x + (2 * NG * PV_FOX + NG * s + NG + 2))
                dst = gate_dram[2 * x + s] if isinstance(x, int) else gate_dram[bass.ds(2 * x + s, 1)]\
                    .rearrange("o p n -> (o p) n")
                sp.dma_start(dst, SGs[:, s]).then_inc(g_stored[s], 16)

            sp.wait_ge(prep_stored, 16 * 6 * HP)
            sp.wait_ge(bg_stored, 16)
            sp.wait_ge(sh_stored, 16)
            sp.wait_ge(d_col_ready, 1)
            load_chunk(0)
            with sp.Fori(0, C_FOX) as c:
                sp_chunk(c, False, True)
            with sp.Fori(C_FOX, NC - 1) as c:
                sp_chunk(c, True, True)
            sp_chunk(NC - 1, True, False)

            sp.wait_ge(ch_pe.sem, ch_pe.before(NC))
            sp.wait_ge(ch_dve.sem, ch_dve.before(NC))
            sp.dma_start(A["o_sp"], St).then_inc(sp_stored, 16)
            sp.dma_start(dS.rearrange("p b h k -> p (b h k)"), A["st"]).then_inc(ds_load, 16)
            sp.wait_ge(ds_act, 1)
            for p in range(HP):
                sp.dma_start(samp_dram[:, :, p * P:(p + 1) * P].rearrange("k b c -> b k c"),
                             d_nat[p * DEC:(p + 1) * DEC]).then_inc(ds_store, 16)
            sp.wait_ge(ds_store, 16 * HP)

            def spread(dst, kind):
                for e in range(2):
                    sp.dma_start(dst[e * HD:(e + 1) * HD].rearrange("p b h k -> p (b h k)"),
                                 samp_dram[kind, e * (DEC // 2):(e + 1) * (DEC // 2), :]
                                 .rearrange("b n -> (b n)").partition_broadcast(HD)).then_inc(ds_load, 16)

            for dst, kind in ((dKK, 1), (dW, 0), (dB, 2), (dK, 3)):
                spread(dst, kind)
            for e in range(2):
                sp.dma_start(dV[e * HD:(e + 1) * HD],
                             samp_dram[5, e * (DEC // 2):(e + 1) * (DEC // 2), :]
                             .rearrange("b (h v) -> v b h", h=NH),
                             allow_slow_non_contiguous=True).then_inc(ds_load, 16)
            x = NC - C_FOX
            for s in range(2):
                sp_gate(x, s)
                load_w(x + (V_GATE0 + 1), s)
            sp.wait_ge(ds_dve, 1)
            spread(dR, 4)
            sp.wait_ge(ds_dve, 2)
            sp.dma_start(A["o_ss"], dS.rearrange("p b h k -> p (b h k)")).then_inc(out_stored, 16)
            sp.wait_ge(ds_dve, 3)
            for e in range(2):
                sp.dma_start(ysamp_dram[e * (DEC // 2):(e + 1) * (DEC // 2)].rearrange("b h v -> v b h"),
                             dU[e * HD:(e + 1) * HD], allow_slow_non_contiguous=True).then_inc(ds_y, 16)
            sp.wait_ge(ds_y, 32)
            sp.dma_start(dYn[0:DEC], ysamp_dram.rearrange("b h v -> b (h v)")).then_inc(ds_yb, 16)
            with sp.Fori(NC - C_FOX + 1, PV_GATE) as x:
                for s in range(2):
                    sp_gate(x, s)
                    load_w(x + (V_GATE0 + 1), s)
            sp.wait_ge(lf_ready, 1)
            sp.dma_start(cneg_dram, f_c[0:NH, :]).then_inc(cneg_stored, 16)
            sp.dma_start(A["o_lf"], lfT[0:NH, :]).then_inc(out_stored, 16)
            sp.dma_start(A["o_kv"], FX[:, HP:3 * HP, :]).then_inc(kv_stored, 16)
            sp.wait_ge(cneg_stored, 16)
            sp.wait_ge(ids_in, 16)

            def page_id(n, pg):
                return sp.value_load(PT_SB[0:1, bass.ds(n * NPG + pg, 1)], min_val=0, max_val=POOL - 1)

            def load_keys(n, s):
                for pg in range(NPG):
                    page = page_id(n, pg)
                    sp.dma_start(Kp[s][:, pg, :, :],
                                 A["kp"][bass.ds(page, 1), :, :, :].rearrange("o p h t -> (o p) h t"))\
                      .then_inc(kp_in[s], 16)
                    sp.dma_start(lfp[:, n, pg, :],
                                 A["vp"][bass.ds(page, 1), :, NH * HD:VW].rearrange("o p h -> (o p) h"))\
                      .then_inc(lfp_in, 16)

            def load_values(n, s):
                for pg in range(NPG):
                    page = page_id(n, pg)
                    sp.dma_start(Vp[s][:, pg, :],
                                 A["vp"][bass.ds(page, 1), :, :].rearrange("o p n -> (o p) n"))\
                      .then_inc(vp_in[s], 16)

            def load_round(load, used, n):
                for s in range(2):
                    sp.wait_ge(used, n + s + 1)
                    load(n + s, s)

            def load_cneg(i):
                sp.wait_ge(qk_free, i + 1)
                for hl in range(2):
                    sp.dma_start(ka[HD:HD + 1, hl, :], cneg_dram[2 * i + hl:2 * i + hl + 1, :])\
                      .then_inc(cneg_in[hl], 16)

            for s in range(2):
                sp.wait_ge(g_stored[s], 16 * (PV_GATE + 1))
            load_cneg(0)
            load_round(load_keys, kp_used, 0)
            sp.wait_ge(ds_dve, 4)
            sp.wait_ge(out_stored, 16 * 2)
            sp.wait_ge(ds_pe, 2)
            sp.dma_start(BGb, bg_dram).then_inc(bg_back, 16)
            for i in range(HP):
                if i:
                    load_cneg(i)
                load, used = (load_keys, kp_used) if i < HP // 2 else (load_values, vp_used)
                load_round(load, used, NDA * (i % 2) + 2)
                if i % 2 == 0:
                    load_round(load, used, NDA)
                elif i + 1 < HP:
                    sp.wait_ge(kp_used, DEC + 2)
                    load_round(load_values, vp_used, 0)
            sp.wait_ge(da_step, 6)
            sp.wait_ge(o_done, 2)
            sp.dma_start(XT, A["xt"]).then_inc(x_back, 16)

            def gates_back(n):
                for s in range(2):
                    src = gate_dram[2 * n + s] if isinstance(n, int) else gate_dram[bass.ds(2 * n + s, 1)]\
                        .rearrange("o p n -> (o p) n")
                    sp.dma_start(GR[:, s], src).then_inc(g_back[s], 16)

            gates_back(0)
            with sp.Fori(1, KT) as n:
                sp.wait_ge(sg_ready, 2 * n)
                gates_back(n)
                load_w(n + V_BR0, 0)
                load_w(n + V_BR0, 1)
            load_pairs(V_OUT0, V_FF0 + 1)
            with sp.Fori(V_FF0 + 1, PAIRS) as v:
                for s in range(2):
                    sp.wait_ge(w_split[s], v + (PV_RW - V_FF0))
                    load_w(v, s, wait=False)
            for k in range(KT):
                sp.wait_ge(h_ready, 2 * KT + k + 1)
                sp.dma_start(A["o_y"][:, k, :], HT[:, k, :]).then_inc(out_stored, 16)
            sp.wait_ge(kv_stored, 16)
            sp.wait_ge(sp_stored, 16)
            sp.wait_ge(out_stored, 16 * (2 + KT))

        @block.tensor
        def _(pe):
            pe.wait_ge(consts_in, 80)
            pe_norm(pe, 0)
            pe.wait_ge(rms_ready, 1)
            pe_unit_split(pe, 0, 0, H0, lambda k: pe.wait_ge(h0_ready, k + 1), of=RWKV)
            pe_unit_split(pe, 0, 1, H0, of=RWKV)
            with pe.Fori(1, PV_RW) as v:
                pe_unit_split(pe, v, 0, H0, of=RWKV)
                pe_unit_split(pe, v, 1, H0, of=RWKV)
            pe.wait_ge(evac[0], PV_RW)
            pe.wait_ge(evac[1], PV_RW)
            pe.wait_ge(pa, 2)
            for p in range(HP):
                for m in range(2):
                    if p:
                        pe.wait_ge(pa, 2 + 2 * p - 1 + m)
                    rows = slice(m * HD, (m + 1) * HD)
                    for g in range(NG):
                        last = pe.matmul(PS[:, 3 * m + g, 0:G], wl[rows, p * P:(p + 1) * P],
                                         RW[rows, 12, g * G:(g + 1) * G], start=True, stop=True)
                    last.then_inc(pp, 1)
            for p in range(HP):
                for m in range(2):
                    if p == 0:
                        pe.wait_ge(pa, 10)
                    pe.wait_ge(pd, 3 * p + 1 + m)
                    if p and m == 0:
                        pe.wait_ge(pa, 10 + p)
                    if p and m == 1:
                        pe.wait_ge(pd, 3 * p)
                    for g in range(NG):
                        last = pe.matmul(PS[:, 3 * m + g, 0:G], blk, ptmp[m][:, g * G:(g + 1) * G],
                                         start=True, stop=True)
                    last.then_inc(pp, 1)

            for p in range(HP):
                if p == 0:
                    pe.wait_ge(pa, 2 + 3 * HP)
                else:
                    pe.wait_ge(pa, 2 + 3 * HP + p)
                for g in range(NG):
                    last = pe.matmul(PS[:, g, 0:G], wg[:, p * P:(p + 1) * P],
                                     RW[:, 13, g * G:(g + 1) * G], start=True, stop=True)
                last.then_inc(pp, 1)

            pe.wait_ge(pd, 3 * HP)
            pe.wait_ge(pa, 2 + 4 * HP)
            pe.sem_inc(ch_pe.sem, 1)

            def pe_chunk(c):
                fill = Filler(pe, c + V_FOX0)

                def wait(steps, name):
                    pe.wait_ge(steps.sem, steps.after(c, name))

                def natural(src, bank, name):
                    for p in range(HP):
                        last = pe.transpose(PS[0:C, bank, p * P:(p + 1) * P], src[:, p], ident)
                    ch_pe.done(last, name)

                def vcols(h):
                    at = h % HP * P + h // HP * HD
                    return slice(at, at + HD)

                def hrows(h):
                    return slice(h // HP * HD, (h // HP + 1) * HD)

                fill.run(16)
                wait(ch_dve, "k")
                pe.wait_ge(ch_act.sem, ch_act.before(c))
                natural(Kc, 0, "nat_k")
                wait(ch_dve, "b")
                natural(Bc, 1, "nat_b")
                wait(ch_dve, "a")
                natural(AR[:, :, 0], 2, "nat_a")
                natural(Vc, 3, "nat_v")
                for i in range(2):
                    for m, src, bank in (("k", Kc, 4), ("b", Bc, 0)):
                        if i:
                            wait(ch_dve, f"mask_{m}0")
                        elif m == "b":
                            wait(ch_act, "nat_k")
                            wait(ch_dve, "nat_b")
                        for j in range(2):
                            for e in range(2):
                                rows, p = slice(e * HD, (e + 1) * HD), 2 * i + j
                                last = pe.matmul(PS[0:C, bank + e, j * 2 * C:(j + 1) * 2 * C], src[rows, p],
                                                 AR[rows, p].rearrange("p a b -> p (a b)"), start=True,
                                                 stop=True)
                        ch_pe.done(last, f"prod_{m}{i}")
                fill.run(4)
                wait(ch_dve, "mask_k1")
                wait(ch_dve, "nat_v")
                for h in range(NH):
                    last = pe.matmul(PS[0:C, 3, h * HD:(h + 1) * HD], MK[0:C, h, 0], Vn[0:C, vcols(h)],
                                     start=True, stop=True)
                ch_pe.done(last, "z")
                fill.run(4)
                wait(ch_dve, "xt_init")
                for q in range(2):
                    for j in range(4):
                        last = pe.transpose(PS[0:C, q, j * C:(j + 1) * C], XTr[0:C, 4 * q + j], ident[0:C, 0:C])
                    ch_pe.done(last, f"x_{q}")
                for lv in LEVELS:
                    for q in range(2):
                        if q == 0:
                            pe.wait_ge(ch_pool.sem, ch_pool.after(c, f"bm_{lv}"))
                        if lv == 1:
                            wait(ch_act, f"x_{q}")
                        else:
                            wait(ch_dve, f"x_{lv - 1}_{q}_xt")
                        for j in range(4):
                            h = 4 * q + j
                            last = pe.matmul(PS[0:C, q, j * C:(j + 1) * C], Bm[lv % 2][0:C, h], Xm[0:C, h],
                                             start=True, stop=True)
                        ch_pe.done(last, f"t1_{lv}_{q}")
                    fill.run(1)
                    for q in range(2):
                        wait(ch_act, f"t1_{lv}_{q}")
                        if lv == 1 and q == 0:
                            wait(ch_act, "nat_a")
                        for j in range(4):
                            h = 4 * q + j
                            if lv < N_LV - 1:
                                pe.matmul(PS[0:C, 2 + q, j * C:(j + 1) * C], XTr[0:C, h], T1[0:C, h],
                                          start=True, stop=True)
                            last = pe.matmul(PS[0:C, 4 + q, j * C:(j + 1) * C], T1[0:C, h], XTr[0:C, h],
                                             start=True, stop=True)
                        ch_pe.done(last, f"t2_{lv}_{q}")
                    fill.run(1)
                fill.run(2)
                wait(ch_dve, f"x_{N_LV - 1}_1_xt")
                for h in range(NH):
                    e, p = h // HP, h % HP
                    last = pe.matmul(PS[e * HD:(e + 1) * HD, 0, p * C:(p + 1) * C], An[0:C, vcols(h)],
                                     XTr[0:C, h], start=True, stop=True)
                ch_pe.done(last, "wt")
                fill.run(2)
                wait(ch_act, "wt")
                wait(ch_act, "z")
                for h in range(NH):
                    e, p, rows = h // HP, h % HP, hrows(h)
                    out = PS[0:C, 4 + e, p * HD:(p + 1) * HD]
                    pe.matmul(out, XTr[0:C, h], Zm[0:C, h * HD:(h + 1) * HD], start=True, stop=False)
                    last = pe.matmul(out, WT[rows, p], St[rows, p], start=False, stop=True)
                ch_pe.done(last, "u")
                fill.run(2)
                wait(ch_act, "nu")
                for h in range(NH):
                    e, p, rows = h // HP, h % HP, hrows(h)
                    out = PS[0:C, 2 + e, p * HD:(p + 1) * HD]
                    pe.matmul(out, AR[rows, p, 1], St[rows, p], start=True, stop=False)
                    pe.matmul(out, MK[0:C, h, 1], Vn[0:C, vcols(h)], start=False, stop=False)
                    last = pe.matmul(out, MB[0:C, h, 1], NU[0:C, h * HD:(h + 1) * HD], start=False, stop=True)
                ch_pe.done(last, "y")
                for h in range(NH):
                    p, rows = h % HP, hrows(h)
                    out = PS[rows, 1, p * HD:(p + 1) * HD]
                    pe.matmul(out, ident[rows, rows], St[rows, p], start=True, stop=False)
                    pe.matmul(out, Kn[0:C, vcols(h)], Vn[0:C, vcols(h)], start=False, stop=False)
                    last = pe.matmul(out, Bn[0:C, vcols(h)], NU[0:C, h * HD:(h + 1) * HD], start=False, stop=True)
                ch_pe.done(last, "s")
                fill.run()
                wait(ch_dve, "norm")
                for p in range(HP):
                    last = pe.transpose(PS[:, 0, p * C:(p + 1) * C], Yc[0:C, p * P:(p + 1) * P], ident[0:C, 0:C])
                ch_pe.done(last, "yt")

            with pe.Fori(0, C_FOX) as c:
                pe_chunk(c)
            with pe.Fori(C_FOX, NC) as c:
                pe_chunk(c)

            pe.wait_ge(ch_act.sem, ch_act.before(NC))
            for kind in range(6):
                last = pe.transpose(PS[0:HP * DEC, kind // 4, kind % 4 * P:(kind % 4 + 1) * P],
                                    d_col[:, kind].rearrange("p a b -> p (a b)"), ident)
            last.then_inc(ds_pe, 1)
            pe.wait_ge(ds_act, 1)
            for k in range(KT):
                for g in range(NG):
                    last = pe.matmul(PS[0:NH, g, 0:G], wf[:, k, :], HT[:, k, g * G:(g + 1) * G],
                                     start=(k == 0), stop=(k == KT - 1))
            last.then_inc(f_ready, 1)
            for t in range(NC):
                if t >= 2:
                    pe.wait_ge(vt_read, t - 1)
                for hp in range(HP):
                    last = pe.transpose(PS[0:C, 3 + t % 2, hp * P:(hp + 1) * P],
                                        FX[:, 2 * HP + hp, t * C:(t + 1) * C], ident)
                last.then_inc(vt_ready, 1)

            with pe.Fori(V_GATE0 + (NC - C_FOX), V_BR0) as v:
                Filler(pe, v).run()
            pe.wait_ge(ds_dve, 4)
            for p in range(HP):
                last = pe.transpose(PS[:, 2, p * DEC:(p + 1) * DEC], dYn[0:DEC, p * P:(p + 1) * P],
                                    ident[0:DEC, 0:DEC])
            last.then_inc(ds_pe, 1)
            pe.wait_ge(vt_read, NC)
            pe.wait_ge(f_read, 1)
            pe.wait_ge(sub_read, 2 + 2 * NG * PV_FILL)
            pe.wait_ge(ds_act, 2 + HP)
            pe.wait_ge(da_step, 1)
            pe.sem_inc(kp_used, 2)
            pe.sem_inc(vp_used, 2)

            def pe_keys(n, s):
                for pg in range(NPG):
                    for hp in range(HP):
                        at = DA_COL + pg * NH + 2 * hp
                        last = pe.matmul(PS[:, 7, at:at + 2], Kp[s][:, pg, hp, :],
                                         qbd[:, hp, bass.ds(n, 1), :].rearrange("p o h -> p (o h)"),
                                         start=True, stop=True)
                last.then_inc(kp_used, 1)

            def pe_values(n, s):
                for hp in range(HP):
                    for pg in range(NPG):
                        last = pe.matmul(PS[:, 7, DA_COL + 2 * hp:DA_COL + 2 * hp + 2], Vp[s][:, pg, hp * P:(hp + 1) * P],
                                         da_s[:, bass.ds(n, 1), pg, 2 * hp:2 * hp + 2]
                                         .rearrange("p o h -> p (o h)"), start=(pg == 0), stop=(pg == NPG - 1))
                last.then_inc(vp_used, 1)

            def pe_pair(i, first, pages_in, pe_pages):
                def scores(j):
                    hl, qt = tiles[j]
                    if qt == 0:
                        pe.wait_ge(qk_staged, 2 * i + hl + 1)
                        pe.wait_ge(cneg_in[hl], 16 * i + 16)
                    bank = 0 if j % 2 else 3
                    if j >= 2:
                        pe.wait_ge(p_ready, N_IT * i + j - 1)
                    for c0 in range(0, (qt + 1) * C, 512):
                        n = min(512, (qt + 1) * C - c0)
                        last = pe.matmul(PS[0:C, bank + c0 // 512, 0:n],
                                         qa[0:HD + 1, hl, qt * C:(qt + 1) * C],
                                         ka[0:HD + 1, hl, c0:c0 + n], start=True, stop=True)
                    last.then_inc(s_done, 1)

                def transposed(j):
                    hl, qt = tiles[j]
                    pe.wait_ge(dg_ready, N_IT * i + j + 1)
                    for g in range(groups[j]):
                        n = gr_before[j] + g
                        slot = n % 2
                        if n >= 2:
                            pe.wait_ge(pt_read[slot], (N_GR // 2) * i + n // 2)
                        for b in range(4 * g, min(4 * g + 4, qt + 1)):
                            last = pe.matmul(PS[0:C, 5 + slot, (b - 4 * g) * C:(b - 4 * g + 1) * C],
                                             Pm[0:C, j % 2, b * C:(b + 1) * C], dg[0:C, j % 2],
                                             start=True, stop=True)
                        last.then_inc(pt_done, 1)

                def values(j):
                    hl, qt = tiles[j]
                    if j == 0:
                        pe.wait_ge(v_staged, i + 1)
                    end = gr_before[j] + groups[j]
                    pe.wait_ge(pt_read[0], (N_GR // 2) * i + (end + 1) // 2)
                    if end >= 2:
                        pe.wait_ge(pt_read[1], (N_GR // 2) * i + end // 2)
                    if j:
                        pe.wait_ge(o_read, N_IT * i + j)
                    if j in DA_AT:
                        q = DA_AT.index(j)
                        pe.wait_ge(pages_in[q % 2], 16 * NPG * 2 * i + 16 * NPG * (q // 2 + 1 - 2 * first))
                        pe_pages(NDA * i + (q - NDA * first), q % 2)
                    for b in range(qt + 1):
                        last = pe.matmul(PS[hl * HD:(hl + 1) * HD, 7, 0:C], vst[0:C, b, hl * HD:(hl + 1) * HD],
                                         PTm[0:C, j % 2, b, :], start=(b == 0), stop=(b == qt))
                    last.then_inc(pv_done, 1)

                scores(0)
                for j in range(N_IT):
                    if j + 1 < N_IT:
                        scores(j + 1)
                    transposed(j)
                    if j:
                        values(j - 1)
                values(N_IT - 1)
            with pe.Fori(0, HP // 2) as i:
                pe_pair(i, 0, kp_in, pe_keys)
            pe.wait_ge(p_ready, N_IT * HP // 2)
            pe.wait_ge(pt_read[0], N_GR // 2 * (HP // 2))
            pe.wait_ge(pt_read[1], N_GR // 2 * (HP // 2))
            pe.wait_ge(o_read, N_IT * HP // 2)
            pe.wait_ge(lfp_in, 16 * NPG * DEC)
            bias4 = PS[:, 7, :].rearrange("p (b g h) -> p b g h", b=DEC, g=NPG)
            pe.matmul(PS[:, 7, :], suf, lfp.rearrange("p b g h -> p (b g h)"), start=True, stop=False)
            for s in range(1, NPG):
                pe.matmul(bias4[:, :, 0:NPG - s, :], ones, lfp[:, :, s:NPG, :], start=False, stop=False)
            last = pe.matmul(bias4, ones[0:NH, :],
                             lfd[0:NH].unsqueeze(2).to_broadcast([NH, DEC, NPG, NH]), start=False, stop=True)
            last.then_inc(da_ready, 1)
            last = pe.matmul(PS[:, 5, 0:DEC * NH].rearrange("p (b a h) -> p a b h", b=DEC, a=HP), ones,
                             qkbd, start=True, stop=True)
            last.then_inc(da_ready, 1)
            pe.wait_ge(da_step, 2)
            pe.transpose(PS[0:DEC * NH, 4, 0:P], da_mx, ident).then_inc(da_ready, 1)
            pe.wait_ge(da_step, 3)
            pe.matmul(PS[:, 4, 256:256 + DEC * NH], ones[0:DEC * NH, :], da_dg[0:DEC * NH], start=True,
                      stop=True).then_inc(da_ready, 1)
            pe.wait_ge(da_step, 5)
            pe.matmul(PS[:, 4, 384:384 + DEC * NH], ones, da_den, start=True, stop=True)\
              .then_inc(da_ready, 1)
            with pe.Fori(HP // 2, HP) as i:
                pe_pair(i, HP // 2, vp_in, pe_values)
            pe.wait_ge(da_step, 6)
            pe.wait_ge(o_done, 2)
            with pe.Fori(V_BR0, V_OUT0) as v:
                pe_unit(pe, v, 0, YT, HP)
                pe_unit(pe, v, 1, FX, HP)
            pe.wait_ge(mg_ready, KT)
            with pe.Fori(V_OUT0, V_OUT0 + PV_OUT) as v:
                pe_unit(pe, v, 0, MG)
                pe_unit(pe, v, 1, MG)
            pe.wait_ge(evac[0], V_FF0 - PV_FILL)
            pe_norm(pe, 1)
            pe.wait_ge(rms_ready, 2)
            pe_unit_split(pe, V_FF0, 0, halves(HS), lambda k: pe.wait_ge(h_ready, KT + 1 + k))
            pe_unit_split(pe, V_FF0, 1, halves(HS))

            def pe_up(c, j):
                pe_unit_split(pe, KT * c + j + V_FF0, 0, halves(HS))
                pe_unit_split(pe, KT * c + j + V_FF0, 1, halves(HS))

            def pe_down(c):
                v0 = KT * c + (V_FF0 + KT // 2)
                pe_unit_split(pe, v0, 0, halves(FS), lambda k: pe.wait_ge(ff_ready, KT * c + (k + 3)))
                pe_unit_split(pe, v0, 1, halves(FS))
                with pe.Fori(1, KT // 2) as j:
                    pe_unit_split(pe, j + v0, 0, halves(FS))
                    pe_unit_split(pe, j + v0, 1, halves(FS))

            with pe.Fori(1, KT // 2) as j:
                pe_up(0, j)
            pe_down(0)
            with pe.Fori(1, FF_CH) as c:
                with pe.Fori(0, KT // 2) as j:
                    pe_up(c, j)
                pe_down(c)
            pe.wait_ge(evac[0], PAIRS - PV_FILL)
            pe_norm(pe, 2)

        @block.scalar
        def _(act):
            order = Order(act, act_order)
            act.wait_ge(consts_in, 80)
            act.wait_ge(x_in, 64)
            for k in range(KT):
                act_square(act, 0, k, k % 2)
            act_split(act, 0, 0, of=RWKV)
            act_rms(act, 0)
            for k in range(KT):
                act.wait_ge(h_ready, k + 1)
                act.copy(H0[0][:, k], HT[:, k, :]).then_inc(h0_hi, 1)
                if k == 2:
                    act_split(act, 0, 1, of=RWKV)

            def keep(v, s, dst):
                act.wait_ge(unit_done, 2 * v + s + 1)
                act.copy(g3(dst), grp(s)).then_inc(evac[s], 1)

            act.wait_ge(h_ready, KT)
            with act.Fori(0, PV_RW - 1) as v:
                for s in range(2):
                    keep(v, s, RW[:, bass.ds(2 * v + s, 1), :].rearrange("p o n -> p (o n)"))
                    act_split(act, v + 1, s, of=RWKV)
            for s in range(2):
                keep(PV_RW - 1, s, RW[:, 2 * PV_RW - 2 + s, :])
            act.wait_ge(mixed, RW_T)
            act.activation(RW[0:HD, 12, :], RW[0:HD, 12, :], ACT.Tanh).then_inc(pa, 1)
            act.activation(RW[:, 13, :], RW[:, 13, :], ACT.Sigmoid).then_inc(pa, 1)
            for p in range(HP):
                for m, dst, par0 in ((0, LW, V_W0), (1, BB, V_A0)):
                    act.wait_ge(pp, 2 * p + m + 1)
                    act.activation(g3(dst[:, p]), grp(m), ACT.Sigmoid,
                                   bias=par[:, par0 + p:par0 + p + 1]).then_inc(pa, 1)
            for p in range(HP):
                act.wait_ge(pp, 2 * HP + 2 * p + 1)
                act.activation(g3(ptmp[0]), grp(0), ACT.Sqrt).then_inc(pa, 1)
            for p in range(HP):
                act.wait_ge(pp, 4 * HP + p + 1)
                act.copy(g3(GT[:, p]), grp(0)).then_inc(pa, 1)
            act.wait_ge(pd, 3 * HP)
            for kind, src in ((1, KK), (2, BB), (3, RW[:, HP:2 * HP]), (4, RW[:, 0:HP]), (5, RW[:, 2 * HP:3 * HP])):
                order(act.copy(d_col[:, kind], src[:, :, TP:TS]))
            order(act.activation(d_col[:, 0], LW[:, :, TP:TS], ACT.Exp))
            act.sem_inc(d_col_ready, 1)
            act.wait_ge(prep_stored, 16 * 6 * HP)
            act.wait_ge(bg_stored, 16)
            act.wait_ge(sh_stored, 16)
            act.sem_inc(sub_read, 2)
            act.sem_inc(g_stored[0], 16)
            act.sem_inc(g_stored[1], 16)
            act.sem_inc(ch_act.sem, 1)

            def gate_out(x, m):
                s, g = divmod(m, NG)
                if g == 0:
                    act.wait_ge(g_stored[s], 16 * x + 16)
                act_fill(act, x + V_GATE0, m, SGs[:, s, g * G:(g + 1) * G])

            def act_chunk(c, gates):
                def out(m):
                    if gates:
                        gate_out(c - C_FOX, m)
                    else:
                        s, g = divmod(m, NG)
                        act_fill(act, c + V_FOX0, m, FX[:, bass.ds(2 * c + s, 1), g * G:(g + 1) * G]
                                 .rearrange("p o n -> p (o n)"))

                def wait(steps, name):
                    act.wait_ge(steps.sem, steps.after(c, name))

                here = bass.ds(c * C, C)
                act.wait_ge(ch_pe.sem, ch_pe.before(c))
                act.wait_ge(ch_dve.sem, ch_dve.before(c))
                act.wait_ge(st_in, 16 * c + 16)
                ch_act.done(act.copy(Vc, CH[:, 2]), "v")
                wait(ch_dve, "scan_3")
                ch_act.done(act.activation(E1, Lc, ACT.Exp), "e1")
                ch_act.done(act.activation(E3, Lc, ACT.Exp, scale=-1.0), "e3")
                wait(ch_dve, "lm")
                ch_act.done(act.activation(E2, Lm, ACT.Exp), "e2")
                out(0)
                out(1)
                wait(ch_pe, "nat_k")
                ch_act.done(act.copy(Kn[0:C], PS[0:C, 0, :]), "nat_k")
                wait(ch_pe, "nat_a")
                ch_act.done(act.copy(An[0:C], PS[0:C, 2, :]), "nat_a")
                wait(ch_pe, "z")
                ch_act.done(act.copy(Zm[0:C], PS[0:C, 3, :]), "z")

                def quad(ap, q):
                    return ap[0:C, 4 * q:4 * q + 4].rearrange("p a b -> p (a b)")

                for q in range(2):
                    wait(ch_pe, f"x_{q}")
                    ch_act.done(act.copy(quad(Xm, q), PS[0:C, q, 0:4 * C]), f"x_{q}")
                out(2)
                for lv in LEVELS:
                    for q in range(2):
                        wait(ch_pe, f"t1_{lv}_{q}")
                        if lv > 1:
                            wait(ch_pe, f"t2_{lv - 1}_{q}")
                        ch_act.done(act.copy(quad(T1, q), PS[0:C, q, 0:4 * C]), f"t1_{lv}_{q}")
                    if lv == 4:
                        out(3)
                wait(ch_pe, "wt")
                ch_act.done(act.copy(WT, PS[:, 0, 0:HP * C].rearrange("p (a b) -> p a b", a=HP)), "wt")
                out(4)
                wait(ch_pe, "u")
                ch_act.done(act.mul(NU[0:C].rearrange("p (e n) -> p e n", e=2), PS[0:C, 4:6, 0:HP * HD],
                                    -1.0), "nu")
                wait(ch_dve, "var")
                ch_act.done(act.activation(gst[0:C, 2], gst[0:C, 1], ACT.Ln, scale=1.0 / HD,
                                           bias=par[0:C, V_GEPS:V_GEPS + 1]), "ln")
                wait(ch_act, "ln")
                ch_act.done(act.activation(gst[0:C, 3], gst[0:C, 2], ACT.Exp, scale=-0.5), "rstd")
                out(5)
                wait(ch_pe, "yt")
                for p in range(HP):
                    ch_act.done(act.activation(YT[:, p, here], PS[:, 0, p * C:(p + 1) * C], ACT.Identity,
                                               scale=par[:, V_LW + p:V_LW + p + 1],
                                               bias=par[:, V_LB + p:V_LB + p + 1]), f"y_{p}")
            with act.Fori(0, C_FOX) as c:
                act_chunk(c, False)
            with act.Fori(C_FOX, NC) as c:
                act_chunk(c, True)
            act.wait_ge(ch_pe.sem, ch_pe.before(NC))
            act.wait_ge(ds_pe, 1)
            act.copy(d_nat[0:HP * DEC].rearrange("p k c -> p (k c)"),
                     PS[0:HP * DEC, 0:2, :].rearrange("p a b -> p (a b)")[:, 0:6 * P]).then_inc(ds_act, 1)
            act.wait_ge(f_ready, 1)
            act.wait_ge(sp_stored, 16)
            order(act.activation(g3(f_neg[0:NH]), PS[0:NH, 0:3, 0:G], ACT.Identity,
                                 bias=par[0:NH, V_BF:V_BF + 1]))
            order(act.activation(f_t[0:NH], f_neg[0:NH], ACT.Abs))
            order(act.activation(f_t[0:NH], f_t[0:NH], ACT.Exp, scale=-1.0))
            act.activation(f_t[0:NH], f_t[0:NH], ACT.Ln,
                           bias=cst[0:NH, C_ONE:C_ONE + 1]).then_inc(f_read, 1)
            for t in range(NC):
                act.wait_ge(vt_ready, t + 1)
                act.copy(vnat[0:C, t, :], PS[0:C, 3 + t % 2, :]).then_inc(vt_read, 1)

            with act.Fori(NC - C_FOX, PV_GATE) as x:
                for m in range(2 * NG):
                    gate_out(x, m)
            act.wait_ge(ds_var, 1)
            order(act.activation(dst4[0:DEC, 2], dst4[0:DEC, 1], ACT.Ln, scale=1.0 / HD,
                                 bias=par[0:DEC, V_GEPS:V_GEPS + 1]))
            act.activation(dst4[0:DEC, 3], dst4[0:DEC, 2], ACT.Exp, scale=-0.5).then_inc(ds_act, 1)
            act.wait_ge(ds_pe, 2)
            for p in range(HP):
                act.activation(YT[:, p, TP:TS], PS[:, 2, p * DEC:(p + 1) * DEC], ACT.Identity,
                               scale=par[:, V_LW + p:V_LW + p + 1],
                               bias=par[:, V_LB + p:V_LB + p + 1]).then_inc(ds_act, 1)
            def act_pair(i):
                def exps(j):
                    hl, qt = tiles[j]
                    bank = 0 if j % 2 else 3
                    n = (qt + 1) * C
                    act.wait_ge(max_ready, N_IT * i + j + 1)
                    if j >= 2:
                        act.wait_ge(pt_done, N_GR * i + gr_before[j - 1])
                    if j >= 4:
                        act.wait_ge(dg_ready, N_IT * i + j - 3)
                    act.activation(Pm[0:C, j % 2, 0:n], sflat(bank, n), ACT.Exp,
                                   bias=rowmax[0:C, j % 2:j % 2 + 1],
                                   accum_out=rowsum[0:C, j % 4:j % 4 + 1]).then_inc(p_ready, 1)

                def blocks(j):
                    hl, qt = tiles[j]
                    for g in range(groups[j]):
                        n = gr_before[j] + g
                        if n % 2 == 0:
                            act.wait_ge(pt_done, N_GR * i + n + 1)
                            if g == 0 or g == 1:
                                if j >= 2:
                                    act.wait_ge(pv_done, N_IT * i + j - 1)
                            m = min(4, qt + 1 - 4 * g)
                            act.copy(PTm[0:C, j % 2, 4 * g:4 * g + m, :],
                                     PS[0:C, 5, 0:m * C].rearrange("p (a b) -> p a b", a=m))\
                               .then_inc(pt_read[0], 1)

                exps(0)
                for j in range(N_IT):
                    if j + 1 < N_IT:
                        exps(j + 1)
                    blocks(j)
            with act.Fori(0, HP // 2) as i:
                act_pair(i)
            act.wait_ge(da_step, 4)
            act.activation(da_s.rearrange("p b g h -> p (b g h)"), da_s.rearrange("p b g h -> p (b g h)"),
                           ACT.Exp).then_inc(da_exp, 1)
            act.activation(da_po, da_po, ACT.Exp).then_inc(da_exp, 1)
            with act.Fori(HP // 2, HP) as i:
                act_pair(i)
            act.wait_ge(o_done, 2)
            with act.Fori(0, KT) as n:
                for s in range(2):
                    act.wait_ge(g_back[s], 16 * n + 16)
                    act.wait_ge(sg_used, 2 * n + (s + 1))
                    act.activation(SG[:, s], GR[:, s], ACT.Sigmoid).then_inc(sg_ready, 1)
            with act.Fori(0, PV_OUT) as j:
                for s in range(2):
                    act.wait_ge(evac[s], j + (V_OUT0 - PV_FILL + 1))
                    act_square(act, 1, 2 * j + s, s)
            act_split(act, V_FF0, 0)
            act_rms(act, 1)
            for k in range(KT):
                act.wait_ge(h_raw, k + 1)
                act.copy(HS[:, 0, k], norms[1][0][:, k % 2]).then_inc(h_hi, 1)
                if k == 2:
                    act_split(act, V_FF0, 1)

            def act_up(c):
                with act.Fori(0, KT // 2) as j:
                    for s in range(2):
                        act.wait_ge(unit_done, 2 * KT * c + 2 * j + (2 * V_FF0 + s + 1))
                        act.wait_ge(ff_ready, KT * c + 2 * j + (s + 1))
                        act.activation(g3(RL[s]), grp(s), ACT.Relu).then_inc(evac[s], 1)
                        act_split(act, KT * c + j + (V_FF0 + 1), s)
                        act.wait_ge(ff_raw, KT * c + 2 * j + (s + 1))
                        act.copy(FS[:, 0, bass.ds(2 * j + s, 1)].rearrange("p o n -> p (o n)"), RL[s])\
                           .then_inc(ff_hi, 1)

            with act.Fori(0, FF_CH - 1) as c:
                act_up(c)
                with act.Fori(0, KT // 2) as j:
                    for s in range(2):
                        act_split(act, KT * c + j + (V_FF0 + KT // 2 + 1), s)
            act_up(FF_CH - 1)
            for j in range(KT // 2):
                for s in range(2):
                    v = PAIRS - KT // 2 + j
                    act.wait_ge(evac[s], v + 1 - PV_FILL)
                    act_square(act, 2, 2 * j + s, s)
                    if v + 1 < PAIRS:
                        act_split(act, v + 1, s)
            act_rms(act, 2)

        @block.vector
        def _(dve):
            order = Order(dve, dve_order)
            dve.wait_ge(consts_in, 80)
            dve.wait_ge(x_in, 64)
            order(dve.memset(norms[0][1], 0.0))
            for k in range(KT):
                dve_add_square(dve, 0, k, k % 2)
            dve_rms(dve, 0, order)
            def low_half0(k):
                dve.wait_ge(h0_hi, k + 1)
                dve.tensor_tensor(H0[1][:, k], HT[:, k, :], H0[0][:, k], ALU.subtract).then_inc(h0_ready, 1)

            dve_split(dve, 0, 0, of=RWKV)
            for k in range(KT):
                normed(dve, 0, k, V_NM, HT[:, k, :]).then_inc(h_ready, 1)
                if k:
                    low_half0(k - 1)
                if k == 4:
                    dve_split(dve, 0, 1, of=RWKV)
            low_half0(KT - 1)
            dve.wait_ge(h_ready, KT)
            mix = Order(dve, mix_order)
            dve.wait_ge(lora_in, 16)
            mix(dve.memset(mtmp[:, TS:TT], 0.0))
            def mix_pair(i, more):
                for s in range(2):
                    tile = bass.ds(2 * i + s, 1)

                    def cut(a, b):
                        return RW[:, tile, a:b].rearrange("p o n -> p (o n)")

                    dve.wait_ge(evac[s], i + 1)
                    if more:
                        dve_split(dve, i + 1, s, of=RWKV)
                    mix(dve.tensor_copy(sh_out[:, tile, :], RW[:, tile, TP - 1:TS]))
                    mix(dve.tensor_tensor(mtmp[:, 1:TP], cut(0, TP - 1), cut(1, TP), ALU.subtract))
                    mix(dve.tensor_scalar(mtmp[:, 0:1], cut(0, 1), -1.0, None, ALU.mult))
                    mix(dve.tensor_tensor(mtmp[:, TP:TS], sh_in[:, tile, :].rearrange("p o n -> p (o n)"),
                                          cut(TP, TS), ALU.subtract))
                    dve.scalar_tensor_tensor(cut(0, TT), mtmp, par[:, bass.ds(2 * i + (V_MU + s), 1)],
                                             cut(0, TT), ALU.mult, ALU.add).then_inc(mixed, 1)
                    dve.wait_ge(mixed, 2 * i + (s + 1))
            with dve.Fori(0, PV_RW - 1) as i:
                mix.enter(i, 8)
                mix_pair(i, True)
                mix.leave(PV_RW - 1)
            mix_pair(PV_RW - 1, False)
            for p in range(HP):
                r_, k_, v_ = RW[:, p, :], RW[:, HP + p, :], RW[:, 2 * HP + p, :]
                if p == 0:
                    dve.wait_ge(pa, 10)
                order(dve.tensor_scalar(LW[:, p], LW[:, p], -E_HALF, None, ALU.mult))
                order(dve.tensor_scalar(KK[:, p], k_, par[:, V_KK + p:V_KK + p + 1], None, ALU.mult))
                dve.tensor_tensor(ptmp[0], KK[:, p], KK[:, p], ALU.mult).then_inc(pd, 1)
                order(dve.tensor_scalar(mtmp, BB[:, p], 1.0, par[:, V_KA + p:V_KA + p + 1],
                                        ALU.subtract, ALU.mult))
                order(dve.scalar_tensor_tensor(k_, mtmp, 1.0, k_, ALU.add, ALU.mult))
                dve.scalar_tensor_tensor(ptmp[1], r_, par[:, V_RK + p:V_RK + p + 1], k_, ALU.mult, ALU.mult)\
                   .then_inc(pd, 1)
                dve.wait_ge(pa, 11 + p)
                order(dve.tensor_scalar(ptmp[0], ptmp[0], 1e-12, None, ALU.max))
                order(dve.reciprocal(ptmp[0], ptmp[0]))
                order(dve.tensor_tensor(KK[:, p], KK[:, p], ptmp[0], ALU.mult))
                order(dve.tensor_tensor(BB[:, p], KK[:, p], BB[:, p], ALU.mult))
                dve.wait_ge(pp, 2 * HP + 2 * p + 2)
                dve.tensor_tensor(g3(BON[:, p]), grp(1), g3(v_), ALU.mult).then_inc(pd, 1)
                dve.wait_ge(pd, 3 * p + 3)

            dve.wait_ge(prep_stored, 16 * 6 * HP)
            dve.wait_ge(bg_stored, 16)
            dve.wait_ge(sh_stored, 16)
            dve.wait_ge(d_col_ready, 1)
            order(dve.memset(St, 0.0))
            order(dve.memset(YT[:, :, TS:TT], 0.0))
            dve.sem_inc(ch_dve.sem, 1)
            with dve.Fori(0, NC) as c:
                def wait(steps, name):
                    dve.wait_ge(steps.sem, steps.after(c, name))

                def done(ins, name):
                    ch_dve.done(ins, name)
                    dve.wait_ge(ch_dve.sem, ch_dve.after(c, name))

                dve.wait_ge(ch_pe.sem, ch_pe.before(c))
                dve.wait_ge(st_in, 16 * c + 16)
                for p in range(HP):
                    done(dve.tensor_tensor_scan(Lc[:, p], ones[:, 0:C], CH[:, 3, p], 0.0, ALU.mult, ALU.add),
                         f"scan_{p}")
                done(dve.tensor_tensor(Lm, Lc, CH[:, 3], ALU.subtract), "lm")
                wait(ch_act, "e1")
                done(dve.tensor_tensor(AR[:, :, 1], CH[:, 0], E1, ALU.mult), "r")
                wait(ch_act, "e3")
                done(dve.tensor_tensor(Kc, CH[:, 1], E3, ALU.mult), "k")
                done(dve.tensor_tensor(Bc, CH[:, 5], E3, ALU.mult), "b")
                wait(ch_act, "e2")
                done(dve.tensor_tensor(AR[:, :, 0], CH[:, 4], E2, ALU.mult), "a")
                wait(ch_pe, "nat_b")
                done(dve.tensor_copy(Bn[0:C], PS[0:C, 1, :]), "nat_b")
                wait(ch_pe, "nat_v")
                done(dve.tensor_copy(Vn[0:C], PS[0:C, 3, :]), "nat_v")
                cm = cst[0:C, C_CM:C_CM + 2 * C].unsqueeze(1).unsqueeze(1).to_broadcast([C, 2, 2, 2 * C])
                for i in range(2):
                    for m, dst, bank in (("k", MK, 4), ("b", MB, 0)):
                        wait(ch_pe, f"prod_{m}{i}")
                        done(dve.tensor_tensor(
                            dst[0:C].rearrange("p (e a) x t -> p e a (x t)", e=2)[:, :, 2 * i:2 * i + 2],
                            PS[0:C, bank:bank + 2, 0:4 * C].rearrange("p e (a n) -> p e a n", a=2),
                            cm, ALU.mult), f"mask_{m}{i}")
                wait(ch_pool, "bm_0")
                done(dve.tensor_tensor(XTr[0:C], ident[0:C, 0:C].unsqueeze(1).to_broadcast([C, NH, C]),
                                       Bm[0][0:C], ALU.subtract), "xt_init")

                def quad(ap, q):
                    return ap[0:C, 4 * q:4 * q + 4].rearrange("p a b -> p (a b)")

                for lv in LEVELS:
                    for q in range(2):
                        wait(ch_pe, f"t2_{lv}_{q}")
                        if lv < N_LV - 1:
                            done(dve.tensor_tensor(quad(Xm, q), quad(Xm, q), PS[0:C, 2 + q, 0:4 * C],
                                                   ALU.subtract), f"x_{lv}_{q}_x")
                        done(dve.tensor_tensor(quad(XTr, q), quad(XTr, q), PS[0:C, 4 + q, 0:4 * C],
                                               ALU.subtract), f"x_{lv}_{q}_xt")

                def heads(ap):
                    return ap.rearrange("p (h v) -> p h v", h=NH)

                def spread(ap):
                    return ap.unsqueeze(2).to_broadcast([C, NH, HD])

                def by_head(ap):
                    return ap.rearrange("p (e a v) -> p e a v", e=2, a=HP)

                def spread4(k):
                    return gst[0:C, k].rearrange("p (e a) -> p e a", e=2).unsqueeze(3).to_broadcast([C, 2, HP, HD])

                y = PS[0:C, 2:4, 0:HP * HD].rearrange("p e (a v) -> p e a v", a=HP)
                ych = Yc[0:C].rearrange("p (a e v) -> p e a v", a=HP, e=2)
                wait(ch_pe, "y")
                done(dve.tensor_reduce(gst[0:C, 0].rearrange("p (e a) -> p e a", e=2), y, AX.X, ALU.add), "sum")
                done(dve.tensor_scalar(gst[0:C, 0], gst[0:C, 0], 1.0 / HD, None, ALU.mult), "mean")
                wait(ch_pe, "s")
                done(dve.tensor_tensor(St, PS[:, 1, 0:HP * HD].rearrange("p (a b) -> p a b", a=HP),
                                       E1[:, :, C - 1:C].to_broadcast([P, HP, HD]), ALU.mult), "state")
                done(dve.tensor_tensor(ych, y, spread4(0), ALU.subtract), "center")
                done(dve.tensor_tensor(by_head(Zm[0:C]), ych, ych, ALU.mult), "sq")
                done(dve.tensor_reduce(gst[0:C, 1].rearrange("p (e a) -> p e a", e=2), by_head(Zm[0:C]), AX.X,
                                       ALU.add), "var")
                wait(ch_act, "rstd")
                done(dve.tensor_tensor(ych, ych, spread4(3), ALU.mult), "norm")

            dve.wait_ge(f_read, 1)
            order(dve.tensor_scalar(lfT[0:NH], f_neg[0:NH], 0.0, None, ALU.min))
            order(dve.tensor_tensor(lfT[0:NH], lfT[0:NH], f_t[0:NH], ALU.subtract))
            order(dve.memset(f_ones[0:NH], 1.0))
            order(dve.tensor_tensor_scan(f_c[0:NH], f_ones[0:NH], lfT[0:NH, 0:TP], 0.0, ALU.mult, ALU.add))
            dve.tensor_scalar(f_c[0:NH], f_c[0:NH], -1.0, None, ALU.mult).then_inc(lf_ready, 1)

            def on_keys(ap):
                return ap.unsqueeze(3).to_broadcast([P, DEC // 2, NH, HD])

            dve.wait_ge(ds_load, 16 * 11)
            order(dve.tensor_tensor(dT, dS, dKK, ALU.mult))
            order(dve.tensor_reduce(dU, dT, AX.X, ALU.add))
            dve.sem_inc(ds_dve, 1)
            order(dve.tensor_tensor(dS, dS, dW, ALU.mult))
            order(dve.tensor_tensor(dT, dB, on_keys(dU), ALU.mult))
            order(dve.tensor_tensor(dS, dS, dT, ALU.subtract))
            order(dve.tensor_tensor(dT, dK, on_keys(dV), ALU.mult))
            dve.tensor_tensor(dS, dS, dT, ALU.add).then_inc(ds_dve, 1)
            dve.wait_ge(ds_dve, 2)
            dve.wait_ge(ds_load, 16 * 13)
            order(dve.tensor_tensor(dT, dS, dR, ALU.mult))
            dve.tensor_reduce(dU, dT, AX.X, ALU.add).then_inc(ds_dve, 1)
            dve.wait_ge(ds_yb, 16)

            def heads(ap):
                return ap.rearrange("p (h v) -> p h v", h=NH)

            def spread(ap):
                return ap.unsqueeze(2).to_broadcast([DEC, NH, HD])

            order(dve.tensor_reduce(dst4[0:DEC, 0], heads(dYn[0:DEC]), AX.X, ALU.add))
            order(dve.tensor_scalar(dst4[0:DEC, 0], dst4[0:DEC, 0], 1.0 / HD, None, ALU.mult))
            order(dve.tensor_tensor(heads(dYn[0:DEC]), heads(dYn[0:DEC]), spread(dst4[0:DEC, 0]), ALU.subtract))
            order(dve.tensor_tensor(dSQ[0:DEC], dYn[0:DEC], dYn[0:DEC], ALU.mult))
            order(dve.tensor_reduce(dst4[0:DEC, 1], heads(dSQ[0:DEC]), AX.X, ALU.add))
            dve.sem_inc(ds_var, 1)
            dve.wait_ge(ds_act, 2)
            dve.tensor_tensor(heads(dYn[0:DEC]), heads(dYn[0:DEC]), spread(dst4[0:DEC, 3]), ALU.mult)\
               .then_inc(ds_dve, 1)
            dve.wait_ge(out_stored, 16 * 2)
            for s in range(2):
                dve.wait_ge(g_stored[s], 16 * (PV_GATE + 1))
            dve.wait_ge(cneg_stored, 16)
            order(dve.memset(qa[HD:HD + 1, :, :], 1.0))
            order(dve.memset(qbd, 0.0))
            for e in range(2):
                half = slice(e * HD, (e + 1) * HD)
                order(dve.tensor_scalar(qbd[half, :, :, e], FX[half, 0:HP, TP:TS], SCALE, None, ALU.mult))
            order(dve.tensor_tensor(qkbd, qbd, FX[:, HP:2 * HP, TP:TS].unsqueeze(3)
                                    .to_broadcast([P, HP, DEC, 2]), ALU.mult))
            dve.tensor_tensor(lfd[0:NH], lfT[0:NH, TP:TS].unsqueeze(2).to_broadcast([NH, DEC, NH]),
                              ident[0:NH, 0:NH].unsqueeze(1).to_broadcast([NH, DEC, NH]), ALU.mult)\
               .then_inc(da_step, 1)

            def move(dst, src):
                return dve.tensor_scalar(dst, src, 1.0, None, ALU.mult)

            def keys_out(n):
                move(da_s[:, n, :, :].rearrange("p o g h -> p (o g h)"), PS[:, 7, DA_COL:DA_COL + NPG * NH])

            def values_out(n):
                move(da_pv[:, :, n, :],
                     PS[:, 7, DA_COL:DA_COL + NH].rearrange("p (a o e) -> p a o e", a=HP, o=1))

            def dve_pair(i, first, pages_out):
                def maxes(j):
                    hl, qt = tiles[j]
                    bank = 0 if j % 2 else 3
                    dve.wait_ge(s_done, N_IT * i + j + 1)
                    diag = sflat(bank, C, qt * C)
                    order(dve.tensor_tensor(diag, diag, cst[0:C, C_AM:C_AM + C], ALU.add))
                    dve.tensor_reduce(rowmax[0:C, j % 2:j % 2 + 1], sflat(bank, (qt + 1) * C), AX.X, ALU.max,
                                      negate=True).then_inc(max_ready, 1)

                def blocks(j):
                    hl, qt = tiles[j]
                    for g in range(groups[j]):
                        n = gr_before[j] + g
                        if n % 2 == 1:
                            dve.wait_ge(pt_done, N_GR * i + n + 1)
                            if j >= 2:
                                dve.wait_ge(pv_done, N_IT * i + j - 1)
                            m = min(4, qt + 1 - 4 * g)
                            dve.tensor_copy(PTm[0:C, j % 2, 4 * g:4 * g + m, :],
                                            PS[0:C, 6, 0:m * C].rearrange("p (a b) -> p a b", a=m))\
                               .then_inc(pt_read[1], 1)

                def output(j):
                    hl, qt = tiles[j]
                    dve.wait_ge(pv_done, N_IT * i + j + 1)
                    if j + 0 in DA_AT:
                        pages_out(bass.ds(NDA * i + (DA_AT.index(j) - NDA * first), 1))
                    half = slice(hl * HD, (hl + 1) * HD)
                    move(FX[half, bass.ds(i, 1), qt * C:(qt + 1) * C].rearrange("p o n -> p (o n)"),
                         PS[half, 7, 0:C]).then_inc(o_read, 1)

                def diagonal(j):
                    dve.wait_ge(p_ready, N_IT * i + j + 1)
                    if j >= 2:
                        dve.wait_ge(pt_done, N_GR * i + gr_before[j - 1])
                    order(dve.reciprocal(rowinv[0:C, j % 2:j % 2 + 1], rowsum[0:C, j % 4:j % 4 + 1]))
                    dve.tensor_scalar(dg[0:C, j % 2], ident[0:C, 0:C], rowinv[0:C, j % 2:j % 2 + 1], None,
                                      ALU.mult).then_inc(dg_ready, 1)

                order.enter(i, 2 * N_IT + 2, first)
                dve.sem_inc(qk_free, 1)
                for hl in range(2):
                    half = slice(hl * HD, (hl + 1) * HD)
                    order(dve.tensor_scalar(qa[0:HD, hl, :],
                                            FX[half, bass.ds(i, 1), 0:TP].rearrange("p o n -> p (o n)"),
                                            SCALE, None, ALU.mult))
                    ins = dve.tensor_copy(ka[0:HD, hl, :],
                                          FX[half, bass.ds(i + HP, 1), 0:TP].rearrange("p o n -> p (o n)"))
                    ins.then_inc(qk_staged, 1)
                maxes(0)
                dve.tensor_copy(vst[0:C], vnat[0:C, :, bass.ds(i * P, P)]).then_inc(v_staged, 1)
                diagonal(0)
                for j in range(N_IT):
                    if j + 1 < N_IT:
                        maxes(j + 1)
                    blocks(j)
                    if j + 1 < N_IT:
                        diagonal(j + 1)
                    if j:
                        output(j - 1)
                output(N_IT - 1)
                order.leave(HP // 2)

            with dve.Fori(0, HP // 2) as i:
                dve_pair(i, 0, keys_out)

            dve.wait_ge(da_ready, 1)
            order(dve.tensor_copy(da_bias.rearrange("p b g h -> p (b g h)"), PS[:, 7, :]))
            flat_s = da_s.rearrange("p b g h -> p (b g h)")
            order(dve.tensor_tensor(flat_s, flat_s, da_bias.rearrange("p b g h -> p (b g h)"), ALU.add))
            dve.tensor_reduce(da_mx.rearrange("p (b h) -> p b h", b=DEC), da_s.rearrange("p b g h -> p b h g"),
                              AX.X, ALU.max).then_inc(da_step, 1)
            dve.wait_ge(da_ready, 3)
            order(dve.tensor_reduce(da_c1[0:DEC * NH], PS[0:DEC * NH, 4, 0:P], AX.X, ALU.max))
            dve.tensor_scalar(da_dg[0:DEC * NH], ident[0:DEC * NH, 0:DEC * NH], da_c1[0:DEC * NH], None,
                              ALU.mult).then_inc(da_step, 1)
            dve.wait_ge(da_ready, 4)
            order(dve.tensor_copy(da_own, PS[:, 5, 0:DEC * NH]))
            order(dve.tensor_tensor(da_mx, PS[:, 4, 256:256 + DEC * NH], da_own, ALU.max))
            order(dve.tensor_tensor(da_po, da_own, da_mx, ALU.subtract))
            dve.tensor_tensor(da_s, da_s, da_mx.rearrange("p (b h) -> p b h", b=DEC).unsqueeze(2)
                              .to_broadcast([P, DEC, NPG, NH]), ALU.subtract).then_inc(da_step, 1)
            dve.wait_ge(da_exp, 2)
            dve.tensor_reduce(da_den.rearrange("p (b h) -> p b h", b=DEC), da_s.rearrange("p b g h -> p b h g"),
                              AX.X, ALU.add).then_inc(da_step, 1)
            dve.wait_ge(da_ready, 5)
            order(dve.tensor_tensor(da_mx, PS[:, 4, 384:384 + DEC * NH], da_po, ALU.add))
            order(dve.reciprocal(da_mx, da_mx))
            with dve.Fori(HP // 2, HP) as i:
                dve_pair(i, HP // 2, values_out)

            def by_pair(ap, e):
                return ap.rearrange("p (b a e) -> p a b e", b=DEC, a=HP)[e * HD:(e + 1) * HD, :, :, e]

            for e in range(2):
                half = slice(e * HD, (e + 1) * HD)
                pv = da_pv[half, :, :, e]
                order(dve.tensor_tensor(da_o[half], by_pair(da_po, e), FX[half, 2 * HP:3 * HP, TP:TS], ALU.mult))
                order(dve.tensor_tensor(da_o[half], da_o[half], pv, ALU.add))
                last = dve.tensor_tensor(FX[half, 0:HP, TP:TS], da_o[half], by_pair(da_mx, e), ALU.mult)
                if e == 0:
                    order(last)
            last.then_inc(da_step, 1)
            dve.sem_inc(sg_used, 2)
            with dve.Fori(0, KT) as n:
                for s in range(2):
                    dst = MG[:, bass.ds(n, 1), :].rearrange("p o n -> p (o n)") if s == 0 else gtmp
                    dve.wait_ge(sg_ready, 2 * n + (s + 1))
                    dve.wait_ge(unit_done, 2 * n + (2 * V_BR0 + s + 1))
                    dve.tensor_tensor(g3(dst), g3(SG[:, s]), grp(s), ALU.mult).then_inc(evac[s], 1)
                    dve.wait_ge(evac[s], n + (V_BR0 - PV_FILL + 1))
                    dve.sem_inc(sg_used, 1)
                dst = MG[:, bass.ds(n, 1), :].rearrange("p o n -> p (o n)")
                dve.tensor_tensor(dst, dst, gtmp, ALU.add).then_inc(mg_ready, 1)
                dve.wait_ge(mg_ready, n + 1)
            dve.wait_ge(x_back, 16)
            order(dve.memset(norms[1][1], 0.0))

            def residual(j, unit, s):
                dst = g3(XT[:, bass.ds(2 * j + s, 1), :].rearrange("p o n -> p (o n)"))
                dve.wait_ge(unit_done, unit)
                dve.tensor_tensor(dst, dst, grp(s), ALU.add).then_inc(evac[s], 1)

            with dve.Fori(0, PV_OUT) as j:
                for s in range(2):
                    residual(j, 2 * j + (2 * V_OUT0 + s + 1), s)
                    dve_add_square(dve, 1, 2 * j + s, s)
            dve_split(dve, V_FF0, 0)
            dve_rms(dve, 1, order)
            dve.sem_inc(ff_ready, 2)
            raw = norms[1][0]

            def low_half(k):
                dve.wait_ge(h_hi, k + 1)
                dve.tensor_tensor(HS[:, 1, k], raw[:, k % 2], HS[:, 0, k], ALU.subtract).then_inc(h_ready, 1)

            for k in range(KT):
                if k >= 2:
                    dve.wait_ge(h_ready, KT + k - 1)
                normed(dve, 1, k, V_NF, raw[:, k % 2]).then_inc(h_raw, 1)
                if k:
                    low_half(k - 1)
                if k == 4:
                    dve_split(dve, V_FF0, 1)
            low_half(KT - 1)

            def dve_up(c):
                with dve.Fori(0, KT // 2) as j:
                    for s in range(2):
                        dve.wait_ge(evac[s], KT * c + j + (V_FF0 - PV_FILL + 1))
                        dve.tensor_tensor(RL[s], RL[s], RL[s], ALU.mult).then_inc(ff_raw, 1)
                        dve_split(dve, KT * c + j + (V_FF0 + 1), s)
                        dve.wait_ge(ff_hi, KT * c + 2 * j + (s + 1))
                        dst = bass.ds(2 * j + s, 1)
                        dve.tensor_tensor(FS[:, 1, dst].rearrange("p o n -> p (o n)"), RL[s],
                                          FS[:, 0, dst].rearrange("p o n -> p (o n)"),
                                          ALU.subtract).then_inc(ff_ready, 1)
                        dve.wait_ge(ff_ready, KT * c + 2 * j + (s + 3))

            def dve_down(c, j, s):
                residual(j, 2 * KT * c + 2 * j + (2 * V_FF0 + KT + s + 1), s)

            with dve.Fori(0, FF_CH - 1) as c:
                dve_up(c)
                with dve.Fori(0, KT // 2) as j:
                    for s in range(2):
                        dve_down(c, j, s)
                        dve_split(dve, KT * c + j + (V_FF0 + KT // 2 + 1), s)
            dve_up(FF_CH - 1)
            order(dve.memset(norms[2][1], 0.0))
            for j in range(KT // 2):
                for s in range(2):
                    dve_down(FF_CH - 1, j, s)
                    dve_add_square(dve, 2, 2 * j + s, s)
                    if j + 1 < KT // 2:
                        dve_split(dve, V_FF0 + KT * FF_CH - KT // 2 + j + 1, s)
            dve_rms(dve, 2, order)
            for k in range(KT):
                normed(dve, 2, k, V_NL, HT[:, k, :]).then_inc(h_ready, 1)

        @block.gpsimd
        def _(pool):
            pool.sem_inc(ch_pool.sem, 1)
            with pool.Fori(0, NC) as c:
                pool.wait_ge(ch_dve.sem, ch_dve.after(c, "mask_b1"))
                for lv in range(N_LV):
                    if lv == 2:
                        pool.wait_ge(ch_dve.sem, ch_dve.after(c, "xt_init"))
                    if lv > 2:
                        pool.wait_ge(ch_pe.sem, ch_pe.after(c, f"t1_{lv - 2}_1"))
                    mask = cst[0:C, C_LV + lv * C:C_LV + (lv + 1) * C].unsqueeze(1).to_broadcast([C, NH, C])
                    ch_pool.done(pool.tensor_tensor(Bm[lv % 2][0:C], MB[0:C, :, 0], mask, ALU.mult), f"bm_{lv}")
            pool.wait_ge(bg_back, 16)
            pool.wait_ge(ds_act, 2 + HP)
            pool.tensor_tensor(YT, YT, BGb[:, 0:HP], ALU.add).then_inc(o_done, 1)
            pool.wait_ge(o_done, 1)
            pool.tensor_tensor(YT, YT, BGb[:, HP:2 * HP], ALU.mult).then_inc(o_done, 1)


def _tiles(w):
    k, n = w.shape
    return w.reshape(k // P, P, n // P, P).transpose(2, 1, 0, 3).reshape(n // P, P, k)


def _constants():
    import numpy as np
    z = np.zeros((P, C_ALL), np.float32)
    i, j, t = np.arange(P)[:, None], np.arange(P)[None], np.arange(C)[None]
    z[:, C_ID:C_ID + P] = i == j
    z[:, C_ONE:C_ONE + P] = 1
    z[:, C_BLK:C_BLK + P] = i // HD == j // HD
    z[:, C_SUF:C_SUF + P] = i > j
    z[:, C_AM:C_AM + C] = np.where(t <= i, 0, -1e30)
    z[:, C_CM:C_CM + C] = i < t
    z[:, C_CM + C:C_CM + 2 * C] = i <= t
    for level in range(N_LV):
        n = 1 << level
        z[:, C_LV + level * C:C_LV + (level + 1) * C] = (i // n % 2 == 0) & (t // n == i // n + 1)
    return z


def lay_out(inp):
    import numpy as np
    f = np.float32
    x = np.concatenate([inp["meta_tokens"], inp["x_prompt"][0], inp["x_sample"][:, 0],
                        np.zeros((TT - TS, D), f)])
    xt = x.T.reshape(KT, P, TT).transpose(1, 0, 2)
    w = inp["w_in"][0]
    n_rw, n_fox = RW_T * P, 3 * NH * HD
    w_rw, w_fox = w[:, :n_rw], w[:, n_rw:n_rw + n_fox]
    w_f, w_g = w[:, n_rw + n_fox:n_rw + n_fox + NH], w[:, n_rw + n_fox + NH:]
    gr, gf = _tiles(w_g[:, :D]), _tiles(w_g[:, D:])
    pad = np.zeros((KT, P, D - NH * HD), f)
    br = np.concatenate([_tiles(inp["w_br_rwkv"][0]), pad], 2)
    bf = np.concatenate([_tiles(inp["w_br_fox"][0]), pad], 2)
    gates = np.stack([gr, gf], 1).reshape(2 * KT, P, D)
    branches = np.stack([br, bf], 1).reshape(2 * KT, P, D)
    up = _tiles(inp["w_ffn_up"][0])
    ff = []
    for c in range(FF_CH):
        ff += [up[c * KT:(c + 1) * KT], _tiles(inp["w_ffn_down"][0][c * D:(c + 1) * D])]
    wu = np.concatenate([_tiles(w_rw), _tiles(w_fox), gates, branches, _tiles(inp["w_out"][0])] + ff)

    def cols(v):
        return v.reshape(-1, P).T

    bfg = np.zeros((P, 1), f)
    bfg[:NH, 0] = inp["b_forget"][0]
    par = np.concatenate([cols(inp["norm_mix"][0]), cols(inp["norm_ffn"][0]), cols(inp["norm_final"]),
                          cols(inp["mu_shift"][0]), cols(inp["w0"][0]), cols(inp["a0"][0]), cols(inp["k_k"][0]),
                          cols(inp["k_a"][0]), cols(inp["r_k"][0]), cols(inp["ln_x_w"][0]),
                          cols(inp["ln_x_b"][0]), np.full((P, 1), 1e-6, f), np.full((P, 1), 64e-5, f), bfg,
                          np.zeros((P, 1), f)], 1)
    kp = inp["cache_k"][0].reshape(POOL, PAGE, HP, P).transpose(0, 3, 2, 1)
    vp = np.concatenate([inp["cache_v"][0].reshape(POOL, PAGE, NH * HD), inp["cache_logf"][0]], 2)
    st = inp["state_wkv"][0].reshape(2, DEC // 2, NH, HD, HD).transpose(0, 3, 1, 2, 4).reshape(P, -1)
    sh = inp["state_shift"][0].reshape(DEC, RW_T, P).transpose(2, 1, 0)
    return {"xt": xt, "wu": wu, "cst": _constants(), "par": par,
            "wf": w_f.reshape(KT, P, NH).transpose(1, 0, 2),
            "wl": np.concatenate([inp["w_decay_up"][0], inp["w_a_up"][0]]), "wg": inp["w_g_up"][0],
            "page_table": inp["page_table"].reshape(1, -1), "kp": kp, "vp": vp, "st": st, "sh": sh}


_OUTS = {"o_y": (P, KT, TT), "o_kv": (P, 2 * HP, TT), "o_lf": (NH, TT), "o_sh": (P, RW_T, DEC + 1),
         "o_sp": (P, HP, HD), "o_ss": (P, DEC // 2 * NH * HD)}


def give_back(o):
    y = o["o_y"].transpose(2, 1, 0).reshape(TT, D)
    kv = o["o_kv"].transpose(2, 1, 0).reshape(TT, 2, NH, HD)
    lf = o["o_lf"].T
    sh = o["o_sh"].transpose(2, 1, 0).reshape(DEC + 1, RW_T * P)
    sp = o["o_sp"].reshape(2, HD, HP, HD).transpose(2, 0, 3, 1).reshape(NH, HD, HD)
    ss = o["o_ss"].reshape(2, HD, DEC // 2, NH, HD).transpose(0, 2, 3, 1, 4).reshape(DEC, NH, HD, HD)
    return (y[T_META:TP][None], y[TP:TS][:, None], sh[0:1][None], sp[None, None],
            kv[:TP, 0][None, None], kv[:TP, 1][None, None], lf[:TP][None, None], sh[1:][None], ss[None],
            kv[TP:TS, 0][None, :, None], kv[TP:TS, 1][None, :, None], lf[TP:TS][None, :, None])


def kernel(**inputs):
    import numpy as np
    import concourse.bacc as bacc
    from concourse.bass_utils import run_bass_kernel_spmd

    nc = bacc.Bacc("TRN2", target_bir_lowering=False, num_devices=1, dynamic_dma_scratch_size=1024)
    arrays, aps = {}, {}
    for name, a in lay_out({k: np.asarray(v) for k, v in inputs.items()}).items():
        a = np.ascontiguousarray(a)
        arrays["in_" + name] = a
        aps[name] = nc.dram_tensor("in_" + name, a.shape, mybir.dt.from_np(a.dtype), kind="ExternalInput").ap()
    for name, shape in _OUTS.items():
        aps[name] = nc.dram_tensor("out_" + name, shape, F32, kind="ExternalOutput").ap()
    build(nc, aps)
    r = run_bass_kernel_spmd(nc, [arrays], core_ids=[0])
    got = {name: np.asarray(r.results[0]["out_" + name]) for name in _OUTS}
    return tuple(np.ascontiguousarray(a) for a in give_back(got))
```
